# Optimizing a Trainium2 kernel written in Bass

```python
import math
import jax, jax.numpy as jnp
from jax import lax
import numpy as np

D_MODEL = 1024
BATCH = 1
SEQ = 1024
DEPTH = 2

N_MIXERS = 2
EXPAND = 2
D_INNER = EXPAND * D_MODEL
CONF_KERNEL = 31
HEADDIM = 64
SSD_HEADS = D_INNER // HEADDIM
SSD_GROUPS = 4
D_STATE = 128
SSD_CONV = 5
CHUNK = 128
SSD_CONV_DIM = D_INNER + 2 * SSD_GROUPS * D_STATE
SSD_IN = D_INNER + SSD_CONV_DIM + 2 * SSD_HEADS
N_CONF_LAYERS = (DEPTH + 1) // 2
N_SSD_LAYERS = DEPTH // 2
EPS = 1e-5

kernel_name = "bidir_conformer_ssd_hybrid"

def rmsnorm(x, w):
    xf = x.astype(jnp.float32)
    y = xf * lax.rsqrt(jnp.mean(xf * xf, axis=-1, keepdims=True) + EPS)
    return (y * w.astype(jnp.float32)).astype(x.dtype)

def layernorm(x, w, b):
    xf = x.astype(jnp.float32)
    mu = jnp.mean(xf, axis=-1, keepdims=True)
    xc = xf - mu
    var = jnp.mean(xc * xc, axis=-1, keepdims=True)
    y = xc * lax.rsqrt(var + EPS)
    return (y * w.astype(jnp.float32) + b.astype(jnp.float32)).astype(x.dtype)

def dwconv_centred(x, w, b):
    width, ch = w.shape
    pad = (width - 1) // 2
    y = lax.conv_general_dilated(
        x, w[:, None, :].astype(x.dtype), window_strides=(1,), padding=[(pad, pad)],
        dimension_numbers=("NWC", "WIO", "NWC"), feature_group_count=ch)
    return y + b.astype(x.dtype)

def conformer_mixer(h, w_in, dw_w, dw_b, ln_w, ln_b, w_out):
    proj = h @ w_in
    v, g, z = jnp.split(proj, 3, axis=-1)
    u = v * jax.nn.sigmoid(g)
    u = dwconv_centred(u, dw_w, dw_b)
    u = layernorm(u, ln_w, ln_b)
    u = jax.nn.silu(u) * jax.nn.silu(z)
    return u @ w_out

def ssd_chunked(x, dt, A, B, C):
    in_dtype = x.dtype
    f32 = jnp.float32
    x, dt, A, B, C = (t.astype(f32) for t in (x, dt, A, B, C))
    b, s, H, P = x.shape
    G, N = B.shape[2], B.shape[3]
    hpg = H // G
    nc = s // CHUNK
    xdt = (x * dt[..., None]).reshape(b, nc, CHUNK, G, hpg, P)
    a = (dt * A).reshape(b, nc, CHUNK, G, hpg)
    a = jnp.transpose(a, (0, 3, 4, 1, 2))
    Bc = B.reshape(b, nc, CHUNK, G, N)
    Cc = C.reshape(b, nc, CHUNK, G, N)
    acs = jnp.cumsum(a, axis=-1)

    diff = acs[..., :, None] - acs[..., None, :]
    mask = jnp.tril(jnp.ones((CHUNK, CHUNK), dtype=bool))
    Lmat = jnp.where(mask, jnp.exp(jnp.where(mask, diff, 0.0)), 0.0)
    CB = jnp.einsum("bclgn,bcsgn->bgcls", Cc, Bc)
    M = CB[:, :, None] * Lmat
    y_diag = jnp.einsum("bghcls,bcsghp->bclghp", M, xdt)

    decay_states = jnp.exp(acs[..., -1:] - acs)
    states = jnp.einsum("bclgn,bghcl,bclghp->bcghpn", Bc, decay_states, xdt)

    chunk_decay = jnp.exp(acs[..., -1])

    def step(hstate, inp):
        dec, st = inp
        return hstate * dec[..., None, None] + st, hstate

    h0 = jnp.zeros((b, G, hpg, P, N), f32)
    _, state_in = lax.scan(step, h0, (jnp.moveaxis(chunk_decay, 3, 0), jnp.moveaxis(states, 1, 0)))
    state_in = jnp.moveaxis(state_in, 0, 1)

    y_off = jnp.einsum("bclgn,bcghpn,bghcl->bclghp", Cc, state_in, jnp.exp(acs))
    y = (y_diag + y_off).reshape(b, s, H, P)
    return y.astype(in_dtype)

def ssd_mixer(h, w_in, conv_w, conv_b, dt_bias, A_log, D_skip, norm_w, w_out):
    b, s, _ = h.shape
    proj = h @ w_in
    z = proj[..., :D_INNER]
    xBC = proj[..., D_INNER:D_INNER + SSD_CONV_DIM]
    dt_raw = proj[..., D_INNER + SSD_CONV_DIM:]
    xBC = jax.nn.silu(dwconv_centred(xBC, conv_w, conv_b))
    xs = xBC[..., :D_INNER].reshape(b, s, SSD_HEADS, HEADDIM)
    Bm = xBC[..., D_INNER:D_INNER + SSD_GROUPS * D_STATE].reshape(b, s, SSD_GROUPS, D_STATE)
    Cm = xBC[..., D_INNER + SSD_GROUPS * D_STATE:].reshape(b, s, SSD_GROUPS, D_STATE)
    dt = jax.nn.softplus(dt_raw.reshape(b, s, 2, SSD_HEADS).astype(jnp.float32)
                         + dt_bias.astype(jnp.float32))
    A = -jnp.exp(A_log.astype(jnp.float32))
    y_fwd = ssd_chunked(xs, dt[:, :, 0], A[0], Bm, Cm)
    flip = lambda t: jnp.flip(t, axis=1)
    y_bwd = flip(ssd_chunked(flip(xs), flip(dt[:, :, 1]), A[1], flip(Bm), flip(Cm)))
    y = y_fwd + y_bwd + xs * D_skip[:, None].astype(xs.dtype)
    y = y.reshape(b, s, D_INNER)
    y = rmsnorm(y * jax.nn.silu(z), norm_w)
    return y @ w_out

def setup_inputs(seed: int = 0) -> dict:
    key = jax.random.key(seed)
    ks = jax.random.split(key, 20)
    f32 = jnp.float32
    NC, NS = N_CONF_LAYERS, N_SSD_LAYERS
    x = jax.random.normal(ks[0], (BATCH, SEQ, D_MODEL), f32)
    norm_w = 1.0 + 0.02 * jax.random.normal(ks[1], (DEPTH, D_MODEL), f32)
    final_norm_w = 1.0 + 0.02 * jax.random.normal(ks[2], (D_MODEL,), f32)
    cm_w_in = jax.random.normal(ks[3], (NC, D_MODEL, 3 * D_INNER), f32) * D_MODEL ** -0.5
    cm_dw_w = jax.random.normal(ks[4], (NC, CONF_KERNEL, D_INNER), f32) * CONF_KERNEL ** -0.5
    cm_dw_b = 0.02 * jax.random.normal(ks[5], (NC, D_INNER), f32)
    cm_ln_w = 1.0 + 0.02 * jax.random.normal(ks[6], (NC, D_INNER), f32)
    cm_ln_b = 0.02 * jax.random.normal(ks[7], (NC, D_INNER), f32)
    cm_w_out = jax.random.normal(ks[8], (NC, D_INNER, D_MODEL), f32) * D_INNER ** -0.5
    ssd_w_in = jax.random.normal(ks[9], (NS, D_MODEL, SSD_IN), f32) * D_MODEL ** -0.5
    ssd_conv_w = jax.random.normal(ks[10], (NS, SSD_CONV, SSD_CONV_DIM), f32) * SSD_CONV ** -0.5
    ssd_conv_b = 0.02 * jax.random.normal(ks[11], (NS, SSD_CONV_DIM), f32)
    u = jax.random.uniform(ks[12], (NS, 2, SSD_HEADS), f32)
    dt0 = jnp.exp(u * (math.log(0.1) - math.log(0.001)) + math.log(0.001))
    ssd_dt_bias = dt0 + jnp.log(-jnp.expm1(-dt0))
    ssd_A_log = jnp.log(jax.random.uniform(ks[13], (NS, 2, SSD_HEADS), f32, 1.0, 16.0))
    ssd_D = 1.0 + 0.1 * jax.random.normal(ks[14], (NS, SSD_HEADS), f32)
    ssd_norm_w = 1.0 + 0.02 * jax.random.normal(ks[15], (NS, D_INNER), f32)
    ssd_w_out = jax.random.normal(ks[16], (NS, D_INNER, D_MODEL), f32) * D_INNER ** -0.5
    return {"x": x, "norm_w": norm_w, "final_norm_w": final_norm_w,
            "cm_w_in": cm_w_in, "cm_dw_w": cm_dw_w, "cm_dw_b": cm_dw_b,
            "cm_ln_w": cm_ln_w, "cm_ln_b": cm_ln_b, "cm_w_out": cm_w_out,
            "ssd_w_in": ssd_w_in, "ssd_conv_w": ssd_conv_w, "ssd_conv_b": ssd_conv_b,
            "ssd_dt_bias": ssd_dt_bias, "ssd_A_log": ssd_A_log, "ssd_D": ssd_D,
            "ssd_norm_w": ssd_norm_w, "ssd_w_out": ssd_w_out}

def reference(x, norm_w, final_norm_w, cm_w_in, cm_dw_w, cm_dw_b, cm_ln_w, cm_ln_b, cm_w_out,
              ssd_w_in, ssd_conv_w, ssd_conv_b, ssd_dt_bias, ssd_A_log, ssd_D, ssd_norm_w, ssd_w_out):
    h = x
    for i in range(DEPTH):
        hn = rmsnorm(h, norm_w[i])
        j = i // N_MIXERS
        if i % N_MIXERS == 0:
            out = conformer_mixer(hn, cm_w_in[j], cm_dw_w[j], cm_dw_b[j], cm_ln_w[j], cm_ln_b[j], cm_w_out[j])
        else:
            out = ssd_mixer(hn, ssd_w_in[j], ssd_conv_w[j], ssd_conv_b[j], ssd_dt_bias[j], ssd_A_log[j],
                            ssd_D[j], ssd_norm_w[j], ssd_w_out[j])
        h = h + out
    return rmsnorm(h, final_norm_w)


_drawn_inputs = setup_inputs


def setup_inputs(seed=0):
    import zlib

    import numpy as np

    out = dict(_drawn_inputs(seed))
    spreads = {}
    factors = {'final_norm_w': 2.783,
     'cm_dw_b': 3.303,
     'cm_ln_w': 5.369,
     'cm_ln_b': 6.457,
     'ssd_conv_b': 2.683,
     'ssd_norm_w': 3.952}
    for name, (base, spread) in spreads.items():
        noise = np.random.default_rng([zlib.crc32(name.encode()), seed]).standard_normal(out[name].shape)
        drawn = base * np.exp(spread * noise) if base else spread * noise
        out[name] = __import__('jax').numpy.asarray(drawn.astype(out[name].dtype))
    for name, factor in factors.items():
        out[name] = (out[name] * factor).astype(out[name].dtype)
    return out
```

```python
from contextlib import ExitStack

import concourse.bass as bass
from concourse import mybir

F = mybir.dt.float32
R = mybir.dt.float32r
ALU = mybir.AluOpType
ACT = mybir.ActivationFunctionType

P = 128
D = 1024
S = 1024
E = 2048
KD = D // P
KE = E // P
T = S // P
TAPS = 31
PAD = (TAPS - 1) // 2
CTAPS = 5
CPAD = (CTAPS - 1) // 2
H = 32
HD = 64
G = 4
NXBC = KE + 2 * G
EPS = 1e-5
HALF = 512
W = KD * P
UP = S + 2 * PAD + 2
CP = S + 2 * CPAD

N_CONF = 0
N_OUT1 = 3 * KE
N_DT = N_OUT1 + KE
N_XBC = N_DT + 1
N_Z = N_XBC + NXBC
N_OUT2 = N_Z + KE
N_END = N_OUT2 + KE

V_DWB, V_LNW, V_LNB, V_CB, V_SNW = 0, KE, 2 * KE, 3 * KE, 3 * KE + NXBC
NV = V_SNW + KE
C_NAMES = ["ident", "upto", "from_", "ones", "mean", "neg_f", "neg_b", "pick"]


def loop(engine, n, body):
    body(0)
    with engine.Fori(1, n) as i:
        body(i)


def later(i):
    return not isinstance(i, int) or i > 0


def program(nc, wst, x, cvec, dww, cw, rows, srow, cst, out):
    with ExitStack() as ctx:
        def sb(name, shape, dt=F):
            return ctx.enter_context(nc.sbuf_tensor(name, shape, dt))

        def sem(name):
            return ctx.enter_context(nc.semaphore(name))

        def dram(name, shape):
            return nc.dram_tensor(name, shape, F, kind="Internal").ap()

        z1_d = dram("z1_d", [KE, P, S])
        h_d = dram("h_d", [T, P, D])
        xs_d = dram("xs_d", [T, P, E])
        bc_d = dram("bc_d", [T, P, 3, G, P])
        z2_d = dram("z2_d", [T, P, E])
        sb_d = dram("sb_d", [T, P, E])
        y_d = dram("y_d", [KE, P, S])

        wraw = sb("wraw", [P, 2, W])
        wh = sb("wh", [P, 2, W], R)
        wl = sb("wl", [P, 2, W], R)
        xTh = sb("xTh", [P, KD, S], R)
        xTl = sb("xTl", [P, KD, S], R)
        acs_hl = sb("acs_hl", [P, T, P], R)
        acs_hi = sb("acs_hi", [P, 4, P], R)
        identR = sb("identR", [P, P], R)
        negR = sb("negR", [P, 2, P], R)
        pickR = sb("pickR", [P, 2 * H], R)
        c_f = {n: sb("c_" + n, [P, P if n != "pick" else 2 * H]) for n in C_NAMES}
        vec = sb("vec", [P, NV])
        taps = sb("taps", [P, KE * TAPS])
        ctaps = sb("ctaps", [P, NXBC * CTAPS])
        hrow = sb("hrow", [P, 5 * H])
        tap4 = sb("tap4", [P, 4 * TAPS])
        stat = sb("stat", [P, 64])
        arow = sb("arow", [P, 2 * H])
        AR = 26250
        arena = sb("arena", [P, AR])
        used = [0]

        def at(off, *shape):
            n = 1
            for s in shape:
                n *= s
            assert off + n <= AR, (off, shape)
            v = arena[:, off:off + n]
            names = "abcd"[:len(shape)]
            if len(shape) > 1:
                v = v.rearrange(f"p ({' '.join(names)}) -> p {' '.join(names)}",
                                **dict(zip(names, shape)))
            return v

        r_x = at(0, 2, D)
        r_n = at(2 * D, 2, D)
        r_w = at(4 * D, D)
        r_junk = at(5 * D, D)
        cv = at(0, KE, S)
        o = KE * S
        upad = at(o, 4, UP)
        xres = at(o, T, HALF)
        o += 4 * UP
        sigb = at(o, 2, HALF)
        vb = at(o + S, 2, HALF)
        sqb = at(o, 2, S)
        zst = at(o + 2 * S, 2, S)
        csum = at(o + 4 * S, S)
        rstd = csum
        cpad = at(0, 2, CP)
        csil = at(2 * CP, 2, S)
        stg = at(2 * CP + 2 * S, 2, T, P)
        z2b = at(2 * CP + 4 * S, T, HALF)
        dtt = at(2 * CP + 8 * S, 6, HALF)
        a2 = at(2 * CP + 8 * S + 6 * HALF, T, 2, 2 * H)
        o = 0
        xs_s = at(o, 2, E); o += 2 * E
        bc_s = at(o, 2, 3, G, P); o += 2 * 3 * G * P
        z_s = at(o, E); o += E
        sf = at(o, E); o += E
        sbk = at(o, E); o += E
        xf_s = at(o, 2, HALF)
        xb_s = at(o, E)
        o += 2 * HALF
        tmpb = at(o, 2, HALF); o += 2 * HALF
        yacc = at(o, E); o += E
        xD = at(o, 2, HALF); o += 2 * HALF
        Lb = at(o, 2, 4, P); o += 2 * HALF
        Mb = at(o, 4, 4, P); o += 4 * HALF
        yst = at(o, 2, 4, P); o += 2 * HALF
        sqj = at(o, HALF); o += HALF
        o_small = max(o, 2 * CP + 8 * S + 8 * HALF)
        o = o_small
        dt_s = at(o, T, 2 * H); o += HALF
        e_s = at(o, T, 2 * H); o += HALF
        dec_s = at(o, T, 2 * H); o += HALF
        coef_s = at(o, T, 2 * H); o += HALF
        nacs_s = at(o, T, 2 * H); o += HALF
        dtc = at(o, 2 * H); o += 2 * H
        nac = at(o, 2 * H); o += 2 * H
        ss_y = at(o, T, G); o += T * G
        rs_y = at(o, 3, T); o += 3 * T
        y_ld = at(0, 2, S)
        hf = at(2 * S, T, D)
        f_w = at(2 * S + T * D, D)
        f_o = at(2 * S + T * D + D, 2, D)
        f_junk = at(2 * S + T * D + 3 * D, D)
        assert 2 * S + T * D + 4 * D <= o_small

        ps = ctx.enter_context(nc.psum_tensor("ps", [P, 8, HALF], F))

        c_ld = sem("c_ld")
        w_raw = [sem("w_raw0"), sem("w_raw1")]
        w_hi, w_lo = sem("w_hi"), sem("w_lo")
        cr = sem("cr")
        cr2 = sem("cr2")
        r_ld = [[sem(f"r{l}_ld0"), sem(f"r{l}_ld1")] for l in range(2)]
        rw_ld = [sem("rw_ld0"), sem("rw_ld1"), sem("rw_ld2")]
        r_ss = [sem(f"r{l}_ss") for l in range(2)]
        r_rs = [sem(f"r{l}_rs") for l in range(2)]
        r_xn = [sem(f"r{l}_xn") for l in range(2)]
        r_ps = [sem(f"r{l}_ps") for l in range(2)]
        r_hi = [sem(f"r{l}_hi") for l in range(2)]
        r_lo = [sem(f"r{l}_lo") for l in range(2)]
        a_fill, a_evac, a_um, a_tap, a_conv, a_cv, a_csum = (
            sem(n) for n in ("a_fill", "a_evac", "a_um", "a_tap", "a_conv", "a_cv", "a_csum"))
        a_tap4 = sem("a_tap4")
        a_pad = sem("a_pad")
        z_st = [sem("z_st0"), sem("z_st1")]
        z_ld = [sem("z_ld0"), sem("z_ld1")]
        l_mean, l_xc, l_sq, l_var, l_std, l_rstd = (
            sem(n) for n in ("l_mean", "l_xc", "l_sq", "l_var", "l_std", "l_rstd"))
        n_mul, n_silu, n_y = sem("n_mul"), sem("n_silu"), sem("n_y")
        n_zs = sem("n_zs")
        o_hi = [sem(f"o{l}_hi") for l in range(2)]
        o_lo = [sem(f"o{l}_lo") for l in range(2)]
        o_mm = [sem(f"o{l}_mm") for l in range(2)]
        o_t = [sem(f"o{l}_t") for l in range(2)]
        o_h = [sem(f"o{l}_h") for l in range(2)]
        xr_ld = [sem("xr_ld0"), sem("xr_ld1")]
        h_st = [sem("h_st0"), sem("h_st1")]
        d_ps, d_dt, d_neg, d_exp, d_A, d_a = (sem(n) for n in ("d_ps", "d_dt", "d_neg", "d_exp", "d_A", "d_a"))
        d_acs, d_sc, d_se, d_tr = sem("d_acs"), sem("d_sc"), sem("d_se"), sem("d_tr")
        d_trh, d_trl, d_coef = sem("d_trh"), sem("d_trl"), sem("d_coef")
        b_fill, b_evac, b_tap, b_sil, b_tr, b_te = (sem(n) for n in ("b_fill", "b_evac", "b_tap", "b_sil", "b_tr", "b_te"))
        b_pad = sem("b_pad")
        b_st = [sem("b_st0"), sem("b_st1")]
        b_sc = [sem("b_sc0"), sem("b_sc1")]
        q_mm, q_t, q_sil, q_st = sem("q_mm"), sem("q_t"), sem("q_sil"), sem("q_st")
        d_v = sem("d_v")
        p_x = [sem("p_x0"), sem("p_x1")]
        p_b = [sem("p_b0"), sem("p_b1")]
        p_xb, p_mm, p_dec, p_s = sem("p_xb"), sem("p_mm"), sem("p_dec"), sem("p_s")
        p_st = [sem("p_st0"), sem("p_st1")]
        s_x = [sem("s_x0"), sem("s_x1")]
        s_b = [sem("s_b0"), sem("s_b1")]
        s_z, s_s = sem("s_z"), sem("s_s")
        s_cb, s_L, s_ex, s_M, s_yd, s_yo = (sem(n) for n in ("s_cb", "s_L", "s_ex", "s_M", "s_yd", "s_yo"))
        s_ya, s_tb, s_ad, s_xD, s_dd, s_g = (sem(n) for n in ("s_ya", "s_tb", "s_ad", "s_xD", "s_dd", "s_g"))
        s_xf, s_stt, s_sd, s_S, s_tr, s_te = (sem(n) for n in ("s_xf", "s_stt", "s_sd", "s_S", "s_tr", "s_te"))
        s_sq, s_dc, s_nc = sem("s_sq"), sem("s_dc"), sem("s_nc")
        s_zero = sem("s_zero")
        s_ys = [sem("s_ys0"), sem("s_ys1")]
        y_l = [sem("y_l0"), sem("y_l1")]
        rs_r, rs_p = sem("rs_r"), sem("rs_p")
        f_ss, f_rs, f_out = sem("f_ss"), sem("f_rs"), sem("f_out")
        f_st = [sem("f_st0"), sem("f_st1")]

        block = ctx.enter_context(nc.Block())
        mm = nc.tensor.matmul

        def tile_done(l, m):
            if m % KE == KE - 1:
                return o_t[l], T * (m // KE + 1)
            return o_mm[l], m + 1 - m // KE

        def bcast(ap, n):
            return ap.unsqueeze(2).to_broadcast([P, ap.shape[-1], n])

        @block.sync
        def _(sp):
            def wload(n, i=0, per=0):
                if not isinstance(i, int) or n + per * i >= 2:
                    sp.wait_ge(w_lo, n + per * i - 1)
                if isinstance(i, int):
                    src = wst[n + per * i]
                else:
                    src = wst[bass.ds(n + per * i, 1)].rearrange("a p w -> (a p) w")
                sp.dma_start(wraw[:, n % 2], src).then_inc(w_raw[n % 2], 16)

            def norm_loads(l, src):
                for t in range(T):
                    if t >= 2:
                        sp.wait_ge(r_xn[l], t - 1)
                    sp.dma_start(r_x[:, t % 2], src[t]).then_inc(r_ld[l][t % 2], 16)
                    if l == 0 and t == 1:
                        wload(0)
                        wload(1)

            norm_loads(0, x)

            def conf(p):
                for b in range(2):
                    for j in range(3):
                        wload(3 * b + j + 2, p, 6)
                    sp.wait_ge(a_evac, 12 * p + 6 * b + 6)
                    dst = z1_d[2 * p + b] if isinstance(p, int) else \
                        z1_d[bass.ds(2 * p + b, 1)].rearrange("a p s -> (a p) s")
                    sp.dma_start(dst, zst[:, b]).then_inc(z_st[b], 16)
            loop(sp, KE // 2, conf)

            for b in range(2):
                sp.wait_ge(z_st[b], 16 * KE // 2)
            for k in range(2):
                sp.dma_start(zst[:, k], z1_d[k]).then_inc(z_ld[k], 16)
            sp.wait_ge(a_conv, 2 * KE)
            sp.dma_start(xres[:], x.rearrange("t p d -> p t d")[:, :, 0:HALF]).then_inc(xr_ld[0], 16)
            for k in range(KE):
                if k + 2 < KE:
                    sp.wait_ge(n_y, k + 1)
                    sp.dma_start(zst[:, k % 2], z1_d[k + 2]).then_inc(z_ld[k % 2], 16)
                if k % 2 == 0:
                    wload(N_OUT1 + 2 + k // 2)
            for h in range(2):
                for n in ((N_OUT1 + 10, N_OUT1 + 11), ())[h]:
                    wload(n)
                for t in range(T):
                    sp.wait_ge(o_h[0], T * h + t + 1)
                    sp.dma_start(h_d[t, :, HALF * h:HALF * (h + 1)], xres[:, t]).then_inc(h_st[h], 16)
                sp.wait_ge(h_st[h], 16 * T)
                if h == 0:
                    sp.dma_start(xres[:], x.rearrange("t p d -> p t d")[:, :, HALF:D]).then_inc(xr_ld[1], 16)
                    for n in range(N_OUT1 + 12, N_DT + 3):
                        wload(n)

            norm_loads(1, h_d)

            wload(N_DT + 3)

            def stores(n, b, what):
                sp.wait_ge(b_te, 4 * n + 2 * b + 2)
                dst = xs_d.rearrange("t p e -> p t e")[:, :, bass.ds((2 * n + b) * P, P)]
                sp.dma_start(dst, stg[:, b]).then_inc(b_st[b], 16)

            def xside(j):
                for b in range(2):
                    wload(N_XBC + 3 + b, j, 2)
                    if b == 0:
                        if later(j):
                            stores(j - 1, 1, None)
                    else:
                        stores(j, 0, None)
            loop(sp, KE // 2, xside)
            stores(KE // 2 - 1, 1, None)
            for g in range(G):
                wload(N_XBC + KE + 2 * g + 3)
                sp.wait_ge(b_sil, KE + 2 * g + 1)
                sp.dma_start(bc_d.rearrange("t p k g n -> p k g t n")[:, 0, g],
                             csil[:, 0].rearrange("p (t n) -> p t n", t=T)).then_inc(b_sc[0], 16)
                wload(N_XBC + KE + 2 * g + 4)
                sp.wait_ge(b_sil, KE + 2 * g + 2)
                sp.dma_start(bc_d.rearrange("t p k g n -> p k g t n")[:, 1, g],
                             csil[:, 1].rearrange("p (t n) -> p t n", t=T)).then_inc(b_sc[1], 16)
                sp.wait_ge(b_te, 2 * KE + 2 * g + 2)
                sp.dma_start(bc_d.rearrange("t p k g n -> p k g t n")[:, 2, g], stg[:, 0]).then_inc(b_st[0], 16)

            for q in range(G):
                for m in range(4):
                    if N_Z + 3 + 4 * q + m < N_OUT2 + 2:
                        wload(N_Z + 3 + 4 * q + m)
                sp.wait_ge(q_sil, T * (q + 1))
                sp.dma_start(z2_d.rearrange("t p e -> p t e")[:, :, HALF * q:HALF * (q + 1)],
                             z2b[:]).then_inc(q_st, 16)
            sp.wait_ge(q_st, 16 * G)
            for b in range(2):
                sp.wait_ge(b_st[b], 16 * (KE // 2 + (G if b == 0 else 0)))
                sp.wait_ge(b_sc[b], 16 * G)

            for r, c in enumerate(range(T - 1, 0, -1)):
                b = r % 2
                if r >= 2:
                    sp.wait_ge(p_mm, r - 1)
                sp.dma_start(xs_s[:, b], xs_d[c]).then_inc(p_x[b], 16)
                sp.dma_start(bc_s[:, b], bc_d[c]).then_inc(p_b[b], 16)
                sp.wait_ge(p_s, r + 1)
                sp.dma_start(sb_d[c], (sf, sbk)[b]).then_inc(p_st[b], 16)
            sp.wait_ge(p_s, T)
            sp.dma_start(sb_d[0], (sf, sbk)[(T - 1) % 2]).then_inc(p_st[(T - 1) % 2], 16)
            for b in range(2):
                sp.wait_ge(p_st[b], 16 * T // 2)
            sp.wait_ge(p_mm, T - 1)

            def src1(d, c):
                return d[c] if isinstance(c, int) else d[bass.ds(c, 1)].squeeze(0)

            def xb_loads(c, b):
                sp.dma_start(xs_s[:, b], src1(xs_d, c)).then_inc(s_x[b], 16)
                sp.dma_start(bc_s[:, b], src1(bc_d, c)).then_inc(s_b[b], 16)

            for b in range(2):
                xb_loads(b, b)
            sp.dma_start(sbk, sb_d[0]).then_inc(s_s, 16)
            sp.dma_start(z_s, z2_d[0]).then_inc(s_z, 16)

            def y_stores(c, i):
                sp.wait_ge(s_te, 4 * c + i + 1)
                dst = y_d.rearrange("j p s -> p j s")[:, 4 * i:4 * i + 4, bass.ds(c * P, P)]
                sp.dma_start(dst, yst[:, i % 2]).then_inc(s_ys[i % 2], 16)

            def chunk_dma(c2):
                for b in range(2):
                    c = 2 * c2 + b
                    if later(c):
                        for i in range(4):
                            y_stores(c - 1, i)
                        sp.dma_start(z_s, src1(z2_d, c)).then_inc(s_z, 16)
                        sp.wait_ge(s_g, 4 * c)
                        if b == 1 and not isinstance(c2, int) or isinstance(c, int) and c + 1 < T or b == 0:
                            xb_loads(c + 1, 1 - b)
                    sp.wait_ge(s_yo, 8 * c + 8)
                    if not (isinstance(c, int) and c == T - 1):
                        sp.dma_start(sbk, src1(sb_d, c + 1)).then_inc(s_s, 16)
            chunk_dma(0)
            with sp.Fori(1, T // 2 - 1) as c2:
                chunk_dma(c2)
            chunk_dma(T // 2 - 1)
            for i in range(4):
                y_stores(T - 1, i)
            for b in range(2):
                sp.wait_ge(s_ys[b], 16 * 2 * T)

            sp.wait_ge(s_g, 4 * T)
            sp.dma_start(hf[:], h_d.rearrange("t p d -> p t d")).then_inc(xr_ld[0], 16)
            for h in range(2):
                for k in range(KE):
                    m = KE * h + k
                    if m >= 2:
                        sp.wait_ge(o_lo[1], m - 1)
                    sp.dma_start(y_ld[:, k % 2], y_d[k]).then_inc(y_l[k % 2], 16)
                    if k % 2 == 0 and m // 2 + 2 < KE:
                        wload(N_OUT2 + 2 + m // 2)
            for t in range(T):
                sp.wait_ge(f_out, t + 1)
                sp.dma_start(out[t], f_o[:, t % 2]).then_inc(f_st[t % 2], 16)
            for b in range(2):
                sp.wait_ge(f_st[b], 16 * T // 2)

        @block.scalar
        def _(act):
            for name in C_NAMES:
                act.dma_start(c_f[name][:], cst[name]).then_inc(c_ld, 16)
            act.dma_start(r_w[:], rows[0:1, :].to_broadcast([P, D])).then_inc(rw_ld[0], 16)
            act.dma_start(vec[:], cvec).then_inc(c_ld, 16)
            act.dma_start(taps[:], dww).then_inc(c_ld, 16)
            act.dma_start(ctaps[:], cw).then_inc(c_ld, 16)
            act.dma_start(hrow[:], srow.to_broadcast([P, 5 * H])).then_inc(c_ld, 16)
            n_const = 16 * (len(C_NAMES) + 4)
            act.wait_ge(c_ld, n_const)
            nc.scalar.copy(identR[:], c_f["ident"][:])
            nc.scalar.copy(negR[:, 0], c_f["neg_f"][:])
            nc.scalar.copy(negR[:, 1], c_f["neg_b"][:])
            nc.scalar.copy(pickR[:], c_f["pick"][:]).then_inc(cr, 1)

            def split(n, i=0, per=0, free=None):
                act.wait_ge(w_raw[n % 2], 16 * (n // 2 + (per // 2) * i + 1))
                if free is not None:
                    act.wait_ge(*free)
                nc.scalar.copy(wh[:, n % 2], wraw[:, n % 2]).then_inc(w_hi, 1)

            def norm(l):
                def hi(t):
                    for q in range(2):
                        act.wait_ge(r_ps[l], 2 * t + q + 1)
                        nc.scalar.copy(xTh[:, 4 * q:4 * q + 4, t * P:(t + 1) * P],
                                       ps[:, 2 * (t % 2) + q].rearrange("p (k s) -> p k s", k=4)).then_inc(r_hi[l], 1)
                for t in range(T):
                    act.wait_ge(r_ld[l][t % 2], 16 * (t // 2 + 1))
                    if t >= 1:
                        act.wait_ge(r_ss[l], t)
                    nc.scalar.activation(r_junk[:], r_x[:, t % 2], ACT.Square,
                                         accum_out=stat[:, t:t + 1]).then_inc(r_ss[l], 1)
                    if t >= 1:
                        hi(t - 1)
                hi(T - 1)

            norm(0)
            split(0)
            split(1)

            def conv_out(p):
                for b in range(2):
                    for h in range(2):
                        i = 2 * p + b
                        act.wait_ge(a_conv, 4 * p + 2 * b + h + 1)
                        dst = arena[:, bass.ds(i * S + HALF * h, HALF)]
                        nc.scalar.activation(dst, ps[:, 4 + 2 * b + h], ACT.Identity,
                                             bias=vec[:, bass.ds(V_DWB + i, 1)]).then_inc(a_cv, 1)

            def conf(p):
                for b in range(2):
                    i6 = 12 * p + 6 * b
                    for j in range(3):
                        if not (isinstance(p, int) and p == 0 and b == 0 and j == 0):
                            split(3 * b + j + 1, p, 6, free=(a_fill, 2 * (6 * p + 3 * b + j + 1 - 1)))
                        for h in range(2):
                            f = 2 * j + h
                            act.wait_ge(a_fill, i6 + f + 1)
                            src = ps[:, (6 * b + f) % 4]
                            if j < 2 and not (isinstance(p, int) and p == 0 and b == 0):
                                act.wait_ge(a_um, 4 * p + 2 * b - 1 + h)
                            if j == 0:
                                nc.scalar.activation(sigb[:, h], src, ACT.Sigmoid).then_inc(a_evac, 1)
                            elif j == 1:
                                nc.scalar.copy(vb[:, h], src).then_inc(a_evac, 1)
                            else:
                                if later(p):
                                    act.wait_ge(z_st[b], 16 * p)
                                nc.scalar.copy(zst[:, b, HALF * h:HALF * (h + 1)], src).then_inc(a_evac, 1)
                if later(p):
                    conv_out(p - 1)
            loop(act, KE // 2, conf)
            conv_out(KE // 2 - 1)

            for k in range(KE):
                act.wait_ge(l_xc, k + 1)
                if k >= 2:
                    act.wait_ge(l_var, k - 1)
                nc.scalar.square(sqb[:, k % 2], cv[:, k]).then_inc(l_sq, 1)
            split(N_OUT1 + 1, free=(a_fill, 6 * KE))
            act.wait_ge(l_var, KE)
            for h in range(2):
                nc.scalar.activation(rstd[:, HALF * h:HALF * (h + 1)], ps[:, 2 + h], ACT.Sqrt,
                                     bias=EPS).then_inc(l_std, 1)

            def silu_y(k):
                act.wait_ge(z_ld[k % 2], 16 * (k // 2 + 1))
                nc.scalar.activation(zst[:, k % 2], zst[:, k % 2], ACT.Silu).then_inc(n_zs, 1)
                act.wait_ge(n_mul, k + 1)
                nc.scalar.activation(cv[:, k], cv[:, k], ACT.Silu, scale=vec[:, V_LNW + k:V_LNW + k + 1],
                                     bias=vec[:, V_LNB + k:V_LNB + k + 1]).then_inc(n_silu, 1)

            def y_hi(l, m, src, scale):
                if m >= 2:
                    act.wait_ge(*tile_done(l, m - 2))
                if scale is None:
                    nc.scalar.copy(xTh[:, m % 2], src).then_inc(o_hi[l], 1)
                else:
                    nc.scalar.activation(xTh[:, m % 2], src, ACT.Copy, scale=scale).then_inc(o_hi[l], 1)

            silu_y(0)
            for m in range(2 * KE):
                if m + 1 < KE:
                    silu_y(m + 1)
                if m < KE:
                    act.wait_ge(n_y, m + 1)
                y_hi(0, m, cv[:, m % KE], None)
                if m % 2 == 1:
                    split(N_OUT1 + m // 2 + 2, free=tile_done(0, m))

            act.wait_ge(o_lo[0], 2 * KE)
            act.dma_start(r_w[:], rows[1:2, :].to_broadcast([P, D])).then_inc(rw_ld[1], 16)
            norm(1)

            act.wait_ge(d_dt, 1)
            nc.scalar.activation(dtt[:, 1], dtt[:, 0], ACT.Abs).then_inc(d_neg, 1)
            act.wait_ge(d_neg, 1)
            nc.scalar.activation(dtt[:, 2], dtt[:, 1], ACT.Exp, scale=-1.0).then_inc(d_exp, 1)
            nc.scalar.activation(arow[:], hrow[:, 2 * H:4 * H], ACT.Exp).then_inc(d_A, 1)

            def evac_sil(j, b, n2):
                for h in range(2):
                    act.wait_ge(b_fill, 4 * j + 2 * b + h + 1)
                    if h == 0 and later(j):
                        act.wait_ge(b_tap, CTAPS * (2 * j + b - 1))
                    if h == 0 and not later(j):
                        act.wait_ge(b_pad, 1)
                    nc.scalar.copy(cpad[:, b, CPAD + HALF * h:CPAD + HALF * (h + 1)], ps[:, h]).then_inc(b_evac, 1)

            def sil(j, b):
                act.wait_ge(b_tap, CTAPS * (2 * j + b + 1))
                nc.scalar.activation(csil[:, b], ps[:, 2 + 2 * b:4 + 2 * b].rearrange("p a s -> p (a s)"),
                                     ACT.Silu).then_inc(b_sil, 1)

            def tr_out(n, b, cnt):
                for h in range(2):
                    act.wait_ge(b_tr, cnt + h + 1)
                    nc.scalar.copy(stg[:, b, 4 * h:4 * h + 4],
                                   ps[:, 6 + h].rearrange("p (t c) -> p t c", t=4)).then_inc(b_te, 1)

            def xside(j):
                for b in range(2):
                    if later(j) or b:
                        split(N_XBC + b + 1, j, 2, free=(b_fill, 4 * j + 2 * b))
                    else:
                        split(N_XBC + 1, free=(d_ps, 1))
                    evac_sil(j, b, None)
                    if later(j) or b:
                        jj, bb = (j, 0) if b else (j - 1, 1)
                        if later(jj):
                            act.wait_ge(b_st[bb], 16 * jj)
                        tr_out(None, bb, 4 * jj + 2 * bb)
                    sil(j, b)
            loop(act, KE // 2, xside)
            act.wait_ge(b_st[1], 16 * (KE // 2 - 1))
            tr_out(None, 1, 4 * (KE // 2 - 1) + 2)

            def flat(v):
                return v.rearrange("p t h -> p (t h)")

            act.wait_ge(d_acs, 3)
            nc.scalar.activation(flat(e_s), ps[:, 4], ACT.Exp).then_inc(d_se, 1)
            nc.scalar.activation(flat(nacs_s), ps[:, 4], ACT.Copy, scale=-1.0).then_inc(d_se, 1)
            act.wait_ge(d_sc, 1)
            nc.scalar.activation(flat(dec_s), ps[:, 5], ACT.Exp).then_inc(d_se, 1)
            nc.scalar.activation(dtt[:, 5], dtt[:, 0], ACT.Exp).then_inc(d_se, 1)

            def decay_rows():
                for u in range(2):
                    pf, pb = (ps[:, 4 + d].rearrange("p (t l) -> p t l", t=4) for d in range(2))
                    cs = slice(4 * u, 4 * u + 4)
                    act.wait_ge(d_tr, 2 * u + 2)
                    nc.scalar.copy(acs_hl[0:32, cs], pf[0:32])
                    nc.scalar.copy(acs_hl[32:64, cs], pb[32:64])
                    if u:
                        act.wait_ge(d_trl, 2)
                    nc.scalar.copy(acs_hi[64:96], pf[64:96])
                    nc.scalar.copy(acs_hi[96:128], pb[96:128]).then_inc(d_trh, 1)

            for g in range(G):
                for b in range(2):
                    j = KE // 2 + g
                    split(N_XBC + KE + 2 * g + b + 1, free=(b_fill, 4 * j + 2 * b))
                    evac_sil(j, b, None)
                    if g == 0 and b == 0:
                        decay_rows()
                    if b == 1:
                        act.wait_ge(b_st[0], 16 * (KE // 2 + g))
                        tr_out(None, 0, 2 * KE + 2 * g)
                    if g:
                        act.wait_ge(b_sc[b], 16 * g)
                    sil(j, b)

            for q in range(G):
                for m in range(4):
                    n = N_Z + 4 * q + m + 1
                    if m:
                        split(n, free=(q_mm, 3 * q + m))
                    else:
                        split(n, free=(q_t, T * q) if q else (b_fill, 2 * NXBC))
                if q:
                    act.wait_ge(q_st, 16 * q)
                for t in range(T):
                    act.wait_ge(q_t, T * q + t + 1)
                    nc.scalar.activation(z2b[:, t], ps[:, t], ACT.Silu).then_inc(q_sil, 1)
            split(N_OUT2 + 1, free=(q_t, T * G))

            def evac_y(c, i):
                act.wait_ge(s_g, 4 * c + i + 1)
                if i or later(c):
                    act.wait_ge(s_sq, 4 * c + i)
                nc.scalar.activation(sqj, z_s[:, HALF * i:HALF * (i + 1)], ACT.Square,
                                     accum_out=ss_y.rearrange("p t g -> p (t g)")[:, bass.ds(4 * c + i, 1)]).then_inc(s_sq, 1)
                act.wait_ge(s_tr, 4 * c + i + 1)
                if i >= 2:
                    act.wait_ge(s_ys[i % 2], 32 * c + 16)
                elif later(c):
                    act.wait_ge(s_ys[i % 2], 32 * c)
                nc.scalar.copy(yst[:, i % 2], ps[:, 7].rearrange("p (j s) -> p j s", j=4)).then_inc(s_te, 1)

            def chunk(c2):
                for b in range(2):
                    c = 2 * c2 + b
                    if later(c):
                        act.wait_ge(s_ex, 16 * c)
                    nc.scalar.copy(nac, nacs_s[:, bass.ds(c, 1)].rearrange("p a h -> p (a h)")).then_inc(s_nc, 1)
                    act.wait_ge(s_nc, c + 1)
                    for u in range(16):
                        hq, d = divmod(u, 2)
                        act.wait_ge(s_L, 16 * c + u + 1)
                        if u >= 2 or later(c):
                            act.wait_ge(s_M, 16 * c + u - 1)
                        for e in range(4):
                            col = d * H + 4 * hq + e
                            last = nc.scalar.activation(Lb[:, u % 2, e], ps[:, 3 + u % 2, P * e:P * (e + 1)],
                                                        ACT.Exp, bias=nac[:, col:col + 1])
                        last.then_inc(s_ex, 1)
                        if u in (3, 5, 7, 9) and later(c):
                            evac_y(c - 1, (u - 3) // 2)
            loop(act, T // 2, chunk)
            for i in range(4):
                evac_y(T - 1, i)
            for m in range(2 * KE):
                act.wait_ge(y_l[m % 2], 16 * (m // 2 + 1))
                y_hi(1, m, y_ld[:, m % 2], vec[:, V_SNW + m % KE:V_SNW + m % KE + 1])
                if m % 2 == 1 and N_OUT2 + m // 2 + 2 < N_END:
                    split(N_OUT2 + m // 2 + 2, free=tile_done(1, m))
                if m == 0:
                    act.wait_ge(s_S, 4 * T)
                    act.dma_start(f_w[:], rows[2:3, :].to_broadcast([P, D])).then_inc(rw_ld[2], 16)
            for t in range(T):
                act.wait_ge(o_h[1], T + t + 1)
                if t:
                    act.wait_ge(f_ss, t)
                nc.scalar.activation(f_junk, hf[:, t], ACT.Square, accum_out=stat[:, t:t + 1]).then_inc(f_ss, 1)


        @block.gpsimd
        def _(pool):
            tt = nc.gpsimd.tensor_tensor

            def split(n, i=0, per=0):
                pool.wait_ge(w_hi, n + per * i + 1)
                tt(wl[:, n % 2], wraw[:, n % 2], wh[:, n % 2].bitcast(F), ALU.subtract).then_inc(w_lo, 1)

            nc.gpsimd.memset(stat[:, 63:64], -0.5).then_inc(cr2, 1)
            nc.gpsimd.memset(csum, 0.0).then_inc(cr2, 1)
            nc.gpsimd.memset(upad, 0.0).then_inc(a_pad, 1)

            def norm(l):
                for t in range(T):
                    pool.wait_ge(r_ss[l], t + 1)
                    nc.gpsimd.tensor_scalar(stat[:, 16 + t:17 + t], stat[:, t:t + 1], 1.0 / D, EPS,
                                            ALU.mult, ALU.add).then_inc(r_rs[l], 1)
                    pool.wait_ge(r_rs[l], 2 * t + 1)
                    if l == 0 and t == 0:
                        pool.wait_ge(cr2, 1)
                    tt(stat[:, 32 + t:33 + t], stat[:, 16 + t:17 + t], stat[:, 63:64], ALU.pow).then_inc(r_rs[l], 1)

            norm(0)
            split(0)
            split(1)
            pool.wait_ge(a_pad, 1)

            def add_tile(i):
                pool.wait_ge(a_cv, 2 * i + 2)
                pool.wait_ge(a_csum, i) if later(i) else pool.wait_ge(cr2, 2)
                tt(csum, csum, arena[:, bass.ds(i * S, S)], ALU.add).then_inc(a_csum, 1)

            def conf(q):
                for r in range(4):
                    i = 4 * q + r
                    if later(i):
                        split(3 * r + 1, q, 12)
                    split(3 * r + 2, q, 12)
                    if later(q):
                        pool.wait_ge(a_conv, 2 * i - 6)
                    for h in range(2):
                        pool.wait_ge(a_evac, 6 * i + 3 + h)
                        tt(upad[:, r, PAD + HALF * h:PAD + HALF * (h + 1)], sigb[:, h], vb[:, h],
                           ALU.mult).then_inc(a_um, 1)
                    split(3 * r + 3, q, 12)
                    if r % 2 and (r == 3 or later(q)):
                        add_tile(i - 3)
                        add_tile(i - 2)
            loop(pool, KE // 4, conf)
            add_tile(KE - 2)
            add_tile(KE - 1)
            split(N_OUT1 + 1)

            def y_tile(k):
                pool.wait_ge(n_silu, k + 1)
                pool.wait_ge(n_zs, k + 1)
                tt(cv[:, k], cv[:, k], zst[:, k % 2], ALU.mult).then_inc(n_y, 1)

            y_tile(0)
            for m in range(2 * KE):
                if m + 1 < KE:
                    y_tile(m + 1)
                if m % 2 == 1:
                    split(N_OUT1 + m // 2 + 2)

            norm(1)
            pool.wait_ge(r_ps[1], 2 * T)
            nc.gpsimd.memset(cpad, 0.0).then_inc(b_pad, 1)

            def xside(j):
                for b in range(2):
                    split(N_XBC + 1 + b, j, 2)
            loop(pool, KE // 2, xside)
            for g in range(G):
                for b in range(2):
                    split(N_XBC + KE + 2 * g + b + 1)
            for m in range(KE + 1):
                split(N_Z + 1 + m)

            for r, c in enumerate(range(T - 1, 0, -1)):
                b = r % 2
                pool.wait_ge(p_x[b], 16 * (r // 2 + 1))
                if r:
                    pool.wait_ge(p_mm, r)
                else:
                    pool.wait_ge(d_coef, 1)
                tt(xb_s.rearrange("p (h e) -> p h e", h=H), xs_s[:, b].rearrange("p (h e) -> p h e", h=H),
                   bcast(coef_s[:, c, H:2 * H], HD), ALU.mult).then_inc(p_xb, 1)

            def heads(v):
                return v.rearrange("p (h e) -> p h e", h=8)

            def chunk(c2):
                for b in range(2):
                    c = 2 * c2 + b

                    def x_skip(g):
                        if g == 0:
                            pool.wait_ge(s_x[b], 16 * (c2 + 1))
                        if g >= 2 or later(c):
                            pool.wait_ge(s_yd, 8 * c + 2 * g - 2)
                        if g >= 2 or later(c):
                            pool.wait_ge(s_xD, 4 * c + g - 1)
                        tt(heads(xD[:, g % 2]), heads(xs_s[:, b, HALF * g:HALF * (g + 1)]),
                           bcast(hrow[:, 4 * H + 8 * g:4 * H + 8 * g + 8], HD), ALU.mult).then_inc(s_xD, 1)

                    def x_state(g):
                        if g >= 2 or later(c):
                            pool.wait_ge(s_stt, 4 * c + g - 1)
                            pool.wait_ge(s_xf, 4 * c + g - 1)
                        elif g == 0:
                            pool.wait_ge(p_mm, T - 1)
                        tt(heads(xf_s[:, g % 2]), heads(xs_s[:, b, HALF * g:HALF * (g + 1)]),
                           bcast(coef_s.rearrange("p t h -> p (t h)")[:, bass.ds(c * 2 * H + 8 * g, 8)], HD),
                           ALU.mult).then_inc(s_xf, 1)

                    def y_add(g):
                        pool.wait_ge(s_tb, 4 * c + g + 1)
                        pool.wait_ge(s_ya, 4 * c + g + 1)
                        tt(yacc[:, HALF * g:HALF * (g + 1)], yacc[:, HALF * g:HALF * (g + 1)], tmpb[:, g % 2],
                           ALU.add).then_inc(s_ad, 1)

                    def gate(g):
                        if g == 0:
                            pool.wait_ge(s_z, 16 * (c + 1))
                        pool.wait_ge(s_dd, 4 * c + g + 1)
                        tt(z_s[:, HALF * g:HALF * (g + 1)], yacc[:, HALF * g:HALF * (g + 1)],
                           z_s[:, HALF * g:HALF * (g + 1)], ALU.mult).then_inc(s_g, 1)

                    x_skip(0)
                    y_add(0)
                    x_skip(1)
                    x_state(0)
                    y_add(1)
                    gate(0)
                    x_state(1)
                    x_skip(2)
                    y_add(2)
                    gate(1)
                    x_state(2)
                    x_skip(3)
                    x_state(3)
                    y_add(3)
                    gate(2)
                    gate(3)
            loop(pool, T // 2, chunk)

            pool.wait_ge(rs_r, 1)
            nc.gpsimd.tensor_scalar(rs_y[:, 1], rs_y[:, 0], 1.0 / E, EPS, ALU.mult, ALU.add).then_inc(rs_p, 1)
            pool.wait_ge(rs_p, 1)
            tt(rs_y[:, 2], rs_y[:, 1], stat[:, 63:64].to_broadcast([P, T]), ALU.pow).then_inc(rs_p, 1)
            for m in range(1, 2 * KE, 2):
                if N_OUT2 + m // 2 + 2 < N_END:
                    split(N_OUT2 + m // 2 + 2)
            for t in range(T):
                pool.wait_ge(f_ss, t + 1)
                nc.gpsimd.tensor_scalar(stat[:, 16 + t:17 + t], stat[:, t:t + 1], 1.0 / D, EPS,
                                        ALU.mult, ALU.add).then_inc(f_rs, 1)
                pool.wait_ge(f_rs, 2 * t + 1)
                tt(stat[:, 32 + t:33 + t], stat[:, 16 + t:17 + t], stat[:, 63:64], ALU.pow).then_inc(f_rs, 1)

        @block.vector
        def _(dve):
            tt, ts, stt = nc.vector.tensor_tensor, nc.vector.tensor_scalar, nc.vector.scalar_tensor_tensor

            def norm(l):
                def lo(t):
                    for q in range(2):
                        dve.wait_ge(r_hi[l], 2 * t + q + 1)
                        cols = (slice(None), slice(4 * q, 4 * q + 4), slice(t * P, (t + 1) * P))
                        tt(xTl[cols], ps[:, 2 * (t % 2) + q].rearrange("p (k s) -> p k s", k=4),
                           xTh[cols].bitcast(F), ALU.subtract).then_inc(r_lo[l], 1)
                for t in range(T):
                    if t == 0:
                        dve.wait_ge(rw_ld[l], 16)
                    dve.wait_ge(r_rs[l], 2 * t + 2)
                    if t >= 2:
                        dve.wait_ge(r_ps[l], 2 * t - 2)
                    stt(r_n[:, t % 2], r_x[:, t % 2], stat[:, 32 + t:33 + t], r_w, ALU.mult,
                        ALU.mult).then_inc(r_xn[l], 1)
                    if t >= 1:
                        lo(t - 1)
                lo(T - 1)

            norm(0)

            def conv(q):
                dve.wait_ge(c_ld, 16 * (len(C_NAMES) + 4))
                if later(q):
                    dve.wait_ge(a_conv, 8 * q)
                nc.vector.tensor_copy(tap4[:], taps[:, bass.ds(q * 4 * TAPS, 4 * TAPS)]).then_inc(a_tap4, 1)
                dve.wait_ge(a_tap4, q + 1)
                for pp in range(2):
                    p = 2 * q + pp
                    base = 2 * TAPS * p

                    def w(b, k):
                        return tap4[:, (2 * pp + b) * TAPS + k:(2 * pp + b) * TAPS + k + 1]

                    for b in range(2):
                        i = 2 * p + b
                        dve.wait_ge(a_um, 2 * i + 2)
                        for h in range(2):
                            if later(p):
                                dve.wait_ge(a_cv, 4 * p - 4 + 2 * b + h + 1)
                            ts(ps[:, 4 + 2 * b + h], upad[:, 2 * pp + b, HALF * h:HALF * (h + 1)], w(b, 0), None,
                               ALU.mult).then_inc(a_tap, 1)
                    for k in range(1, TAPS - 1):
                        for b in range(2):
                            dve.wait_ge(a_tap, base + (2 * (b + 1) if k == 1 else 4 + 2 * (k - 2) + b + 1))
                            acc = ps[:, 4 + 2 * b:6 + 2 * b].rearrange("p a s -> p (a s)")
                            stt(acc, upad[:, 2 * pp + b, k:k + S], w(b, k), acc, ALU.mult, ALU.add).then_inc(a_tap, 1)
                    for b in range(2):
                        dve.wait_ge(a_tap, base + 4 + 2 * (TAPS - 3) + b + 1)
                        for h in range(2):
                            acc = ps[:, 4 + 2 * b + h]
                            k = TAPS - 1
                            stt(acc, upad[:, 2 * pp + b, k + HALF * h:k + HALF * (h + 1)], w(b, k), acc, ALU.mult,
                                ALU.add).then_inc(a_conv, 1)
            loop(dve, KE // 4, conv)

            dve.wait_ge(l_mean, 2)
            dve.wait_ge(a_cv, 2 * KE)
            for k in range(KE):
                tt(cv[:, k], cv[:, k], ps[:, 0:2].rearrange("p a s -> p (a s)"), ALU.subtract).then_inc(l_xc, 1)
            for h in range(2):
                dve.wait_ge(l_std, h + 1)
                nc.vector.reciprocal(rstd[:, HALF * h:HALF * (h + 1)], rstd[:, HALF * h:HALF * (h + 1)]).then_inc(l_rstd, 1)
            dve.wait_ge(l_rstd, 2)

            def mul(k):
                tt(cv[:, k], cv[:, k], rstd, ALU.mult).then_inc(n_mul, 1)

            def y_lo(l, m, src, scale):
                dve.wait_ge(o_hi[l], m + 1)
                if scale is None:
                    tt(xTl[:, m % 2], src, xTh[:, m % 2].bitcast(F), ALU.subtract).then_inc(o_lo[l], 1)
                else:
                    stt(xTl[:, m % 2], src, scale, xTh[:, m % 2].bitcast(F), ALU.mult, ALU.subtract).then_inc(o_lo[l], 1)

            mul(0)
            mul(1)

            def residual(h):
                dve.wait_ge(xr_ld[h], 16)
                for t in range(T):
                    dve.wait_ge(o_t[0], T * h + t + 1)
                    tt(xres[:, t], ps[:, t], xres[:, t], ALU.add).then_inc(o_h[0], 1)

            for m in range(2 * KE):
                if m + 2 < KE:
                    mul(m + 2)
                y_lo(0, m, cv[:, m % KE], None)
                if m == KE:
                    residual(0)
            residual(1)

            norm(1)

            steps = [0]

            def step(ins):
                steps[0] += 1
                ins.then_inc(d_v, 1)
                dve.wait_ge(d_v, steps[0])

            dve.wait_ge(d_ps, 1)
            tt(dtt[:, 0].rearrange("p (t h) -> p t h", t=T), ps[:, 7].rearrange("p (t h) -> p t h", t=T),
               hrow[:, 0:2 * H].unsqueeze(1).to_broadcast([P, T, 2 * H]), ALU.add).then_inc(d_dt, 1)
            v, w1, e, r2, _, _ = (dtt[:, n] for n in range(6))
            dve.wait_ge(d_exp, 1)
            step(ts(r2, e, 2.0, None, ALU.add))
            step(nc.vector.reciprocal(w1, r2))
            step(tt(e, e, w1, ALU.mult))
            step(tt(r2, e, e, ALU.mult))
            step(ts(w1, r2, 1.0 / 17, None, ALU.mult))
            for j in range(7, 0, -1):
                step(stt(w1, w1, 1.0 / (2 * j + 1), r2, ALU.add, ALU.mult))
            step(stt(w1, w1, 1.0, e, ALU.add, ALU.mult))
            step(ts(v, v, 0.0, None, ALU.max))
            step(stt(dt_s.rearrange("p t h -> p (t h)"), w1, 2.0, v, ALU.mult, ALU.add))
            dve.wait_ge(d_A, 1)
            for n in range(2):
                stt(a2[:, :, n], dt_s, -1.0, arow[:].unsqueeze(1).to_broadcast([P, T, 2 * H]), ALU.mult,
                    ALU.mult).then_inc(d_a, 1)

            def taps5(j, b):
                i = 2 * j + b
                acc = ps[:, 2 + 2 * b:4 + 2 * b].rearrange("p a s -> p (a s)")
                dve.wait_ge(b_evac, 2 * i + 2)
                if later(j):
                    dve.wait_ge(b_sil, i - 1)
                for k in range(CTAPS):
                    wk = ctaps[:, bass.ds(i * CTAPS + k, 1)]
                    if k == 0:
                        ts(acc, cpad[:, b, 0:S], wk, vec[:, bass.ds(V_CB + i, 1)], ALU.mult, ALU.add).then_inc(b_tap, 1)
                    else:
                        dve.wait_ge(b_tap, CTAPS * i + k)
                        stt(acc, cpad[:, b, k:k + S], wk, acc, ALU.mult, ALU.add).then_inc(b_tap, 1)

            def xside(j):
                taps5(j, 0)
                taps5(j, 1)
            loop(dve, KE // 2, xside)
            dve.wait_ge(d_se, 2)
            nc.vector.tensor_copy(w1, ps[:, 4]).then_inc(d_v, 1)
            steps[0] += 1
            dve.wait_ge(d_v, steps[0])
            tt(v, ps[:, 5], w1, ALU.subtract).then_inc(d_sc, 1)
            dve.wait_ge(d_se, 4)
            tt(coef_s.rearrange("p t h -> p (t h)"), dtt[:, 5], dt_s.rearrange("p t h -> p (t h)"),
               ALU.mult).then_inc(d_coef, 1)

            def decay_rows():
                for u in range(2):
                    cs = slice(4 * u, 4 * u + 4)
                    dve.wait_ge(d_trh, u + 1)
                    for d in range(2):
                        rows_ = slice(64 + 32 * d, 96 + 32 * d)
                        tt(acs_hl[rows_, cs], ps[rows_, 4 + d].rearrange("p (t l) -> p t l", t=4),
                           acs_hi[rows_].bitcast(F), ALU.subtract).then_inc(d_trl, 1)

            for g in range(G):
                if g == 0:
                    decay_rows()
                taps5(KE // 2 + g, 0)
                taps5(KE // 2 + g, 1)

            dve.wait_ge(q_st, 16 * G)
            nc.vector.memset(sf, 0.0).then_inc(p_s, 1)
            dve.wait_ge(p_s, 1)
            for r, c in enumerate(range(T - 1, 0, -1)):
                old, new = ((sf, sbk), (sbk, sf))[r % 2]
                if r >= 1:
                    dve.wait_ge(p_st[(r + 1) % 2], 16 * ((r - 1) // 2 + 1))
                    dve.wait_ge(p_s, r + 1)
                tt(new.rearrange("p (h e) -> p h e", h=H), old.rearrange("p (h e) -> p h e", h=H),
                   bcast(dec_s[:, c, H:2 * H], HD), ALU.mult).then_inc(p_dec, 1)
                dve.wait_ge(p_dec, r + 1)
                dve.wait_ge(p_mm, r + 1)
                tt(new, new, ps[:, 0:4].rearrange("p a s -> p (a s)"), ALU.add).then_inc(p_s, 1)

            dve.wait_ge(p_st[0], 16 * T // 2)
            nc.vector.memset(sf, 0.0).then_inc(s_zero, 1)

            def heads(v_):
                return v_.rearrange("p (h e) -> p h e", h=8)

            def head_col(tab, c, col):
                return bcast(tab.rearrange("p t h -> p (t h)")[:, bass.ds(c * 2 * H + col, 8)], HD)

            def chunk(c2):
                for b in range(2):
                    c = 2 * c2 + b
                    if later(c):
                        dve.wait_ge(s_M, 16 * c)
                    nc.vector.tensor_copy(dtc, dt_s.rearrange("p t h -> p (t h)")[:, bass.ds(c * 2 * H, 2 * H)]).then_inc(s_dc, 1)

                    def from_states(g):
                        dve.wait_ge(s_yo, 8 * c + 2 * g + 1)
                        if later(c):
                            dve.wait_ge(s_g, 4 * c + g - 3)
                        tt(heads(yacc[:, HALF * g:HALF * (g + 1)]), heads(ps[:, 1]), head_col(e_s, c, 8 * g),
                           ALU.mult).then_inc(s_ya, 1)
                        dve.wait_ge(s_yo, 8 * c + 2 * g + 2)
                        if g >= 2 or later(c):
                            dve.wait_ge(s_ad, 4 * c + g - 1)
                        tt(heads(tmpb[:, g % 2]), heads(ps[:, 2]), head_col(e_s, c, H + 8 * g),
                           ALU.mult).then_inc(s_tb, 1)

                    def masked(u):
                        hq, d = divmod(u, 2)
                        if u == 0:
                            dve.wait_ge(s_dc, c + 1)
                            dve.wait_ge(s_cb, c + 1)
                        dve.wait_ge(s_ex, 16 * c + u + 1)
                        if u >= 4 or later(c):
                            dve.wait_ge(s_yd, 8 * c + hq - 1)
                        for n in range(4):
                            col = d * H + 4 * hq + n
                            last = stt(Mb[:, u % 4, n], Lb[:, u % 2, n], dtc[:, col:col + 1],
                                       ps[:, 0, P * (hq // 2):P * (hq // 2 + 1)], ALU.mult, ALU.mult)
                        last.then_inc(s_M, 1)

                    def diag(g):
                        dve.wait_ge(s_yd, 8 * c + 2 * g + 2)
                        dve.wait_ge(s_ad, 4 * c + g + 1)
                        tt(yacc[:, HALF * g:HALF * (g + 1)], ps[:, 5 + g % 2], yacc[:, HALF * g:HALF * (g + 1)],
                           ALU.add).then_inc(s_dd, 1)

                    def state(g):
                        cols = slice(HALF * g, HALF * (g + 1))
                        dve.wait_ge(s_yo, 8 * c + 2 * g + 1)
                        if later(c):
                            dve.wait_ge(s_S, 4 * c + g - 3)
                        tt(heads(sf[:, cols]), heads(sf[:, cols]), head_col(dec_s, c, 8 * g), ALU.mult).then_inc(s_sd, 1)
                        dve.wait_ge(s_sd, 4 * c + g + 1)
                        dve.wait_ge(s_stt, 4 * c + g + 1)
                        tt(sf[:, cols], sf[:, cols], ps[:, 7], ALU.add).then_inc(s_S, 1)

                    from_states(0)
                    for hq in range(8):
                        masked(2 * hq)
                        masked(2 * hq + 1)
                        if hq in (1, 3, 5):
                            from_states((hq + 1) // 2)
                        if hq >= 4:
                            state(hq - 4)
                        if hq in (2, 4, 6):
                            diag(hq // 2 - 1)
                    diag(3)
            loop(dve, T // 2, chunk)

            dve.wait_ge(s_sq, 4 * T)
            nc.vector.tensor_reduce(rs_y[:, 0], ss_y, mybir.AxisListType.X, ALU.add).then_inc(rs_r, 1)

            def residual2(h):
                dve.wait_ge(xr_ld[0], 32)
                if h == 0:
                    dve.wait_ge(rs_p, 2)
                for t in range(T):
                    dve.wait_ge(o_t[1], T * h + t + 1)
                    cols = hf[:, t, HALF * h:HALF * (h + 1)]
                    stt(cols, ps[:, t], rs_y[:, 2, t:t + 1], cols, ALU.mult, ALU.add).then_inc(o_h[1], 1)

            for m in range(2 * KE):
                y_lo(1, m, y_ld[:, m % 2], vec[:, V_SNW + m % KE:V_SNW + m % KE + 1])
                if m == KE:
                    residual2(0)
            residual2(1)
            for t in range(T):
                if t == 0:
                    dve.wait_ge(rw_ld[2], 16)
                dve.wait_ge(f_rs, 2 * t + 2)
                if t >= 2:
                    dve.wait_ge(f_st[t % 2], 16 * (t // 2))
                stt(f_o[:, t % 2], hf[:, t], stat[:, 32 + t:33 + t], f_w, ALU.mult, ALU.mult).then_inc(f_out, 1)

        @block.tensor
        def _(pe):
            def mm3(dst, lh, ll, rh, rl, start, stop):
                mm(dst, ll, rh, start=start, stop=False)
                mm(dst, lh, rl, start=False, stop=False)
                return mm(dst, lh, rh, start=False, stop=stop)

            def norm(l):
                for t in range(T):
                    pe.wait_ge(r_xn[l], t + 1)
                    for q in range(2):
                        if t >= 2:
                            pe.wait_ge(r_lo[l], 2 * (t - 2) + q + 1)
                        for k in range(4):
                            last = nc.tensor.transpose(ps[:, 2 * (t % 2) + q, P * k:P * (k + 1)],
                                                       r_n[:, t % 2, P * (4 * q + k):P * (4 * q + k + 1)],
                                                       c_f["ident"][:])
                        last.then_inc(r_ps[l], 1)

            def by_channel(n, h, bank, sem_):
                cols = slice(HALF * h, HALF * (h + 1))
                for k in range(KD):
                    wc = slice(P * k, P * (k + 1))
                    last = mm3(ps[:, bank], wh[:, n % 2, wc], wl[:, n % 2, wc], xTh[:, k, cols], xTl[:, k, cols],
                               k == 0, k == KD - 1)
                last.then_inc(sem_, 1)

            pe.wait_ge(c_ld, 16 * (len(C_NAMES) + 4))
            norm(0)
            pe.wait_ge(r_lo[0], 2 * T)

            def conf(p):
                for b in range(2):
                    for j in range(3):
                        n = 3 * b + j
                        pe.wait_ge(w_lo, 6 * p + n + 1)
                        for h in range(2):
                            f = 6 * b + 2 * j + h
                            if not isinstance(p, int) or f >= 4:
                                pe.wait_ge(a_evac, 12 * p + f - 3)
                            by_channel(n, h, f % 4, a_fill)
            loop(pe, KE // 2, conf)

            pe.wait_ge(a_csum, KE)
            pe.wait_ge(a_evac, 6 * KE)
            for h in range(2):
                mm(ps[:, h], c_f["mean"][:], csum[:, HALF * h:HALF * (h + 1)], start=True, stop=True).then_inc(l_mean, 1)
            for k in range(KE):
                pe.wait_ge(l_sq, k + 1)
                for h in range(2):
                    last = mm(ps[:, 2 + h], c_f["mean"][:], sqb[:, k % 2, HALF * h:HALF * (h + 1)],
                              start=k == 0, stop=k == KE - 1)
                last.then_inc(l_var, 1)

            def out_product(l, n0, bank_free):
                for h in range(2):
                    def pair(kp, first=False, final=False):
                        for kk in range(2):
                            m = KE * h + 2 * kp + kk
                            if kk == 0:
                                pe.wait_ge(w_lo, n0 + KE // 2 * h + kp + 1)
                            pe.wait_ge(o_lo[l], m + 1)
                            for t in range(T):
                                if first and kk == 0:
                                    if h:
                                        pe.wait_ge(o_h[l], t + 1)
                                    elif t == 0:
                                        bank_free()
                                tc = slice(P * t, P * (t + 1))
                                wc = slice(HALF * kk, HALF * (kk + 1))
                                s_ = (n0 + KE // 2 * h + parity(kp)) % 2
                                last = mm3(ps[:, t], xTh[:, kk, tc], xTl[:, kk, tc], wh[:, s_, wc], wl[:, s_, wc],
                                           first and kk == 0, final and kk == 1)
                                if final and kk == 1:
                                    last.then_inc(o_t[l], 1)
                            if not (final and kk == 1):
                                last.then_inc(o_mm[l], 1)
                    par = [0]

                    def parity(kp):
                        return par[0]
                    par[0] = 0
                    pair(0, first=True)
                    with pe.Fori(0, KE // 4 - 1) as i:
                        par[0] = 1
                        pair(2 * i + 1)
                        par[0] = 0
                        pair(2 * i + 2)
                    par[0] = 1
                    pair(KE // 2 - 1, final=True)

            out_product(0, N_OUT1, lambda: (pe.wait_ge(l_std, 2), pe.wait_ge(a_cv, 2 * KE)))

            norm(1)

            pe.wait_ge(w_lo, N_DT + 1)
            pe.wait_ge(r_lo[1], 2 * T)
            s_ = N_DT % 2
            for t in range(T):
                for k in range(KD):
                    tc, wc = slice(P * t, P * (t + 1)), slice(2 * H * k, 2 * H * (k + 1))
                    last = mm3(ps[:, 7, 2 * H * t:2 * H * (t + 1)], xTh[:, k, tc], xTl[:, k, tc],
                               wh[:, s_, wc], wl[:, s_, wc], k == 0, k == KD - 1)
            last.then_inc(d_ps, 1)

            def fill(j, b):
                i = 2 * j + b
                pe.wait_ge(w_lo, N_XBC + i + 1)
                for h in range(2):
                    if later(j) or b:
                        pe.wait_ge(b_evac, 2 * i + h - 1)
                    by_channel(N_XBC + b, h, h, b_fill)

            def turn(done, b, sil_count, evac_count):
                pe.wait_ge(b_sil, sil_count)
                for h in range(2):
                    if evac_count is not None:
                        pe.wait_ge(b_te, evac_count + h)
                    for t in range(4):
                        last = nc.tensor.transpose(ps[:, 6 + h, P * t:P * (t + 1)],
                                                   csil[:, b, P * (4 * h + t):P * (4 * h + t + 1)], c_f["ident"][:])
                    last.then_inc(b_tr, 1)

            def xside(j):
                fill(j, 0)
                if later(j):
                    turn(None, 1, 2 * j, 4 * j - 3)
                else:
                    pe.wait_ge(d_dt, 1)
                fill(j, 1)
                turn(None, 0, 2 * j + 1, 4 * j - 1 if later(j) else None)
            loop(pe, KE // 2, xside)
            turn(None, 1, KE, 2 * KE - 3)
            a_ = a2[:, :, 0]
            pe.wait_ge(d_a, 2)
            acs = ps[:, 4].rearrange("p (t h) -> p t h", t=T)
            mm(acs[:, :, 0:H], c_f["upto"][:], a_[:, :, 0:H], start=True, stop=True).then_inc(d_acs, 1)
            mm(acs[:, :, H:2 * H], c_f["from_"][:], a_[:, :, H:2 * H], start=True, stop=True).then_inc(d_acs, 1)
            mm(ps[:, 5].rearrange("p (t h) -> p t h", t=T), c_f["ones"][:], a_, start=True, stop=True).then_inc(d_acs, 1)
            fill(KE // 2, 0)
            for u in range(2):
                if u == 0:
                    pe.wait_ge(d_se, 4)
                else:
                    pe.wait_ge(d_trl, 2)
                for d, tri in enumerate(("upto", "from_")):
                    for c in range(4):
                        last = mm(ps[:, 4 + d, P * c:P * (c + 1)],
                                  a2[:, 4 * u + c].rearrange("p n h -> p (n h)"), c_f[tri][:],
                                  start=True, stop=True)
                    last.then_inc(d_tr, 1)
            for g in range(G):
                if g:
                    fill(KE // 2 + g, 0)
                fill(KE // 2 + g, 1)
                turn(None, 0, KE + 2 * g + 1, 2 * KE + 2 * g - 1)

            for q in range(G):
                for kp in range(4):
                    n = N_Z + 4 * q + kp
                    pe.wait_ge(w_lo, n + 1)
                    for kk in range(2):
                        for t in range(T):
                            if kp == 0 and kk == 0:
                                if q:
                                    pe.wait_ge(q_sil, T * (q - 1) + t + 1)
                                elif t == 0:
                                    pe.wait_ge(b_te, 2 * (KE + G))
                                    pe.wait_ge(b_sil, NXBC)
                            k = 2 * kp + kk
                            tc, wc = slice(P * t, P * (t + 1)), slice(HALF * kk, HALF * (kk + 1))
                            last = mm3(ps[:, t], xTh[:, k, tc], xTl[:, k, tc], wh[:, n % 2, wc], wl[:, n % 2, wc],
                                       k == 0, k == KD - 1)
                            if k == KD - 1:
                                last.then_inc(q_t, 1)
                    if kp < 3:
                        last.then_inc(q_mm, 1)

            pe.wait_ge(q_sil, T * G)
            for r in range(T - 1):
                b = r % 2
                pe.wait_ge(p_b[b], 16 * (r // 2 + 1))
                pe.wait_ge(p_xb, r + 1)
                if r:
                    pe.wait_ge(p_s, r + 1)
                for g in range(G):
                    last = mm(ps[:, g], bc_s[:, b, 2, g], xb_s[:, HALF * g:HALF * (g + 1)], start=True, stop=True)
                last.then_inc(p_mm, 1)

            pe.wait_ge(p_s, T)
            pe.wait_ge(cr, 1)

            def chunk(c2):
                for b in range(2):
                    c = 2 * c2 + b

                    def decay(u):
                        hq, d = divmod(u, 2)
                        if u >= 2 or later(c):
                            pe.wait_ge(s_ex, 16 * c + u - 1)
                        bank = 3 + u % 2
                        for e in range(4):
                            col = d * H + 4 * hq + e
                            mm(ps[:, bank, P * e:P * (e + 1)], pickR[:, col:col + 1].to_broadcast([P, P]),
                                      acs_hl[:, bass.ds(c, 1)].rearrange("p a l -> p (a l)"), start=e == 0, stop=False,
                               skip_group_check=True)
                        mm(ps[:, bank].rearrange("p (e l) -> p e l", e=4), identR[:],
                           negR[:, d].unsqueeze(1).to_broadcast([P, 4, P]), start=False, stop=True,
                           skip_group_check=True).then_inc(s_L, 1)

                    def from_states(g):
                        cols = slice(HALF * g, HALF * (g + 1))
                        if g or later(c):
                            pe.wait_ge(s_ya, 4 * c + g)
                        if g == 0:
                            pe.wait_ge(s_zero, 1) if not later(c) else pe.wait_ge(s_S, 4 * c)
                        mm(ps[:, 1], bc_s[:, b, 1, g], sf[:, cols], start=True, stop=True).then_inc(s_yo, 1)
                        if g == 0:
                            pe.wait_ge(s_s, 16 * (c + 1))
                        if g or later(c):
                            pe.wait_ge(s_tb, 4 * c + g)
                        mm(ps[:, 2], bc_s[:, b, 1, g], sbk[:, cols], start=True, stop=True).then_inc(s_yo, 1)

                    def inside(hq):
                        g = hq // 2
                        if hq % 2 == 0:
                            if g >= 2 or later(c):
                                pe.wait_ge(s_dd, 4 * c + g - 1)
                        for d in range(2):
                            u = 2 * hq + d
                            pe.wait_ge(s_M, 16 * c + u + 1)
                            for n in range(4):
                                h8 = 4 * (hq % 2) + n
                                last = mm(ps[:, 5 + g % 2, HD * h8:HD * (h8 + 1)], Mb[:, u % 4, n],
                                          xs_s[:, b, HD * (8 * g + h8):HD * (8 * g + h8 + 1)],
                                          start=hq % 2 == 0 and d == 0 and n == 0, stop=False, skip_group_check=True)
                        if hq % 2:
                            pe.wait_ge(s_xD, 4 * c + g + 1)
                            last = mm(ps[:, 5 + g % 2], c_f["ident"][:], xD[:, g % 2], start=False, stop=True,
                                      skip_group_check=True)
                        last.then_inc(s_yd, 1)

                    def state(g):
                        pe.wait_ge(s_xf, 4 * c + g + 1)
                        if g:
                            pe.wait_ge(s_S, 4 * c + g)
                        elif later(c):
                            pe.wait_ge(s_te, 4 * c)
                        mm(ps[:, 7], bc_s[:, b, 2, g], xf_s[:, g % 2], start=True, stop=True).then_inc(s_stt, 1)

                    if b == 0:
                        pe.wait_ge(s_x[0], 16 * (c2 + 1))
                    else:
                        pe.wait_ge(s_x[1], 16 * (c2 + 1))
                    pe.wait_ge(s_b[b], 16 * (c2 + 1))
                    if later(c):
                        pe.wait_ge(s_M, 16 * c)
                    for g in range(G):
                        last = mm(ps[:, 0, P * g:P * (g + 1)], bc_s[:, b, 0, g], bc_s[:, b, 1, g], start=True, stop=True)
                    last.then_inc(s_cb, 1)
                    decay(0)
                    decay(1)
                    from_states(0)
                    for hq in range(8):
                        if hq < 7:
                            decay(2 * hq + 2)
                            decay(2 * hq + 3)
                        if hq < 4 and later(c):
                            turn_y(c - 1, hq)
                        if hq in (1, 3, 5):
                            from_states((hq + 1) // 2)
                        if hq >= 4:
                            state(hq - 4)
                        inside(hq)

            def turn_y(c, i):
                pe.wait_ge(s_g, 4 * c + i + 1)
                if i:
                    pe.wait_ge(s_te, 4 * c + i)
                else:
                    pe.wait_ge(s_S, 4 * c + 4)
                for n in range(4):
                    j = 4 * i + n
                    last = nc.tensor.transpose(ps[:, 7, P * n:P * (n + 1)], z_s[:, P * j:P * (j + 1)], c_f["ident"][:])
                last.then_inc(s_tr, 1)

            loop(pe, T // 2, chunk)
            for i in range(4):
                turn_y(T - 1, i)
            out_product(1, N_OUT2, lambda: (pe.wait_ge(s_te, 4 * T), pe.wait_ge(s_dd, 4 * T)))


def kernel(**inputs):
    import numpy as np
    import concourse.bacc as bacc
    from concourse.bass_utils import run_bass_kernel_spmd

    f = {k: np.asarray(v) for k, v in inputs.items()}

    def by_channel(w):
        return w.reshape(KD, P, -1, P).transpose(2, 1, 0, 3).reshape(-1, P, W)

    def by_token(w, cols=HALF):
        k = w.shape[0] // P
        return w.reshape(k // 2, 2, P, -1, cols).transpose(3, 0, 2, 1, 4).reshape(-1, P, 2 * cols)

    w_in = by_channel(f["cm_w_in"][0]).reshape(3, KE, P, W)[[1, 0, 2]].transpose(1, 0, 2, 3).reshape(-1, P, W)
    s_in = f["ssd_w_in"][0]
    nx = E + 2 * G * P
    order = list(range(KE)) + [KE + k * G + g for g in range(G) for k in range(2)]
    w_xbc = by_channel(s_in[:, E:E + nx])[order]
    w_dt = np.zeros((1, P, W), np.float32)
    w_dt[0, :, :KD * 2 * H] = s_in[:, E + nx:].reshape(KD, P, 2 * H).transpose(1, 0, 2).reshape(P, -1)
    wst = np.concatenate([w_in, by_token(f["cm_w_out"][0]), w_dt, w_xbc, by_token(s_in[:, :E]),
                          by_token(f["ssd_w_out"][0])])

    def col(v):
        return v.reshape(-1, P).T

    cvec = np.concatenate([col(f["cm_dw_b"][0]), col(f["cm_ln_w"][0]), col(f["cm_ln_b"][0]),
                           col(f["ssd_conv_b"][0])[:, order], col(f["ssd_norm_w"][0])], axis=1)
    dww = f["cm_dw_w"][0].reshape(TAPS, KE, P).transpose(2, 1, 0).reshape(P, -1)
    cw = f["ssd_conv_w"][0].reshape(CTAPS, NXBC, P)[:, order].transpose(2, 1, 0).reshape(P, -1)
    rows = np.concatenate([f["norm_w"], f["final_norm_w"][None]])
    srow = np.concatenate([f["ssd_dt_bias"].reshape(1, -1), f["ssd_A_log"].reshape(1, -1), f["ssd_D"].reshape(1, -1)],
                          axis=1)
    i = np.arange(P)
    tri = {"ident": i[:, None] == i, "upto": i[:, None] <= i, "from_": i[:, None] >= i, "ones": i[:, None] >= 0 * i}
    consts = {n: m.astype(np.float32) for n, m in tri.items()}
    consts["mean"] = np.full((P, P), 1.0 / E, np.float32)
    consts["neg_f"] = np.where(i[:, None] <= i, 0.0, -1e30).astype(np.float32)
    consts["neg_b"] = np.where(i[:, None] >= i, 0.0, -1e30).astype(np.float32)
    consts["pick"] = (i[:, None] % (2 * H) == np.arange(2 * H)).astype(np.float32)

    arrays = {"wst": wst, "x": f["x"].reshape(T, P, D), "cvec": cvec, "dww": dww, "cw": cw, "rows": rows,
              "srow": srow, **{"c_" + n: m for n, m in consts.items()}}
    arrays = {n + "_dram": np.ascontiguousarray(a) for n, a in arrays.items()}
    nc = bacc.Bacc("TRN2", target_bir_lowering=False, num_devices=1)
    aps = {n[:-5]: nc.dram_tensor(n, a.shape, mybir.dt.float32, kind="ExternalInput").ap() for n, a in arrays.items()}
    out = nc.dram_tensor("out_dram", (T, P, D), mybir.dt.float32, kind="ExternalOutput").ap()
    cst = {n: aps.pop("c_" + n) for n in C_NAMES}
    program(nc, out=out, cst=cst, **aps)
    r = run_bass_kernel_spmd(nc, [arrays], core_ids=[0])
    return r.results[0]["out_dram"].reshape(1, S, D)
```

```python
from contextlib import ExitStack

import concourse.bass as bass
from concourse import mybir

F = mybir.dt.float32
R = mybir.dt.float32r
ALU = mybir.AluOpType
ACT = mybir.ActivationFunctionType

P = 128
D = 1024
S = 1024
E = 2048
KD = D // P
KE = E // P
T = S // P
TAPS = 31
PAD = (TAPS - 1) // 2
CTAPS = 5
CPAD = (CTAPS - 1) // 2
H = 32
HD = 64
G = 4
NXBC = KE + 2 * G
EPS = 1e-5
HALF = 512
ZLAG = 4
LOOK = 4
YR = 4
W = KD * P
UP = S + 2 * PAD + 2
CP = S + 2 * CPAD

N_CONF = 0
N_OUT1 = 3 * KE
N_DT = N_OUT1 + KE
N_XBC = N_DT + 1
N_Z = N_XBC + NXBC
N_OUT2 = N_Z + KE
N_END = N_OUT2 + KE

V_DWB, V_LNW, V_LNB, V_CB, V_SNW = 0, KE, 2 * KE, 3 * KE, 3 * KE + NXBC
NV = V_SNW + KE
C_NAMES = ["ident", "upto", "from_", "ones", "mean", "neg_f", "neg_b", "pick"]


def loop(engine, n, body):
    body(0)
    with engine.Fori(1, n) as i:
        body(i)


def later(i):
    return not isinstance(i, int) or i > 0


def program(nc, wst, x, cvec, dww, cw, rows, srow, cst, out):
    with ExitStack() as ctx:
        def sb(name, shape, dt=F):
            return ctx.enter_context(nc.sbuf_tensor(name, shape, dt))

        def sem(name):
            return ctx.enter_context(nc.semaphore(name))

        def dram(name, shape):
            return nc.dram_tensor(name, shape, F, kind="Internal").ap()

        z1_d = dram("z1_d", [KE, P, S])
        h_d = dram("h_d", [T, P, D])
        xs_d = dram("xs_d", [T, P, E])
        bc_d = dram("bc_d", [T, P, 3, G, P])
        z2_d = dram("z2_d", [T, P, E])

        wraw = sb("wraw", [P, 2, W])
        wh = sb("wh", [P, 2, W], R)
        wl = sb("wl", [P, 2, W], R)
        acs_hl = sb("acs_hl", [P, T, P], R)
        acs_hi = sb("acs_hi", [P, 4, P], R)
        identR = sb("identR", [P, P], R)
        negR = sb("negR", [P, 2, P], R)
        pickR = sb("pickR", [P, 2 * H], R)
        c_f = {n: sb("c_" + n, [P, P if n != "pick" else 2 * H]) for n in C_NAMES}
        vec = sb("vec", [P, NV])
        taps = sb("taps", [P, KE * TAPS])
        ctaps = sb("ctaps", [P, NXBC * CTAPS])
        hrow = sb("hrow", [P, 5 * H])
        tap4 = sb("tap4", [P, 4 * TAPS])
        stat = sb("stat", [P, 64])
        arow = sb("arow", [P, 2 * H])
        AR = 26250
        with ExitStack() as first:
            xTh = first.enter_context(nc.sbuf_tensor("xTh", [P, KD, S], R))
            xTl = first.enter_context(nc.sbuf_tensor("xTl", [P, KD, S], R))
            arena = first.enter_context(nc.sbuf_tensor("arena", [P, AR], F))
        keep = sb("keep", [P, T, E])
        y2h = sb("y2h", [P, YR, S], R)
        y2l = sb("y2l", [P, YR, S], R)
        used = [0]

        def at(off, *shape):
            n = 1
            for s in shape:
                n *= s
            assert off + n <= AR, (off, shape)
            v = arena[:, off:off + n]
            names = "abcd"[:len(shape)]
            if len(shape) > 1:
                v = v.rearrange(f"p ({' '.join(names)}) -> p {' '.join(names)}",
                                **dict(zip(names, shape)))
            return v

        r_x = at(0, 2, D)
        r_n = at(2 * D, 2, D)
        r_w = at(4 * D, D)
        r_junk = at(5 * D, D)
        cv = at(0, KE, S)
        o = KE * S
        upad = at(o, 4, UP)
        xres = at(o, T, HALF)
        o += 4 * UP
        sigb = at(o, 2, HALF)
        vb = at(o + S, 2, HALF)
        sqb = at(o, 2, S)
        zst = at(o + 2 * S, 2, S)
        csum = at(o + 4 * S, S)
        rstd = csum
        cpad = at(0, 2, CP)
        csil = at(2 * CP, 2, S)
        stg = at(2 * CP + 2 * S, 2, T, P)
        z2b = at(2 * CP + 4 * S, T, HALF)
        dtt = at(2 * CP + 8 * S, 6, HALF)
        a2 = at(2 * CP + 8 * S + 6 * HALF, T, 2, 2 * H)
        o = 0
        xs_s = at(o, 2, E); o += 2 * E
        bc_s = at(o, 2, 3, G, P); o += 2 * 3 * G * P
        z_s = at(o, E); o += E
        sf = at(o, E); o += E
        xf_s = at(o, 2, HALF)
        xb_s = at(o, E)
        o += 2 * HALF
        tmpb = at(o, 2, HALF); o += 2 * HALF
        yacc = at(o, E); o += E
        xD = at(o, 2, HALF); o += 2 * HALF
        Lb = at(o, 4, 4, P); o += 4 * HALF
        Mb = at(o, 4, 4, P); o += 4 * HALF
        sqj = at(o, HALF); o += HALF
        o_small = max(o, 2 * CP + 8 * S + 8 * HALF)
        o = o_small
        dt_s = at(o, T, 2 * H); o += HALF
        e_s = at(o, T, 2 * H); o += HALF
        dec_s = at(o, T, 2 * H); o += HALF
        coef_s = at(o, T, 2 * H); o += HALF
        nacs_s = at(o, T, 2 * H); o += HALF
        dtc = at(o, 2 * H); o += 2 * H
        nac = at(o, 2 * H); o += 2 * H
        ss_y = at(o, T, G); o += T * G
        rs_y = at(o, 3, T); o += 3 * T
        o = 2 * YR * S
        hf = at(o, T, D); o += T * D
        f_w = at(o, D); o += D
        f_o = at(o, 2, D); o += 2 * D
        f_junk = at(o, D); o += D
        assert o <= o_small

        ps = ctx.enter_context(nc.psum_tensor("ps", [P, 8, HALF], F))

        c_ld = sem("c_ld")
        w_raw = [sem("w_raw0"), sem("w_raw1")]
        w_hi, w_lo = sem("w_hi"), sem("w_lo")
        cr = sem("cr")
        cr2 = sem("cr2")
        r_ld = [[sem(f"r{l}_ld0"), sem(f"r{l}_ld1")] for l in range(2)]
        rw_ld = [sem("rw_ld0"), sem("rw_ld1"), sem("rw_ld2")]
        r_ss = [sem(f"r{l}_ss") for l in range(2)]
        r_rs = [sem(f"r{l}_rs") for l in range(2)]
        r_xn = [sem(f"r{l}_xn") for l in range(2)]
        r_ps = [sem(f"r{l}_ps") for l in range(2)]
        r_hi = [sem(f"r{l}_hi") for l in range(2)]
        r_lo = [sem(f"r{l}_lo") for l in range(2)]
        a_fill, a_evac, a_um, a_tap, a_conv, a_cv, a_csum = (
            sem(n) for n in ("a_fill", "a_evac", "a_um", "a_tap", "a_conv", "a_cv", "a_csum"))
        a_tap4 = sem("a_tap4")
        a_pad = sem("a_pad")
        z_st = [sem("z_st0"), sem("z_st1")]
        z_ld = [sem("z_ld0"), sem("z_ld1")]
        l_mean, l_xc, l_sq, l_var, l_std, l_rstd = (
            sem(n) for n in ("l_mean", "l_xc", "l_sq", "l_var", "l_std", "l_rstd"))
        n_mul, n_silu, n_y = sem("n_mul"), sem("n_silu"), sem("n_y")
        n_zs = sem("n_zs")
        o_hi = [sem(f"o{l}_hi") for l in range(2)]
        o_lo = [sem(f"o{l}_lo") for l in range(2)]
        o_mm = [sem(f"o{l}_mm") for l in range(2)]
        o_t = [sem(f"o{l}_t") for l in range(2)]
        o_h = [sem(f"o{l}_h") for l in range(2)]
        xr_ld = [sem("xr_ld0"), sem("xr_ld1")]
        h_st = [sem("h_st0"), sem("h_st1")]
        d_ps, d_dt, d_neg, d_exp, d_A, d_a = (sem(n) for n in ("d_ps", "d_dt", "d_neg", "d_exp", "d_A", "d_a"))
        d_acs, d_sc, d_se, d_tr = sem("d_acs"), sem("d_sc"), sem("d_se"), sem("d_tr")
        d_trh, d_trl, d_coef = sem("d_trh"), sem("d_trl"), sem("d_coef")
        b_fill, b_evac, b_tap, b_sil, b_tr, b_te = (sem(n) for n in ("b_fill", "b_evac", "b_tap", "b_sil", "b_tr", "b_te"))
        b_pad = sem("b_pad")
        b_st = [sem("b_st0"), sem("b_st1")]
        b_sc = [sem("b_sc0"), sem("b_sc1")]
        q_mm, q_t, q_sil, q_st = sem("q_mm"), sem("q_t"), sem("q_sil"), sem("q_st")
        d_v = sem("d_v")
        p_x = [sem("p_x0"), sem("p_x1")]
        p_b = [sem("p_b0"), sem("p_b1")]
        p_xb, p_mm, p_dec, p_s = sem("p_xb"), sem("p_mm"), sem("p_dec"), sem("p_s")
        s_x = [sem("s_x0"), sem("s_x1")]
        s_b = [sem("s_b0"), sem("s_b1")]
        s_z = sem("s_z")
        s_cb, s_L, s_ex, s_M, s_yd, s_yo = (sem(n) for n in ("s_cb", "s_L", "s_ex", "s_M", "s_yd", "s_yo"))
        s_ya, s_tb, s_ad, s_xD, s_dd, s_g = (sem(n) for n in ("s_ya", "s_tb", "s_ad", "s_xD", "s_dd", "s_g"))
        s_xf, s_stt, s_sd, s_S, s_tr, s_te = (sem(n) for n in ("s_xf", "s_stt", "s_sd", "s_S", "s_tr", "s_te"))
        s_sq, s_dc, s_nc = sem("s_sq"), sem("s_dc"), sem("s_nc")
        s_zero = sem("s_zero")
        rs_r, rs_p = sem("rs_r"), sem("rs_p")
        f_ss, f_rs, f_out = sem("f_ss"), sem("f_rs"), sem("f_out")
        f_st = [sem("f_st0"), sem("f_st1")]

        block = ctx.enter_context(nc.Block())
        mm = nc.tensor.matmul

        def tile_done(l, m):
            if m % KE == KE - 1:
                return o_t[l], T * (m // KE + 1)
            return o_mm[l], m + 1 - m // KE

        def y_tile2(k):
            return keep[:].rearrange("p t (k s) -> p t k s", k=KE)[:, :, k]

        def bcast(ap, n):
            return ap.unsqueeze(2).to_broadcast([P, ap.shape[-1], n])

        @block.sync
        def _(sp):
            def wload(n, i=0, per=0):
                if not isinstance(i, int) or n + per * i >= 2:
                    sp.wait_ge(w_lo, n + per * i - 1)
                if isinstance(i, int):
                    src = wst[n + per * i]
                else:
                    src = wst[bass.ds(n + per * i, 1)].rearrange("a p w -> (a p) w")
                sp.dma_start(wraw[:, n % 2], src).then_inc(w_raw[n % 2], 16)

            def norm_loads(l, src):
                for t in range(T):
                    if t >= 2:
                        sp.wait_ge(r_xn[l], t - 1)
                    sp.dma_start(r_x[:, t % 2], src[t]).then_inc(r_ld[l][t % 2], 16)
                    if l == 0 and t == 1:
                        wload(0)
                        wload(1)

            norm_loads(0, x)

            def z_store(i, b, fills):
                sp.wait_ge(a_evac, fills)
                dst = z1_d[i] if isinstance(i, int) else z1_d[bass.ds(i, 1)].rearrange("a p s -> (a p) s")
                sp.dma_start(dst, zst[:, b]).then_inc(z_st[b], 16)

            for m in range(2 * ZLAG):
                wload(m + 2)

            def conf(p):
                for b in range(2):
                    for j in range(3):
                        wload(2 * ZLAG + 3 * b + j + 2, p, 6)
                    z_store(2 * p + b, b, 4 * ZLAG + 12 * p + 6 * b + 6)
            loop(sp, KE // 2 - 2, conf)
            for t in range(ZLAG):
                wload(6 * KE // 2 - ZLAG + t + 2)
                z_store(KE - ZLAG + t, t % 2, 6 * KE - 2 * ZLAG + 2 * t + 2)

            for b in range(2):
                sp.wait_ge(z_st[b], 16 * KE // 2)
            for k in range(2):
                sp.dma_start(zst[:, k], z1_d[k]).then_inc(z_ld[k], 16)
            sp.wait_ge(a_conv, 2 * KE)
            sp.dma_start(xres[:], x.rearrange("t p d -> p t d")[:, :, 0:HALF]).then_inc(xr_ld[0], 16)
            for k in range(KE):
                if k + 2 < KE:
                    sp.wait_ge(n_y, k + 1)
                    sp.dma_start(zst[:, k % 2], z1_d[k + 2]).then_inc(z_ld[k % 2], 16)
                if k in (0, 1) or k % 2 == 0 and k >= LOOK + YR:
                    wload(N_OUT1 + 2 + (k if k < 2 else 2 + (k - LOOK - YR) // 2))
            for h in range(2):
                for n in (range(N_OUT1 + 4 + (KE - LOOK - YR) // 2, N_OUT1 + 12), ())[h]:
                    wload(n)
                for t in range(T):
                    sp.wait_ge(o_h[0], T * h + t + 1)
                    sp.dma_start(h_d[t, :, HALF * h:HALF * (h + 1)], xres[:, t]).then_inc(h_st[h], 16)
                sp.wait_ge(h_st[h], 16 * T)
                if h == 0:
                    sp.dma_start(xres[:], x.rearrange("t p d -> p t d")[:, :, HALF:D]).then_inc(xr_ld[1], 16)
                    for n in range(N_OUT1 + 12, N_DT + 3):
                        wload(n)

            norm_loads(1, h_d)

            wload(N_DT + 3)

            def stores(n, b, what):
                sp.wait_ge(b_te, 4 * n + 2 * b + 2)
                dst = xs_d.rearrange("t p e -> p t e")[:, :, bass.ds((2 * n + b) * P, P)]
                sp.dma_start(dst, stg[:, b]).then_inc(b_st[b], 16)

            def xside(j):
                for b in range(2):
                    wload(N_XBC + 3 + b, j, 2)
                    if b == 0:
                        if later(j):
                            stores(j - 1, 1, None)
                    else:
                        stores(j, 0, None)
            loop(sp, KE // 2, xside)
            stores(KE // 2 - 1, 1, None)
            for g in range(G):
                wload(N_XBC + KE + 2 * g + 3)
                sp.wait_ge(b_sil, KE + 2 * g + 1)
                sp.dma_start(bc_d.rearrange("t p k g n -> p k g t n")[:, 0, g],
                             csil[:, 0].rearrange("p (t n) -> p t n", t=T)).then_inc(b_sc[0], 16)
                wload(N_XBC + KE + 2 * g + 4)
                sp.wait_ge(b_sil, KE + 2 * g + 2)
                sp.dma_start(bc_d.rearrange("t p k g n -> p k g t n")[:, 1, g],
                             csil[:, 1].rearrange("p (t n) -> p t n", t=T)).then_inc(b_sc[1], 16)
                sp.wait_ge(b_te, 2 * KE + 2 * g + 2)
                sp.dma_start(bc_d.rearrange("t p k g n -> p k g t n")[:, 2, g], stg[:, 0]).then_inc(b_st[0], 16)

            for q in range(G):
                for m in range(4):
                    if N_Z + 3 + 4 * q + m < N_OUT2 + 2:
                        wload(N_Z + 3 + 4 * q + m)
                sp.wait_ge(q_sil, T * (q + 1))
                sp.dma_start(z2_d.rearrange("t p e -> p t e")[:, :, HALF * q:HALF * (q + 1)],
                             z2b[:]).then_inc(q_st, 16)
            sp.wait_ge(q_st, 16 * G)
            for b in range(2):
                sp.wait_ge(b_st[b], 16 * (KE // 2 + (G if b == 0 else 0)))
                sp.wait_ge(b_sc[b], 16 * G)

            for r, c in enumerate(range(T - 1, 0, -1)):
                b = r % 2
                if r >= 2:
                    sp.wait_ge(p_mm, r - 1)
                sp.dma_start(xs_s[:, b], xs_d[c]).then_inc(p_x[b], 16)
                sp.dma_start(bc_s[:, b, 2], bc_d[c, :, 2]).then_inc(p_b[b], 16)
            sp.wait_ge(p_mm, T - 1)

            def src1(d, c):
                return d[c] if isinstance(c, int) else d[bass.ds(c, 1)].squeeze(0)

            def xb_loads(c, b):
                sp.dma_start(xs_s[:, b], src1(xs_d, c)).then_inc(s_x[b], 16)
                sp.dma_start(bc_s[:, b], src1(bc_d, c)).then_inc(s_b[b], 16)

            for b in range(2):
                xb_loads(b, b)
            sp.dma_start(z_s, z2_d[0]).then_inc(s_z, 16)

            def chunk_dma(c2):
                for b in range(2):
                    c = 2 * c2 + b
                    if later(c):
                        sp.wait_ge(s_te, 4 * c)
                        sp.dma_start(z_s, src1(z2_d, c)).then_inc(s_z, 16)
                        sp.wait_ge(s_g, 4 * c)
                        if not (isinstance(c, int) and c + 1 == T):
                            xb_loads(c + 1, 1 - b)
            chunk_dma(0)
            with sp.Fori(1, T // 2 - 1) as c2:
                chunk_dma(c2)
            chunk_dma(T // 2 - 1)

            sp.wait_ge(s_te, 4 * T)
            sp.wait_ge(s_S, 4 * T)
            sp.dma_start(hf[:], h_d.rearrange("t p d -> p t d")).then_inc(xr_ld[0], 16)
            for n in range(N_OUT2 + 2, N_END):
                wload(n)
            for t in range(T):
                sp.wait_ge(f_out, t + 1)
                sp.dma_start(out[t], f_o[:, t % 2]).then_inc(f_st[t % 2], 16)
            for b in range(2):
                sp.wait_ge(f_st[b], 16 * T // 2)

        @block.scalar
        def _(act):
            for name in C_NAMES:
                act.dma_start(c_f[name][:], cst[name]).then_inc(c_ld, 16)
            act.dma_start(r_w[:], rows[0:1, :].to_broadcast([P, D])).then_inc(rw_ld[0], 16)
            act.dma_start(vec[:], cvec).then_inc(c_ld, 16)
            act.dma_start(taps[:], dww).then_inc(c_ld, 16)
            act.dma_start(ctaps[:], cw).then_inc(c_ld, 16)
            act.dma_start(hrow[:], srow.to_broadcast([P, 5 * H])).then_inc(c_ld, 16)
            n_const = 16 * (len(C_NAMES) + 4)
            act.wait_ge(c_ld, n_const)
            nc.scalar.copy(identR[:], c_f["ident"][:])
            nc.scalar.copy(negR[:, 0], c_f["neg_f"][:])
            nc.scalar.copy(negR[:, 1], c_f["neg_b"][:])
            nc.scalar.copy(pickR[:], c_f["pick"][:]).then_inc(cr, 1)

            def split(n, i=0, per=0, free=None):
                act.wait_ge(w_raw[n % 2], 16 * (n // 2 + (per // 2) * i + 1))
                if free is not None:
                    act.wait_ge(*free)
                nc.scalar.copy(wh[:, n % 2], wraw[:, n % 2]).then_inc(w_hi, 1)

            def norm(l):
                def hi(t):
                    for q in range(2):
                        act.wait_ge(r_ps[l], 2 * t + q + 1)
                        nc.scalar.copy(xTh[:, 4 * q:4 * q + 4, t * P:(t + 1) * P],
                                       ps[:, 2 * (t % 2) + q].rearrange("p (k s) -> p k s", k=4)).then_inc(r_hi[l], 1)
                for t in range(T):
                    act.wait_ge(r_ld[l][t % 2], 16 * (t // 2 + 1))
                    if t >= 1:
                        act.wait_ge(r_ss[l], t)
                    nc.scalar.activation(r_junk[:], r_x[:, t % 2], ACT.Square,
                                         accum_out=stat[:, t:t + 1]).then_inc(r_ss[l], 1)
                    if t >= 1:
                        hi(t - 1)
                hi(T - 1)

            norm(0)
            split(0)
            split(1)

            def conv_out(p):
                for b in range(2):
                    for h in range(2):
                        i = 2 * p + b
                        act.wait_ge(a_conv, 4 * p + 2 * b + h + 1)
                        dst = arena[:, bass.ds(i * S + HALF * h, HALF)]
                        nc.scalar.activation(dst, ps[:, 4 + 2 * b + h], ACT.Identity,
                                             bias=vec[:, bass.ds(V_DWB + i, 1)]).then_inc(a_cv, 1)

            def evac(m, i, per, kind, tile):
                n = m + per * i
                for h in range(2):
                    act.wait_ge(a_fill, 2 * n + h + 1)
                    src = ps[:, (2 * m + h) % 4]
                    if kind != "z" and later(tile):
                        act.wait_ge(a_um, 2 * tile - 1 + h)
                    if kind == "g":
                        nc.scalar.activation(sigb[:, h], src, ACT.Sigmoid).then_inc(a_evac, 1)
                    elif kind == "v":
                        nc.scalar.copy(vb[:, h], src).then_inc(a_evac, 1)
                    else:
                        zi, b = tile
                        if later(zi):
                            act.wait_ge(z_st[b], 16 * zi)
                        nc.scalar.copy(zst[:, b, HALF * h:HALF * (h + 1)], src).then_inc(a_evac, 1)

            def block_step(m, i, per, kind, tile):
                if not (m == 0 and per == 0):
                    split(m + 1, i, per, free=(a_fill, 2 * (m + per * i)))
                evac(m, i, per, kind, tile)

            for tile in range(ZLAG):
                for j in range(2):
                    block_step(2 * tile + j, 0, 0, "gv"[j], tile)
            conv_out(0)

            def conf(p):
                for b in range(2):
                    for j in range(3):
                        block_step(2 * ZLAG + 3 * b + j, p, 6, "gvz"[j], 2 * p + ZLAG + b if j < 2 else (p, b))
                conv_out(p + 1)
            loop(act, KE // 2 - 2, conf)
            for t in range(ZLAG):
                block_step(3 * KE - ZLAG + t, 0, 0, "z", (KE // 2 - 2 + t // 2, t % 2))
            conv_out(KE // 2 - 1)

            for k in range(KE):
                act.wait_ge(l_xc, k + 1)
                if k >= 2:
                    act.wait_ge(l_var, k - 1)
                nc.scalar.square(sqb[:, k % 2], cv[:, k]).then_inc(l_sq, 1)
            split(N_OUT1 + 1, free=(a_fill, 6 * KE))
            act.wait_ge(l_var, KE)
            for h in range(2):
                nc.scalar.activation(rstd[:, HALF * h:HALF * (h + 1)], ps[:, 2 + h], ACT.Sqrt,
                                     bias=EPS).then_inc(l_std, 1)

            def silu_y(k):
                act.wait_ge(z_ld[k % 2], 16 * (k // 2 + 1))
                nc.scalar.activation(zst[:, k % 2], zst[:, k % 2], ACT.Silu).then_inc(n_zs, 1)
                act.wait_ge(n_mul, k + 1)
                nc.scalar.activation(cv[:, k], cv[:, k], ACT.Silu, scale=vec[:, V_LNW + k:V_LNW + k + 1],
                                     bias=vec[:, V_LNB + k:V_LNB + k + 1]).then_inc(n_silu, 1)

            def y_hi(l, m, src, scale):
                if m >= YR:
                    act.wait_ge(*tile_done(l, m - YR))
                if scale is None:
                    nc.scalar.copy(xTh[:, m % YR], src).then_inc(o_hi[l], 1)
                else:
                    nc.scalar.activation(y2h[:, m % YR].rearrange("p (t s) -> p t s", t=T), src, ACT.Copy,
                                         scale=scale).then_inc(o_hi[l], 1)

            for k in range(LOOK):
                silu_y(k)
            for m in range(2 * KE + YR - 1):
                if m + LOOK < KE:
                    silu_y(m + LOOK)
                if m < KE:
                    act.wait_ge(n_y, m + 1)
                if m < 2 * KE:
                    y_hi(0, m, cv[:, m % KE], None)
                m -= YR - 1
                if m >= 0 and m % 2 == 1:
                    split(N_OUT1 + m // 2 + 2, free=tile_done(0, m))

            act.wait_ge(o_lo[0], 2 * KE)
            act.dma_start(r_w[:], rows[1:2, :].to_broadcast([P, D])).then_inc(rw_ld[1], 16)
            norm(1)

            act.wait_ge(d_dt, 1)
            nc.scalar.activation(dtt[:, 1], dtt[:, 0], ACT.Abs).then_inc(d_neg, 1)
            act.wait_ge(d_neg, 1)
            nc.scalar.activation(dtt[:, 2], dtt[:, 1], ACT.Exp, scale=-1.0).then_inc(d_exp, 1)
            nc.scalar.activation(arow[:], hrow[:, 2 * H:4 * H], ACT.Exp).then_inc(d_A, 1)

            def evac_sil(j, b, n2):
                for h in range(2):
                    act.wait_ge(b_fill, 4 * j + 2 * b + h + 1)
                    if h == 0 and later(j):
                        act.wait_ge(b_tap, CTAPS * (2 * j + b - 1))
                    if h == 0 and not later(j):
                        act.wait_ge(b_pad, 1)
                    nc.scalar.copy(cpad[:, b, CPAD + HALF * h:CPAD + HALF * (h + 1)], ps[:, h]).then_inc(b_evac, 1)

            def sil(j, b):
                act.wait_ge(b_tap, CTAPS * (2 * j + b + 1))
                nc.scalar.activation(csil[:, b], ps[:, 2 + 2 * b:4 + 2 * b].rearrange("p a s -> p (a s)"),
                                     ACT.Silu).then_inc(b_sil, 1)

            def tr_out(n, b, cnt):
                for h in range(2):
                    act.wait_ge(b_tr, cnt + h + 1)
                    nc.scalar.copy(stg[:, b, 4 * h:4 * h + 4],
                                   ps[:, 6 + h].rearrange("p (t c) -> p t c", t=4)).then_inc(b_te, 1)

            def xside(j):
                for b in range(2):
                    if later(j) or b:
                        split(N_XBC + b + 1, j, 2, free=(b_fill, 4 * j + 2 * b))
                    else:
                        split(N_XBC + 1, free=(d_ps, 1))
                    evac_sil(j, b, None)
                    if later(j) or b:
                        jj, bb = (j, 0) if b else (j - 1, 1)
                        if later(jj):
                            act.wait_ge(b_st[bb], 16 * jj)
                        tr_out(None, bb, 4 * jj + 2 * bb)
                    sil(j, b)
            loop(act, KE // 2, xside)
            act.wait_ge(b_st[1], 16 * (KE // 2 - 1))
            tr_out(None, 1, 4 * (KE // 2 - 1) + 2)

            def flat(v):
                return v.rearrange("p t h -> p (t h)")

            act.wait_ge(d_acs, 3)
            nc.scalar.activation(flat(e_s), ps[:, 4], ACT.Exp).then_inc(d_se, 1)
            nc.scalar.activation(flat(nacs_s), ps[:, 4], ACT.Copy, scale=-1.0).then_inc(d_se, 1)
            act.wait_ge(d_sc, 1)
            nc.scalar.activation(flat(dec_s), ps[:, 5], ACT.Exp).then_inc(d_se, 1)
            nc.scalar.activation(dtt[:, 5], dtt[:, 0], ACT.Exp).then_inc(d_se, 1)

            def decay_rows():
                for u in range(2):
                    pf, pb = (ps[:, 4 + d].rearrange("p (t l) -> p t l", t=4) for d in range(2))
                    cs = slice(4 * u, 4 * u + 4)
                    act.wait_ge(d_tr, 2 * u + 2)
                    nc.scalar.copy(acs_hl[0:32, cs], pf[0:32])
                    nc.scalar.copy(acs_hl[32:64, cs], pb[32:64])
                    if u:
                        act.wait_ge(d_trl, 2)
                    nc.scalar.copy(acs_hi[64:96], pf[64:96])
                    nc.scalar.copy(acs_hi[96:128], pb[96:128]).then_inc(d_trh, 1)

            for g in range(G):
                for b in range(2):
                    j = KE // 2 + g
                    split(N_XBC + KE + 2 * g + b + 1, free=(b_fill, 4 * j + 2 * b))
                    evac_sil(j, b, None)
                    if g == 0 and b == 0:
                        decay_rows()
                    if b == 1:
                        act.wait_ge(b_st[0], 16 * (KE // 2 + g))
                        tr_out(None, 0, 2 * KE + 2 * g)
                    if g:
                        act.wait_ge(b_sc[b], 16 * g)
                    sil(j, b)

            for q in range(G):
                for m in range(4):
                    n = N_Z + 4 * q + m + 1
                    if m:
                        split(n, free=(q_mm, 3 * q + m))
                    else:
                        split(n, free=(q_t, T * q) if q else (b_fill, 2 * NXBC))
                if q:
                    act.wait_ge(q_st, 16 * q)
                for t in range(T):
                    act.wait_ge(q_t, T * q + t + 1)
                    nc.scalar.activation(z2b[:, t], ps[:, t], ACT.Silu).then_inc(q_sil, 1)
            split(N_OUT2 + 1, free=(q_t, T * G))

            def evac_y(c, i):
                act.wait_ge(s_g, 4 * c + i + 1)
                if i or later(c):
                    act.wait_ge(s_sq, 4 * c + i)
                nc.scalar.activation(sqj, z_s[:, HALF * i:HALF * (i + 1)], ACT.Square,
                                     accum_out=ss_y.rearrange("p t g -> p (t g)")[:, bass.ds(4 * c + i, 1)]).then_inc(s_sq, 1)
                act.wait_ge(s_tr, 4 * c + i + 1)
                nc.scalar.copy(keep[:].rearrange("p t e -> p (t e)")[:, bass.ds(c * E + HALF * i, HALF)],
                               ps[:, 7]).then_inc(s_te, 1)

            def chunk(c2):
                for b in range(2):
                    c = 2 * c2 + b
                    if later(c):
                        act.wait_ge(s_ex, 16 * c)
                    nc.scalar.copy(nac, nacs_s[:, bass.ds(c, 1)].rearrange("p a h -> p (a h)")).then_inc(s_nc, 1)
                    act.wait_ge(s_nc, c + 1)
                    for u in range(16):
                        hq, d = divmod(u, 2)
                        act.wait_ge(s_L, 16 * c + u + 1)
                        if u >= 4 or later(c):
                            act.wait_ge(s_M, 16 * c + u - 3)
                        for e in range(4):
                            col = d * H + 4 * hq + e
                            last = nc.scalar.activation(Lb[:, u % 4, e], ps[:, 3 + u % 2, P * e:P * (e + 1)],
                                                        ACT.Exp, bias=nac[:, col:col + 1])
                        last.then_inc(s_ex, 1)
                        if u in (3, 5, 7, 9) and later(c):
                            evac_y(c - 1, (u - 3) // 2)
            loop(act, T // 2, chunk)
            for i in range(4):
                evac_y(T - 1, i)
            for m in range(2 * KE + YR - 1):
                if m < 2 * KE:
                    y_hi(1, m, y_tile2(m % KE), vec[:, V_SNW + m % KE:V_SNW + m % KE + 1])
                m -= YR - 1
                if m >= 0 and m % 2 == 1 and N_OUT2 + m // 2 + 2 < N_END:
                    split(N_OUT2 + m // 2 + 2, free=tile_done(1, m))
                if m == 1 - YR:
                    act.wait_ge(s_S, 4 * T)
                    act.dma_start(f_w[:], rows[2:3, :].to_broadcast([P, D])).then_inc(rw_ld[2], 16)
            for t in range(T):
                act.wait_ge(o_h[1], T + t + 1)
                if t:
                    act.wait_ge(f_ss, t)
                nc.scalar.activation(f_junk, hf[:, t], ACT.Square, accum_out=stat[:, t:t + 1]).then_inc(f_ss, 1)


        @block.gpsimd
        def _(pool):
            tt = nc.gpsimd.tensor_tensor

            def split(n, i=0, per=0):
                pool.wait_ge(w_hi, n + per * i + 1)
                tt(wl[:, n % 2], wraw[:, n % 2], wh[:, n % 2].bitcast(F), ALU.subtract).then_inc(w_lo, 1)

            nc.gpsimd.memset(stat[:, 63:64], -0.5).then_inc(cr2, 1)
            nc.gpsimd.memset(csum, 0.0).then_inc(cr2, 1)
            nc.gpsimd.memset(upad, 0.0).then_inc(a_pad, 1)

            def norm(l):
                for t in range(T):
                    pool.wait_ge(r_ss[l], t + 1)
                    nc.gpsimd.tensor_scalar(stat[:, 16 + t:17 + t], stat[:, t:t + 1], 1.0 / D, EPS,
                                            ALU.mult, ALU.add).then_inc(r_rs[l], 1)
                    pool.wait_ge(r_rs[l], 2 * t + 1)
                    if l == 0 and t == 0:
                        pool.wait_ge(cr2, 1)
                    tt(stat[:, 32 + t:33 + t], stat[:, 16 + t:17 + t], stat[:, 63:64], ALU.pow).then_inc(r_rs[l], 1)

            norm(0)
            split(0)
            split(1)
            pool.wait_ge(a_pad, 1)

            def add_tile(i):
                pool.wait_ge(a_cv, 2 * i + 2)
                pool.wait_ge(a_csum, i) if later(i) else pool.wait_ge(cr2, 2)
                tt(csum, csum, arena[:, bass.ds(i * S, S)], ALU.add).then_inc(a_csum, 1)

            def make_u(i, slot, evacs):
                if later(i - 3):
                    pool.wait_ge(a_conv, 2 * i - 6)
                for h in range(2):
                    pool.wait_ge(a_evac, evacs + h + 1)
                    tt(upad[:, slot, PAD + HALF * h:PAD + HALF * (h + 1)], sigb[:, h], vb[:, h],
                       ALU.mult).then_inc(a_um, 1)

            for i in range(ZLAG):
                if i:
                    split(2 * i + 1)
                split(2 * i + 2)
                make_u(i, i, 4 * i + 2)
            add_tile(0)
            add_tile(1)

            def conf(q):
                for r in range(4):
                    for j in range(3):
                        split(2 * ZLAG + 3 * r + j + 1, q, 12)
                        if j == 1:
                            make_u(4 * q + ZLAG + r, r, 4 * ZLAG + 24 * q + 6 * r + 2)
                    if r % 2:
                        add_tile(4 * q + r + 1)
                        add_tile(4 * q + r + 2)
            loop(pool, KE // 4 - 1, conf)
            for t in range(ZLAG):
                split(3 * KE - ZLAG + t + 1)
            add_tile(KE - 2)
            add_tile(KE - 1)
            split(N_OUT1 + 1)

            def y_tile(k):
                pool.wait_ge(n_silu, k + 1)
                pool.wait_ge(n_zs, k + 1)
                tt(cv[:, k], cv[:, k], zst[:, k % 2], ALU.mult).then_inc(n_y, 1)

            for k in range(LOOK):
                y_tile(k)
            for m in range(2 * KE + YR - 1):
                if m + LOOK < KE:
                    y_tile(m + LOOK)
                m -= YR - 1
                if m >= 0 and m % 2 == 1:
                    split(N_OUT1 + m // 2 + 2)

            norm(1)
            pool.wait_ge(r_ps[1], 2 * T)
            nc.gpsimd.memset(cpad, 0.0).then_inc(b_pad, 1)

            def xside(j):
                for b in range(2):
                    split(N_XBC + 1 + b, j, 2)
            loop(pool, KE // 2, xside)
            for g in range(G):
                for b in range(2):
                    split(N_XBC + KE + 2 * g + b + 1)
            for m in range(KE + 1):
                split(N_Z + 1 + m)

            for r, c in enumerate(range(T - 1, 0, -1)):
                b = r % 2
                pool.wait_ge(p_x[b], 16 * (r // 2 + 1))
                if r:
                    pool.wait_ge(p_mm, r)
                else:
                    pool.wait_ge(d_coef, 1)
                tt(xb_s.rearrange("p (h e) -> p h e", h=H), xs_s[:, b].rearrange("p (h e) -> p h e", h=H),
                   bcast(coef_s[:, c, H:2 * H], HD), ALU.mult).then_inc(p_xb, 1)

            def heads(v):
                return v.rearrange("p (h e) -> p h e", h=8)

            def chunk(c2):
                for b in range(2):
                    c = 2 * c2 + b

                    def x_skip(g):
                        if g == 0:
                            pool.wait_ge(s_x[b], 16 * (c2 + 1))
                        if g >= 2 or later(c):
                            pool.wait_ge(s_yd, 8 * c + 2 * g - 2)
                        if g >= 2 or later(c):
                            pool.wait_ge(s_xD, 4 * c + g - 1)
                        tt(heads(xD[:, g % 2]), heads(xs_s[:, b, HALF * g:HALF * (g + 1)]),
                           bcast(hrow[:, 4 * H + 8 * g:4 * H + 8 * g + 8], HD), ALU.mult).then_inc(s_xD, 1)

                    def x_state(g):
                        if g >= 2 or later(c):
                            pool.wait_ge(s_stt, 4 * c + g - 1)
                            pool.wait_ge(s_xf, 4 * c + g - 1)
                        elif g == 0:
                            pool.wait_ge(p_mm, T - 1)
                        tt(heads(xf_s[:, g % 2]), heads(xs_s[:, b, HALF * g:HALF * (g + 1)]),
                           bcast(coef_s.rearrange("p t h -> p (t h)")[:, bass.ds(c * 2 * H + 8 * g, 8)], HD),
                           ALU.mult).then_inc(s_xf, 1)

                    def y_add(g):
                        pool.wait_ge(s_tb, 4 * c + g + 1)
                        pool.wait_ge(s_ya, 4 * c + g + 1)
                        tt(yacc[:, HALF * g:HALF * (g + 1)], yacc[:, HALF * g:HALF * (g + 1)], tmpb[:, g % 2],
                           ALU.add).then_inc(s_ad, 1)

                    def gate(g):
                        if g == 0:
                            pool.wait_ge(s_z, 16 * (c + 1))
                        pool.wait_ge(s_dd, 4 * c + g + 1)
                        tt(z_s[:, HALF * g:HALF * (g + 1)], yacc[:, HALF * g:HALF * (g + 1)],
                           z_s[:, HALF * g:HALF * (g + 1)], ALU.mult).then_inc(s_g, 1)

                    x_skip(0)
                    y_add(0)
                    x_skip(1)
                    x_state(0)
                    y_add(1)
                    gate(0)
                    x_state(1)
                    x_skip(2)
                    y_add(2)
                    gate(1)
                    x_state(2)
                    x_skip(3)
                    x_state(3)
                    y_add(3)
                    gate(2)
                    gate(3)
            loop(pool, T // 2, chunk)

            pool.wait_ge(rs_r, 1)
            nc.gpsimd.tensor_scalar(rs_y[:, 1], rs_y[:, 0], 1.0 / E, EPS, ALU.mult, ALU.add).then_inc(rs_p, 1)
            pool.wait_ge(rs_p, 1)
            tt(rs_y[:, 2], rs_y[:, 1], stat[:, 63:64].to_broadcast([P, T]), ALU.pow).then_inc(rs_p, 1)
            for m in range(1, 2 * KE, 2):
                if N_OUT2 + m // 2 + 2 < N_END:
                    split(N_OUT2 + m // 2 + 2)
            for t in range(T):
                pool.wait_ge(f_ss, t + 1)
                nc.gpsimd.tensor_scalar(stat[:, 16 + t:17 + t], stat[:, t:t + 1], 1.0 / D, EPS,
                                        ALU.mult, ALU.add).then_inc(f_rs, 1)
                pool.wait_ge(f_rs, 2 * t + 1)
                tt(stat[:, 32 + t:33 + t], stat[:, 16 + t:17 + t], stat[:, 63:64], ALU.pow).then_inc(f_rs, 1)

        @block.vector
        def _(dve):
            tt, ts, stt = nc.vector.tensor_tensor, nc.vector.tensor_scalar, nc.vector.scalar_tensor_tensor

            def norm(l):
                def lo(t):
                    for q in range(2):
                        dve.wait_ge(r_hi[l], 2 * t + q + 1)
                        cols = (slice(None), slice(4 * q, 4 * q + 4), slice(t * P, (t + 1) * P))
                        tt(xTl[cols], ps[:, 2 * (t % 2) + q].rearrange("p (k s) -> p k s", k=4),
                           xTh[cols].bitcast(F), ALU.subtract).then_inc(r_lo[l], 1)
                for t in range(T):
                    if t == 0:
                        dve.wait_ge(rw_ld[l], 16)
                    dve.wait_ge(r_rs[l], 2 * t + 2)
                    if t >= 2:
                        dve.wait_ge(r_ps[l], 2 * t - 2)
                    stt(r_n[:, t % 2], r_x[:, t % 2], stat[:, 32 + t:33 + t], r_w, ALU.mult,
                        ALU.mult).then_inc(r_xn[l], 1)
                    if t >= 1:
                        lo(t - 1)
                lo(T - 1)

            norm(0)

            def conv(q):
                dve.wait_ge(c_ld, 16 * (len(C_NAMES) + 4))
                if later(q):
                    dve.wait_ge(a_conv, 8 * q)
                nc.vector.tensor_copy(tap4[:], taps[:, bass.ds(q * 4 * TAPS, 4 * TAPS)]).then_inc(a_tap4, 1)
                dve.wait_ge(a_tap4, q + 1)
                for pp in range(2):
                    p = 2 * q + pp
                    base = 2 * TAPS * p

                    def w(b, k):
                        return tap4[:, (2 * pp + b) * TAPS + k:(2 * pp + b) * TAPS + k + 1]

                    for b in range(2):
                        i = 2 * p + b
                        dve.wait_ge(a_um, 2 * i + 2)
                        for h in range(2):
                            if later(p):
                                dve.wait_ge(a_cv, 4 * p - 4 + 2 * b + h + 1)
                            ts(ps[:, 4 + 2 * b + h], upad[:, 2 * pp + b, HALF * h:HALF * (h + 1)], w(b, 0), None,
                               ALU.mult).then_inc(a_tap, 1)
                    for k in range(1, TAPS - 1):
                        for b in range(2):
                            dve.wait_ge(a_tap, base + (2 * (b + 1) if k == 1 else 4 + 2 * (k - 2) + b + 1))
                            acc = ps[:, 4 + 2 * b:6 + 2 * b].rearrange("p a s -> p (a s)")
                            stt(acc, upad[:, 2 * pp + b, k:k + S], w(b, k), acc, ALU.mult, ALU.add).then_inc(a_tap, 1)
                    for b in range(2):
                        dve.wait_ge(a_tap, base + 4 + 2 * (TAPS - 3) + b + 1)
                        for h in range(2):
                            acc = ps[:, 4 + 2 * b + h]
                            k = TAPS - 1
                            stt(acc, upad[:, 2 * pp + b, k + HALF * h:k + HALF * (h + 1)], w(b, k), acc, ALU.mult,
                                ALU.add).then_inc(a_conv, 1)
            loop(dve, KE // 4, conv)

            dve.wait_ge(l_mean, 2)
            dve.wait_ge(a_cv, 2 * KE)
            for k in range(KE):
                tt(cv[:, k], cv[:, k], ps[:, 0:2].rearrange("p a s -> p (a s)"), ALU.subtract).then_inc(l_xc, 1)
            for h in range(2):
                dve.wait_ge(l_std, h + 1)
                nc.vector.reciprocal(rstd[:, HALF * h:HALF * (h + 1)], rstd[:, HALF * h:HALF * (h + 1)]).then_inc(l_rstd, 1)
            dve.wait_ge(l_rstd, 2)

            def mul(k):
                tt(cv[:, k], cv[:, k], rstd, ALU.mult).then_inc(n_mul, 1)

            def y_lo(l, m, src, scale):
                dve.wait_ge(o_hi[l], m + 1)
                if scale is None:
                    tt(xTl[:, m % YR], src, xTh[:, m % YR].bitcast(F), ALU.subtract).then_inc(o_lo[l], 1)
                else:
                    yh, yl = (v[:, m % YR].rearrange("p (t s) -> p t s", t=T) for v in (y2h, y2l))
                    stt(yl, src, scale, yh.bitcast(F), ALU.mult, ALU.subtract).then_inc(o_lo[l], 1)

            for k in range(LOOK + 1):
                mul(k)

            def residual(h):
                dve.wait_ge(xr_ld[h], 16)
                for t in range(T):
                    dve.wait_ge(o_t[0], T * h + t + 1)
                    tt(xres[:, t], ps[:, t], xres[:, t], ALU.add).then_inc(o_h[0], 1)

            for m in range(2 * KE):
                if m + LOOK + 1 < KE:
                    mul(m + LOOK + 1)
                if m == KE + YR - 1:
                    residual(0)
                y_lo(0, m, cv[:, m % KE], None)
            residual(1)

            norm(1)

            steps = [0]

            def step(ins):
                steps[0] += 1
                ins.then_inc(d_v, 1)
                dve.wait_ge(d_v, steps[0])

            dve.wait_ge(d_ps, 1)
            tt(dtt[:, 0].rearrange("p (t h) -> p t h", t=T), ps[:, 7].rearrange("p (t h) -> p t h", t=T),
               hrow[:, 0:2 * H].unsqueeze(1).to_broadcast([P, T, 2 * H]), ALU.add).then_inc(d_dt, 1)
            v, w1, e, r2, _, _ = (dtt[:, n] for n in range(6))
            dve.wait_ge(d_exp, 1)
            step(ts(r2, e, 2.0, None, ALU.add))
            step(nc.vector.reciprocal(w1, r2))
            step(tt(e, e, w1, ALU.mult))
            step(tt(r2, e, e, ALU.mult))
            step(ts(w1, r2, 1.0 / 17, None, ALU.mult))
            for j in range(7, 0, -1):
                step(stt(w1, w1, 1.0 / (2 * j + 1), r2, ALU.add, ALU.mult))
            step(stt(w1, w1, 1.0, e, ALU.add, ALU.mult))
            step(ts(v, v, 0.0, None, ALU.max))
            step(stt(dt_s.rearrange("p t h -> p (t h)"), w1, 2.0, v, ALU.mult, ALU.add))
            dve.wait_ge(d_A, 1)
            for n in range(2):
                stt(a2[:, :, n], dt_s, -1.0, arow[:].unsqueeze(1).to_broadcast([P, T, 2 * H]), ALU.mult,
                    ALU.mult).then_inc(d_a, 1)

            def taps5(j, b):
                i = 2 * j + b
                acc = ps[:, 2 + 2 * b:4 + 2 * b].rearrange("p a s -> p (a s)")
                dve.wait_ge(b_evac, 2 * i + 2)
                if later(j):
                    dve.wait_ge(b_sil, i - 1)
                for k in range(CTAPS):
                    wk = ctaps[:, bass.ds(i * CTAPS + k, 1)]
                    if k == 0:
                        ts(acc, cpad[:, b, 0:S], wk, vec[:, bass.ds(V_CB + i, 1)], ALU.mult, ALU.add).then_inc(b_tap, 1)
                    else:
                        dve.wait_ge(b_tap, CTAPS * i + k)
                        stt(acc, cpad[:, b, k:k + S], wk, acc, ALU.mult, ALU.add).then_inc(b_tap, 1)

            def xside(j):
                taps5(j, 0)
                taps5(j, 1)
            loop(dve, KE // 2, xside)
            dve.wait_ge(d_se, 2)
            nc.vector.tensor_copy(w1, ps[:, 4]).then_inc(d_v, 1)
            steps[0] += 1
            dve.wait_ge(d_v, steps[0])
            tt(v, ps[:, 5], w1, ALU.subtract).then_inc(d_sc, 1)
            dve.wait_ge(d_se, 4)
            tt(coef_s.rearrange("p t h -> p (t h)"), dtt[:, 5], dt_s.rearrange("p t h -> p (t h)"),
               ALU.mult).then_inc(d_coef, 1)

            def decay_rows():
                for u in range(2):
                    cs = slice(4 * u, 4 * u + 4)
                    dve.wait_ge(d_trh, u + 1)
                    for d in range(2):
                        rows_ = slice(64 + 32 * d, 96 + 32 * d)
                        tt(acs_hl[rows_, cs], ps[rows_, 4 + d].rearrange("p (t l) -> p t l", t=4),
                           acs_hi[rows_].bitcast(F), ALU.subtract).then_inc(d_trl, 1)

            for g in range(G):
                if g == 0:
                    decay_rows()
                taps5(KE // 2 + g, 0)
                taps5(KE // 2 + g, 1)

            dve.wait_ge(q_t, T * G)
            nc.vector.memset(keep[:, T - 1], 0.0).then_inc(p_s, 1)
            dve.wait_ge(q_st, 16 * G)
            nc.vector.memset(sf, 0.0).then_inc(s_zero, 1)
            for r, c in enumerate(range(T - 1, 0, -1)):
                old, new = keep[:, c], keep[:, c - 1]
                dve.wait_ge(p_s, r + 1)
                tt(new.rearrange("p (h e) -> p h e", h=H), old.rearrange("p (h e) -> p h e", h=H),
                   bcast(dec_s[:, c, H:2 * H], HD), ALU.mult).then_inc(p_dec, 1)
                dve.wait_ge(p_dec, r + 1)
                dve.wait_ge(p_mm, r + 1)
                tt(new, new, ps[:, 0:4].rearrange("p a s -> p (a s)"), ALU.add).then_inc(p_s, 1)

            def heads(v_):
                return v_.rearrange("p (h e) -> p h e", h=8)

            def head_col(tab, c, col):
                return bcast(tab.rearrange("p t h -> p (t h)")[:, bass.ds(c * 2 * H + col, 8)], HD)

            def chunk(c2):
                for b in range(2):
                    c = 2 * c2 + b
                    if later(c):
                        dve.wait_ge(s_M, 16 * c)
                    nc.vector.tensor_copy(dtc, dt_s.rearrange("p t h -> p (t h)")[:, bass.ds(c * 2 * H, 2 * H)]).then_inc(s_dc, 1)

                    def from_states(g):
                        dve.wait_ge(s_yo, 8 * c + 2 * g + 1)
                        if later(c):
                            dve.wait_ge(s_g, 4 * c + g - 3)
                        tt(heads(yacc[:, HALF * g:HALF * (g + 1)]), heads(ps[:, 1]), head_col(e_s, c, 8 * g),
                           ALU.mult).then_inc(s_ya, 1)
                        dve.wait_ge(s_yo, 8 * c + 2 * g + 2)
                        if g >= 2 or later(c):
                            dve.wait_ge(s_ad, 4 * c + g - 1)
                        tt(heads(tmpb[:, g % 2]), heads(ps[:, 2]), head_col(e_s, c, H + 8 * g),
                           ALU.mult).then_inc(s_tb, 1)

                    def masked(u):
                        hq, d = divmod(u, 2)
                        if u == 0:
                            dve.wait_ge(s_dc, c + 1)
                            dve.wait_ge(s_cb, c + 1)
                        dve.wait_ge(s_ex, 16 * c + u + 1)
                        if u >= 4 or later(c):
                            dve.wait_ge(s_yd, 8 * c + hq - 1)
                        for n in range(4):
                            col = d * H + 4 * hq + n
                            last = stt(Mb[:, u % 4, n], Lb[:, u % 4, n], dtc[:, col:col + 1],
                                       ps[:, 0, P * (hq // 2):P * (hq // 2 + 1)], ALU.mult, ALU.mult)
                        last.then_inc(s_M, 1)

                    def diag(g):
                        dve.wait_ge(s_yd, 8 * c + 2 * g + 2)
                        dve.wait_ge(s_ad, 4 * c + g + 1)
                        tt(yacc[:, HALF * g:HALF * (g + 1)], ps[:, 5 + g % 2], yacc[:, HALF * g:HALF * (g + 1)],
                           ALU.add).then_inc(s_dd, 1)

                    def state(g):
                        cols = slice(HALF * g, HALF * (g + 1))
                        dve.wait_ge(s_yo, 8 * c + 2 * g + 1)
                        if later(c):
                            dve.wait_ge(s_S, 4 * c + g - 3)
                        tt(heads(sf[:, cols]), heads(sf[:, cols]), head_col(dec_s, c, 8 * g), ALU.mult).then_inc(s_sd, 1)
                        dve.wait_ge(s_sd, 4 * c + g + 1)
                        dve.wait_ge(s_stt, 4 * c + g + 1)
                        tt(sf[:, cols], sf[:, cols], ps[:, 7], ALU.add).then_inc(s_S, 1)

                    from_states(0)
                    for hq in range(8):
                        masked(2 * hq)
                        masked(2 * hq + 1)
                        if hq in (1, 3, 5):
                            from_states((hq + 1) // 2)
                        if hq >= 4:
                            state(hq - 4)
                        if hq in (2, 4, 6):
                            diag(hq // 2 - 1)
                    diag(3)
            loop(dve, T // 2, chunk)

            dve.wait_ge(s_sq, 4 * T)
            nc.vector.tensor_reduce(rs_y[:, 0], ss_y, mybir.AxisListType.X, ALU.add).then_inc(rs_r, 1)

            def residual2(h):
                dve.wait_ge(xr_ld[0], 32)
                if h == 0:
                    dve.wait_ge(rs_p, 2)
                for t in range(T):
                    dve.wait_ge(o_t[1], T * h + t + 1)
                    cols = hf[:, t, HALF * h:HALF * (h + 1)]
                    stt(cols, ps[:, t], rs_y[:, 2, t:t + 1], cols, ALU.mult, ALU.add).then_inc(o_h[1], 1)

            for m in range(2 * KE):
                if m == KE + YR - 1:
                    residual2(0)
                y_lo(1, m, y_tile2(m % KE), vec[:, V_SNW + m % KE:V_SNW + m % KE + 1])
            residual2(1)
            for t in range(T):
                if t == 0:
                    dve.wait_ge(rw_ld[2], 16)
                dve.wait_ge(f_rs, 2 * t + 2)
                if t >= 2:
                    dve.wait_ge(f_st[t % 2], 16 * (t // 2))
                stt(f_o[:, t % 2], hf[:, t], stat[:, 32 + t:33 + t], f_w, ALU.mult, ALU.mult).then_inc(f_out, 1)

        @block.tensor
        def _(pe):
            def mm3(dst, lh, ll, rh, rl, start, stop):
                mm(dst, ll, rh, start=start, stop=False)
                mm(dst, lh, rl, start=False, stop=False)
                return mm(dst, lh, rh, start=False, stop=stop)

            def norm(l):
                for t in range(T):
                    pe.wait_ge(r_xn[l], t + 1)
                    for q in range(2):
                        if t >= 2:
                            pe.wait_ge(r_lo[l], 2 * (t - 2) + q + 1)
                        for k in range(4):
                            last = nc.tensor.transpose(ps[:, 2 * (t % 2) + q, P * k:P * (k + 1)],
                                                       r_n[:, t % 2, P * (4 * q + k):P * (4 * q + k + 1)],
                                                       c_f["ident"][:])
                        last.then_inc(r_ps[l], 1)

            def by_channel(n, h, bank, sem_):
                cols = slice(HALF * h, HALF * (h + 1))
                for k in range(KD):
                    wc = slice(P * k, P * (k + 1))
                    last = mm3(ps[:, bank], wh[:, n % 2, wc], wl[:, n % 2, wc], xTh[:, k, cols], xTl[:, k, cols],
                               k == 0, k == KD - 1)
                last.then_inc(sem_, 1)

            pe.wait_ge(c_ld, 16 * (len(C_NAMES) + 4))
            norm(0)
            pe.wait_ge(r_lo[0], 2 * T)

            def conf_block(m, i=0, per=0):
                pe.wait_ge(w_lo, m + per * i + 1)
                for h in range(2):
                    f = 2 * m + h
                    if f >= 4:
                        pe.wait_ge(a_evac, f + 2 * per * i - 3)
                    by_channel(m, h, f % 4, a_fill)

            for m in range(2 * ZLAG):
                conf_block(m)

            def conf(p):
                for m in range(6):
                    conf_block(2 * ZLAG + m, p, 6)
            loop(pe, KE // 2 - 2, conf)
            for m in range(3 * KE - ZLAG, 3 * KE):
                conf_block(m)

            pe.wait_ge(a_csum, KE)
            pe.wait_ge(a_evac, 6 * KE)
            for h in range(2):
                mm(ps[:, h], c_f["mean"][:], csum[:, HALF * h:HALF * (h + 1)], start=True, stop=True).then_inc(l_mean, 1)
            for k in range(KE):
                pe.wait_ge(l_sq, k + 1)
                for h in range(2):
                    last = mm(ps[:, 2 + h], c_f["mean"][:], sqb[:, k % 2, HALF * h:HALF * (h + 1)],
                              start=k == 0, stop=k == KE - 1)
                last.then_inc(l_var, 1)

            def out_product(l, n0, bank_free):
                for h in range(2):
                    def pair(kp, first=False, final=False):
                        for kk in range(2):
                            m = KE * h + 2 * kp + kk
                            if kk == 0:
                                pe.wait_ge(w_lo, n0 + KE // 2 * h + kp + 1)
                            pe.wait_ge(o_lo[l], m + 1)
                            for t in range(T):
                                if first and kk == 0:
                                    if h:
                                        pe.wait_ge(o_h[l], t + 1)
                                    elif t == 0:
                                        bank_free()
                                tc = slice(P * t, P * (t + 1))
                                wc = slice(HALF * kk, HALF * (kk + 1))
                                s_ = (n0 + KE // 2 * h + parity(kp)) % 2
                                yh, yl = ((xTh, xTl), (y2h, y2l))[l]
                                ys = 2 * parity(kp) + kk
                                last = mm3(ps[:, t], yh[:, ys, tc], yl[:, ys, tc], wh[:, s_, wc], wl[:, s_, wc],
                                           first and kk == 0, final and kk == 1)
                                if final and kk == 1:
                                    last.then_inc(o_t[l], 1)
                            if not (final and kk == 1):
                                last.then_inc(o_mm[l], 1)
                    par = [0]

                    def parity(kp):
                        return par[0]
                    par[0] = 0
                    pair(0, first=True)
                    with pe.Fori(0, KE // 4 - 1) as i:
                        par[0] = 1
                        pair(2 * i + 1)
                        par[0] = 0
                        pair(2 * i + 2)
                    par[0] = 1
                    pair(KE // 2 - 1, final=True)

            out_product(0, N_OUT1, lambda: (pe.wait_ge(l_std, 2), pe.wait_ge(a_cv, 2 * KE)))

            norm(1)

            pe.wait_ge(w_lo, N_DT + 1)
            pe.wait_ge(r_lo[1], 2 * T)
            s_ = N_DT % 2
            for t in range(T):
                for k in range(KD):
                    tc, wc = slice(P * t, P * (t + 1)), slice(2 * H * k, 2 * H * (k + 1))
                    last = mm3(ps[:, 7, 2 * H * t:2 * H * (t + 1)], xTh[:, k, tc], xTl[:, k, tc],
                               wh[:, s_, wc], wl[:, s_, wc], k == 0, k == KD - 1)
            last.then_inc(d_ps, 1)

            def fill(j, b):
                i = 2 * j + b
                pe.wait_ge(w_lo, N_XBC + i + 1)
                for h in range(2):
                    if later(j) or b:
                        pe.wait_ge(b_evac, 2 * i + h - 1)
                    by_channel(N_XBC + b, h, h, b_fill)

            def turn(done, b, sil_count, evac_count):
                pe.wait_ge(b_sil, sil_count)
                for h in range(2):
                    if evac_count is not None:
                        pe.wait_ge(b_te, evac_count + h)
                    for t in range(4):
                        last = nc.tensor.transpose(ps[:, 6 + h, P * t:P * (t + 1)],
                                                   csil[:, b, P * (4 * h + t):P * (4 * h + t + 1)], c_f["ident"][:])
                    last.then_inc(b_tr, 1)

            def xside(j):
                fill(j, 0)
                if later(j):
                    turn(None, 1, 2 * j, 4 * j - 3)
                else:
                    pe.wait_ge(d_dt, 1)
                fill(j, 1)
                turn(None, 0, 2 * j + 1, 4 * j - 1 if later(j) else None)
            loop(pe, KE // 2, xside)
            turn(None, 1, KE, 2 * KE - 3)
            a_ = a2[:, :, 0]
            pe.wait_ge(d_a, 2)
            acs = ps[:, 4].rearrange("p (t h) -> p t h", t=T)
            mm(acs[:, :, 0:H], c_f["upto"][:], a_[:, :, 0:H], start=True, stop=True).then_inc(d_acs, 1)
            mm(acs[:, :, H:2 * H], c_f["from_"][:], a_[:, :, H:2 * H], start=True, stop=True).then_inc(d_acs, 1)
            mm(ps[:, 5].rearrange("p (t h) -> p t h", t=T), c_f["ones"][:], a_, start=True, stop=True).then_inc(d_acs, 1)
            fill(KE // 2, 0)
            for u in range(2):
                if u == 0:
                    pe.wait_ge(d_se, 4)
                else:
                    pe.wait_ge(d_trl, 2)
                for d, tri in enumerate(("upto", "from_")):
                    for c in range(4):
                        last = mm(ps[:, 4 + d, P * c:P * (c + 1)],
                                  a2[:, 4 * u + c].rearrange("p n h -> p (n h)"), c_f[tri][:],
                                  start=True, stop=True)
                    last.then_inc(d_tr, 1)
            for g in range(G):
                if g:
                    fill(KE // 2 + g, 0)
                fill(KE // 2 + g, 1)
                turn(None, 0, KE + 2 * g + 1, 2 * KE + 2 * g - 1)

            for q in range(G):
                for kp in range(4):
                    n = N_Z + 4 * q + kp
                    pe.wait_ge(w_lo, n + 1)
                    for kk in range(2):
                        for t in range(T):
                            if kp == 0 and kk == 0:
                                if q:
                                    pe.wait_ge(q_sil, T * (q - 1) + t + 1)
                                elif t == 0:
                                    pe.wait_ge(b_te, 2 * (KE + G))
                                    pe.wait_ge(b_sil, NXBC)
                            k = 2 * kp + kk
                            tc, wc = slice(P * t, P * (t + 1)), slice(HALF * kk, HALF * (kk + 1))
                            last = mm3(ps[:, t], xTh[:, k, tc], xTl[:, k, tc], wh[:, n % 2, wc], wl[:, n % 2, wc],
                                       k == 0, k == KD - 1)
                            if k == KD - 1:
                                last.then_inc(q_t, 1)
                    if kp < 3:
                        last.then_inc(q_mm, 1)

            pe.wait_ge(q_sil, T * G)
            for r in range(T - 1):
                b = r % 2
                pe.wait_ge(p_b[b], 16 * (r // 2 + 1))
                pe.wait_ge(p_xb, r + 1)
                if r:
                    pe.wait_ge(p_s, r + 1)
                for g in range(G):
                    last = mm(ps[:, g], bc_s[:, b, 2, g], xb_s[:, HALF * g:HALF * (g + 1)], start=True, stop=True)
                last.then_inc(p_mm, 1)

            pe.wait_ge(p_s, T)
            pe.wait_ge(cr, 1)

            def chunk(c2):
                for b in range(2):
                    c = 2 * c2 + b

                    def decay_ahead(u):
                        if u < 16:
                            decay(u, c)
                        elif not (isinstance(c, int) and c == T - 1):
                            decay(u - 16, c + 1)

                    def decay(u, c):
                        hq, d = divmod(u, 2)
                        if u >= 2 or later(c):
                            pe.wait_ge(s_ex, 16 * c + u - 1)
                        bank = 3 + u % 2
                        for e in range(4):
                            col = d * H + 4 * hq + e
                            mm(ps[:, bank, P * e:P * (e + 1)], pickR[:, col:col + 1].to_broadcast([P, P]),
                                      acs_hl[:, bass.ds(c, 1)].rearrange("p a l -> p (a l)"), start=e == 0, stop=False,
                               skip_group_check=True)
                        mm(ps[:, bank].rearrange("p (e l) -> p e l", e=4), identR[:],
                           negR[:, d].unsqueeze(1).to_broadcast([P, 4, P]), start=False, stop=True,
                           skip_group_check=True).then_inc(s_L, 1)

                    def from_states(g):
                        cols = slice(HALF * g, HALF * (g + 1))
                        if g or later(c):
                            pe.wait_ge(s_ya, 4 * c + g)
                        if g == 0:
                            pe.wait_ge(s_zero, 1) if not later(c) else pe.wait_ge(s_S, 4 * c)
                        mm(ps[:, 1], bc_s[:, b, 1, g], sf[:, cols], start=True, stop=True).then_inc(s_yo, 1)
                        if g or later(c):
                            pe.wait_ge(s_tb, 4 * c + g)
                        mm(ps[:, 2], bc_s[:, b, 1, g],
                           keep[:].rearrange("p t e -> p (t e)")[:, bass.ds(c * E + HALF * g, HALF)],
                           start=True, stop=True).then_inc(s_yo, 1)

                    def inside(hq):
                        g = hq // 2
                        if hq % 2 == 0:
                            if g >= 2 or later(c):
                                pe.wait_ge(s_dd, 4 * c + g - 1)
                        for d in range(2):
                            u = 2 * hq + d
                            pe.wait_ge(s_M, 16 * c + u + 1)
                            for n in range(4):
                                h8 = 4 * (hq % 2) + n
                                last = mm(ps[:, 5 + g % 2, HD * h8:HD * (h8 + 1)], Mb[:, u % 4, n],
                                          xs_s[:, b, HD * (8 * g + h8):HD * (8 * g + h8 + 1)],
                                          start=hq % 2 == 0 and d == 0 and n == 0, stop=False, skip_group_check=True)
                        if hq % 2:
                            pe.wait_ge(s_xD, 4 * c + g + 1)
                            last = mm(ps[:, 5 + g % 2], c_f["ident"][:], xD[:, g % 2], start=False, stop=True,
                                      skip_group_check=True)
                        last.then_inc(s_yd, 1)

                    def state(g):
                        pe.wait_ge(s_xf, 4 * c + g + 1)
                        if g:
                            pe.wait_ge(s_S, 4 * c + g)
                        elif later(c):
                            pe.wait_ge(s_te, 4 * c)
                        mm(ps[:, 7], bc_s[:, b, 2, g], xf_s[:, g % 2], start=True, stop=True).then_inc(s_stt, 1)

                    if b == 0:
                        pe.wait_ge(s_x[0], 16 * (c2 + 1))
                    else:
                        pe.wait_ge(s_x[1], 16 * (c2 + 1))
                    pe.wait_ge(s_b[b], 16 * (c2 + 1))
                    if later(c):
                        pe.wait_ge(s_M, 16 * c)
                    for g in range(G):
                        last = mm(ps[:, 0, P * g:P * (g + 1)], bc_s[:, b, 0, g], bc_s[:, b, 1, g], start=True, stop=True)
                    last.then_inc(s_cb, 1)
                    if not later(c):
                        for u in range(4):
                            decay(u, c)
                    from_states(0)
                    for hq in range(8):
                        decay_ahead(2 * hq + 4)
                        decay_ahead(2 * hq + 5)
                        if hq < 4 and later(c):
                            turn_y(c - 1, hq)
                        if hq in (1, 3, 5):
                            from_states((hq + 1) // 2)
                        if hq >= 4:
                            state(hq - 4)
                        inside(hq)

            def turn_y(c, i):
                pe.wait_ge(s_g, 4 * c + i + 1)
                if i:
                    pe.wait_ge(s_te, 4 * c + i)
                else:
                    pe.wait_ge(s_S, 4 * c + 4)
                for n in range(4):
                    j = 4 * i + n
                    last = nc.tensor.transpose(ps[:, 7, P * n:P * (n + 1)], z_s[:, P * j:P * (j + 1)], c_f["ident"][:])
                last.then_inc(s_tr, 1)

            chunk(0)
            with pe.Fori(1, T // 2 - 1) as c2:
                chunk(c2)
            chunk(T // 2 - 1)
            for i in range(4):
                turn_y(T - 1, i)
            out_product(1, N_OUT2, lambda: (pe.wait_ge(s_te, 4 * T), pe.wait_ge(s_dd, 4 * T)))


def kernel(**inputs):
    import numpy as np
    import concourse.bacc as bacc
    from concourse.bass_utils import run_bass_kernel_spmd

    f = {k: np.asarray(v) for k, v in inputs.items()}

    def by_channel(w):
        return w.reshape(KD, P, -1, P).transpose(2, 1, 0, 3).reshape(-1, P, W)

    def by_token(w, cols=HALF):
        k = w.shape[0] // P
        return w.reshape(k // 2, 2, P, -1, cols).transpose(3, 0, 2, 1, 4).reshape(-1, P, 2 * cols)

    w_in = by_channel(f["cm_w_in"][0]).reshape(3, KE, P, W)
    v, g, z = w_in
    stream = []
    for i in range(KE + ZLAG):
        stream += [g[i], v[i]] if i < KE else []
        stream += [z[i - ZLAG]] if i >= ZLAG else []
    w_in = np.stack(stream)
    s_in = f["ssd_w_in"][0]
    nx = E + 2 * G * P
    order = list(range(KE)) + [KE + k * G + g for g in range(G) for k in range(2)]
    w_xbc = by_channel(s_in[:, E:E + nx])[order]
    w_dt = np.zeros((1, P, W), np.float32)
    w_dt[0, :, :KD * 2 * H] = s_in[:, E + nx:].reshape(KD, P, 2 * H).transpose(1, 0, 2).reshape(P, -1)
    wst = np.concatenate([w_in, by_token(f["cm_w_out"][0]), w_dt, w_xbc, by_token(s_in[:, :E]),
                          by_token(f["ssd_w_out"][0])])

    def col(v):
        return v.reshape(-1, P).T

    cvec = np.concatenate([col(f["cm_dw_b"][0]), col(f["cm_ln_w"][0]), col(f["cm_ln_b"][0]),
                           col(f["ssd_conv_b"][0])[:, order], col(f["ssd_norm_w"][0])], axis=1)
    dww = f["cm_dw_w"][0].reshape(TAPS, KE, P).transpose(2, 1, 0).reshape(P, -1)
    cw = f["ssd_conv_w"][0].reshape(CTAPS, NXBC, P)[:, order].transpose(2, 1, 0).reshape(P, -1)
    rows = np.concatenate([f["norm_w"], f["final_norm_w"][None]])
    srow = np.concatenate([f["ssd_dt_bias"].reshape(1, -1), f["ssd_A_log"].reshape(1, -1), f["ssd_D"].reshape(1, -1)],
                          axis=1)
    i = np.arange(P)
    tri = {"ident": i[:, None] == i, "upto": i[:, None] <= i, "from_": i[:, None] >= i, "ones": i[:, None] >= 0 * i}
    consts = {n: m.astype(np.float32) for n, m in tri.items()}
    consts["mean"] = np.full((P, P), 1.0 / E, np.float32)
    consts["neg_f"] = np.where(i[:, None] <= i, 0.0, -1e30).astype(np.float32)
    consts["neg_b"] = np.where(i[:, None] >= i, 0.0, -1e30).astype(np.float32)
    consts["pick"] = (i[:, None] % (2 * H) == np.arange(2 * H)).astype(np.float32)

    arrays = {"wst": wst, "x": f["x"].reshape(T, P, D), "cvec": cvec, "dww": dww, "cw": cw, "rows": rows,
              "srow": srow, **{"c_" + n: m for n, m in consts.items()}}
    arrays = {n + "_dram": np.ascontiguousarray(a) for n, a in arrays.items()}
    nc = bacc.Bacc("TRN2", target_bir_lowering=False, num_devices=1)
    aps = {n[:-5]: nc.dram_tensor(n, a.shape, mybir.dt.float32, kind="ExternalInput").ap() for n, a in arrays.items()}
    out = nc.dram_tensor("out_dram", (T, P, D), mybir.dt.float32, kind="ExternalOutput").ap()
    cst = {n: aps.pop("c_" + n) for n in C_NAMES}
    program(nc, out=out, cst=cst, **aps)
    r = run_bass_kernel_spmd(nc, [arrays], core_ids=[0])
    return r.results[0]["out_dram"].reshape(1, S, D)
```

```python
from contextlib import ExitStack

import concourse.bass as bass
from concourse import mybir

F = mybir.dt.float32
R = mybir.dt.float32r
ALU = mybir.AluOpType
ACT = mybir.ActivationFunctionType

P = 128
D = 1024
S = 1024
E = 2048
KD = D // P
KE = E // P
T = S // P
TAPS = 31
PAD = (TAPS - 1) // 2
CTAPS = 5
CPAD = (CTAPS - 1) // 2
H = 32
HD = 64
G = 4
NXBC = KE + 2 * G
EPS = 1e-5
HALF = 512
FIRST = [("g", 0), ("v", 0), ("g", 1), ("v", 1), ("g", 2), ("v", 2), ("g", 3), ("v", 3), ("z", 0), ("z", 1)]
STEP = [("g", 0), ("v", 0), ("g", 1), ("v", 1), ("z", 0), ("g", 2), ("v", 2), ("g", 3), ("v", 3), ("z", 1)]
NB = len(STEP)
STEPS = KE // 4 - 1
NZ = 2 * (STEPS + 1)
ZL = KE - 2
LOOK = 4
YR = 4
W = KD * P
PTAPS = 4
EARLY = 1
PTAPS0 = 1
UP = S + 2 * PAD + 2
CP = S + 2 * CPAD

N_CONF = 0
N_OUT1 = 3 * KE
N_DT = N_OUT1 + KE
N_XBC = N_DT + 1
N_Z = N_XBC + NXBC
N_OUT2 = N_Z + KE
N_END = N_OUT2 + KE

V_DWB, V_LNW, V_LNB, V_CB, V_SNW = 0, KE, 2 * KE, 3 * KE, 3 * KE + NXBC
NV = V_SNW + KE
C_NAMES = ["ident", "upto", "from_", "ones", "mean", "neg_f", "neg_b", "pick"]
N_CONST = 16 * (len(C_NAMES) + 3)


def loop(engine, n, body):
    body(0)
    with engine.Fori(1, n) as i:
        body(i)


def later(i):
    return not isinstance(i, int) or i > 0


def program(nc, wst, x, cvec, dww, cw, rows, srow, cst, out):
    with ExitStack() as ctx:
        def sb(name, shape, dt=F):
            return ctx.enter_context(nc.sbuf_tensor(name, shape, dt))

        def sem(name):
            return ctx.enter_context(nc.semaphore(name))

        def dram(name, shape):
            return nc.dram_tensor(name, shape, F, kind="Internal").ap()

        z1_d = dram("z1_d", [KE, P, S])
        h_d = dram("h_d", [T, P, D])
        xs_d = dram("xs_d", [T, P, E])
        bc_d = dram("bc_d", [T, P, 3, G, P])
        z2_d = dram("z2_d", [T, P, E])

        wraw = sb("wraw", [P, 2, W])
        wh = sb("wh", [P, 2, W], R)
        wl = sb("wl", [P, 2, W], R)
        acs_hi = sb("acs_hi", [P, 4, P], R)
        identR = sb("identR", [P, P], R)
        negR = sb("negR", [P, 2, P], R)
        pickR = sb("pickR", [P, 2 * H], R)
        c_f = {n: sb("c_" + n, [P, P if n != "pick" else 2 * H]) for n in C_NAMES}
        vec = sb("vec", [P, NV])
        taps = sb("taps", [P, KE * TAPS])
        ctaps = sb("ctaps", [P, NXBC * CTAPS])
        hrow = sb("hrow", [P, 5 * H])
        tap4 = sb("tap4", [P, 4 * TAPS])
        stat = sb("stat", [P, 64])
        arow = sb("arow", [P, 2 * H])
        AR = 26250
        with ExitStack() as first:
            ptmp = first.enter_context(nc.sbuf_tensor("ptmp", [P, S], F))
            xTh = first.enter_context(nc.sbuf_tensor("xTh", [P, KD, S], R))
            xTl = first.enter_context(nc.sbuf_tensor("xTl", [P, KD, S], R))
            arena = first.enter_context(nc.sbuf_tensor("arena", [P, AR], F))
        acs_hl = sb("acs_hl", [P, T, P], R)
        keep = sb("keep", [P, T, E])
        y2h = sb("y2h", [P, YR, S], R)
        y2l = sb("y2l", [P, YR, S], R)
        used = [0]

        def at(off, *shape):
            n = 1
            for s in shape:
                n *= s
            assert off + n <= AR, (off, shape)
            v = arena[:, off:off + n]
            names = "abcd"[:len(shape)]
            if len(shape) > 1:
                v = v.rearrange(f"p ({' '.join(names)}) -> p {' '.join(names)}",
                                **dict(zip(names, shape)))
            return v

        r_x = at(0, 2, D)
        r_n = at(2 * D, 2, D)
        r_w = at(4 * D, D)
        r_junk = at(5 * D, D)
        cv = at(0, KE, S)
        o = KE * S
        upad = at(o, 4, UP)
        xres = at(o, T, HALF)
        o += 4 * UP
        gate = at(o, 2, S)
        sigb = at(o, 2, HALF)
        vb = at(o + S, 2, HALF)
        sqb = at(o, 2, S)
        zst = at(o + 2 * S, 2, S)
        csum = at(o + 4 * S, S)
        rstd = csum
        cpad = at(0, 2, CP)
        csil = at(2 * CP, 2, S)
        stg = at(2 * CP + 2 * S, 2, T, P)
        z2b = at(2 * CP + 4 * S, T, HALF)
        dtt = at(2 * CP + 8 * S, 6, HALF)
        a2 = at(2 * CP + 8 * S + 6 * HALF, T, 2, 2 * H)
        o = 0
        xs_s = at(o, 2, E); o += 2 * E
        bc_s = at(o, 2, 3, G, P); o += 2 * 3 * G * P
        z_s = at(o, E); o += E
        sf = at(o, E); o += E
        xf_s = at(o, 2, HALF)
        xb_s = at(o, 2, E)
        o += 2 * HALF
        tmpb = at(o, 2, HALF); o += 2 * HALF
        yacc = at(o, E); o += E
        xD = at(o, 2, HALF); o += 2 * HALF
        Lb = at(o, 4, 4, P); o += 4 * HALF
        Mb = at(o, 4, 4, P); o += 4 * HALF
        sqj = at(o, HALF); o += HALF
        o_small = max(o, 2 * CP + 8 * S + 8 * HALF)
        o = o_small
        dt_s = at(o, T, 2 * H); o += HALF
        e_s = at(o, T, 2 * H); o += HALF
        dec_s = at(o, T, 2 * H); o += HALF
        coef_s = at(o, T, 2 * H); o += HALF
        nacs_s = at(o, T, 2 * H); o += HALF
        dtc = at(o, 2 * H); o += 2 * H
        nac = at(o, 2 * H); o += 2 * H
        ss_y = at(o, T, G); o += T * G
        rs_y = at(o, 3, T); o += 3 * T
        o = 2 * YR * S
        hf = at(o, T, D); o += T * D
        f_w = at(o, D); o += D
        f_o = at(o, 2, D); o += 2 * D
        f_junk = at(o, D); o += D
        assert o <= o_small

        ps = ctx.enter_context(nc.psum_tensor("ps", [P, 8, HALF], F))

        c_id = sem("c_id")
        c_ld = sem("c_ld")
        w_raw = [sem("w_raw0"), sem("w_raw1")]
        w_hi, w_lo = sem("w_hi"), sem("w_lo")
        cr = sem("cr")
        cr2 = sem("cr2")
        r_ld = [[sem(f"r{l}_ld0"), sem(f"r{l}_ld1")] for l in range(2)]
        rw_ld = [sem("rw_ld0"), sem("rw_ld1"), sem("rw_ld2")]
        r_ss = [sem(f"r{l}_ss") for l in range(2)]
        r_rs = [sem(f"r{l}_rs") for l in range(2)]
        r_xn = [sem(f"r{l}_xn") for l in range(2)]
        r_ps = [sem(f"r{l}_ps") for l in range(2)]
        r_hi = [sem(f"r{l}_hi") for l in range(2)]
        r_lo = [sem(f"r{l}_lo") for l in range(2)]
        a_fill, a_evac, a_um, a_tap, a_conv, a_cv, a_csum = (
            sem(n) for n in ("a_fill", "a_evac", "a_um", "a_tap", "a_conv", "a_cv", "a_csum"))
        a_tap4 = sem("a_tap4")
        a_pad = sem("a_pad")
        p_prod = sem("p_prod")
        p_tap = sem("p_tap")
        z_st = [sem("z_st0"), sem("z_st1")]
        z_ld = [sem("z_ld0"), sem("z_ld1")]
        l_mean, l_xc, l_sq, l_var, l_std, l_rstd = (
            sem(n) for n in ("l_mean", "l_xc", "l_sq", "l_var", "l_std", "l_rstd"))
        n_mul, n_silu, n_y = sem("n_mul"), sem("n_silu"), sem("n_y")
        n_zs = sem("n_zs")
        o_hi = [sem(f"o{l}_hi") for l in range(2)]
        o_lo = [sem(f"o{l}_lo") for l in range(2)]
        o_mm = [sem(f"o{l}_mm") for l in range(2)]
        o_t = [sem(f"o{l}_t") for l in range(2)]
        o_h = [sem(f"o{l}_h") for l in range(2)]
        xr_ld = [sem("xr_ld0"), sem("xr_ld1")]
        h_st = [sem("h_st0"), sem("h_st1")]
        d_ps, d_dt, d_neg, d_exp, d_A, d_a = (sem(n) for n in ("d_ps", "d_dt", "d_neg", "d_exp", "d_A", "d_a"))
        d_acs, d_sc, d_se, d_tr = sem("d_acs"), sem("d_sc"), sem("d_se"), sem("d_tr")
        d_trh, d_trl, d_coef = sem("d_trh"), sem("d_trl"), sem("d_coef")
        b_fill, b_evac, b_tap, b_sil, b_tr, b_te = (
            sem(n) for n in ("b_fill", "b_evac", "b_tap", "b_sil", "b_tr", "b_te"))
        b_pad = sem("b_pad")
        b_st = [sem("b_st0"), sem("b_st1")]
        b_sc = [sem("b_sc0"), sem("b_sc1")]
        q_mm, q_t, q_sil, q_st = sem("q_mm"), sem("q_t"), sem("q_sil"), sem("q_st")
        d_v = sem("d_v")
        p_x = [sem("p_x0"), sem("p_x1")]
        p_b = [sem("p_b0"), sem("p_b1")]
        p_xb, p_mm, p_dec, p_s = sem("p_xb"), sem("p_mm"), sem("p_dec"), sem("p_s")
        s_x = [sem("s_x0"), sem("s_x1")]
        s_b = [sem("s_b0"), sem("s_b1")]
        s_z = sem("s_z")
        s_cb, s_L, s_ex, s_M, s_yd, s_yo = (sem(n) for n in ("s_cb", "s_L", "s_ex", "s_M", "s_yd", "s_yo"))
        s_ya, s_tb, s_ad, s_xD, s_dd, s_g = (sem(n) for n in ("s_ya", "s_tb", "s_ad", "s_xD", "s_dd", "s_g"))
        s_xf, s_stt, s_sd, s_S, s_tr, s_te = (sem(n) for n in ("s_xf", "s_stt", "s_sd", "s_S", "s_tr", "s_te"))
        s_sq, s_dc, s_nc = sem("s_sq"), sem("s_dc"), sem("s_nc")
        s_zero = sem("s_zero")
        rs_r, rs_p = sem("rs_r"), sem("rs_p")
        f_ss, f_rs, f_out = sem("f_ss"), sem("f_rs"), sem("f_out")
        f_st = [sem("f_st0"), sem("f_st1")]

        block = ctx.enter_context(nc.Block())
        mm = nc.tensor.matmul

        def tile_done(l, m):
            if m % KE == KE - 1:
                return o_t[l], T * (m // KE + 1)
            return o_mm[l], m + 1 - m // KE

        def y_tile2(k):
            return keep[:].rearrange("p t (k s) -> p t k s", k=KE)[:, :, k]

        def bcast(ap, n):
            return ap.unsqueeze(2).to_broadcast([P, ap.shape[-1], n])

        @block.sync
        def _(sp):
            def wload(n, i=0, per=0):
                if not isinstance(i, int) or n + per * i >= 2:
                    sp.wait_ge(w_lo, n + per * i - 1)
                if isinstance(i, int):
                    src = wst[n + per * i]
                else:
                    src = wst[bass.ds(n + per * i, 1)].rearrange("a p w -> (a p) w")
                sp.dma_start(wraw[:, n % 2], src).then_inc(w_raw[n % 2], 16)

            def norm_loads(l, src):
                for t in range(T):
                    if t >= 2:
                        sp.wait_ge(r_xn[l], t - 1)
                    sp.dma_start(r_x[:, t % 2], src[t]).then_inc(r_ld[l][t % 2], 16)
                    if l == 0 and t == 1:
                        wload(0)
                        wload(1)

            norm_loads(0, x)

            def z_store(i, b, fills):
                sp.wait_ge(a_evac, fills)
                dst = z1_d[i] if isinstance(i, int) else z1_d[bass.ds(i, 1)].rearrange("a p s -> (a p) s")
                sp.dma_start(dst, zst[:, b]).then_inc(z_st[b], 16)

            for m, (kind, b) in enumerate(FIRST):
                wload(m + 2)
                if kind == "z":
                    z_store(b, b, 2 * m + 2)

            def conf(q):
                for j, (kind, b) in enumerate(STEP):
                    wload(NB + j + 2, q, NB)
                    if kind == "z":
                        z_store(2 * q + 2 + b, b, 2 * NB * (q + 1) + 2 * j + 2)
            loop(sp, STEPS, conf)
            for t in range(NZ, KE):
                wload(2 * KE + t + 2)
                if t < ZL:
                    z_store(t, t % 2, 4 * KE + 2 * t + 2)

            def gate_load(k):
                sp.wait_ge(z_st[k % 2], 16 * (k // 2 + 1))
                sp.dma_start(gate[:, k % 2], z1_d[k]).then_inc(z_ld[k % 2], 16)

            sp.wait_ge(a_conv, 2 * KE)
            sp.dma_start(xres[:], x.rearrange("t p d -> p t d")[:, :, 0:HALF]).then_inc(xr_ld[0], 16)
            sp.wait_ge(l_var, KE)
            for k in range(2):
                gate_load(k)
            z_store(ZL, 0, 6 * KE - 2)
            for k in range(KE):
                if k == 3:
                    z_store(KE - 1, 1, 6 * KE)
                if k + 2 < KE:
                    sp.wait_ge(n_y, k + 1)
                    gate_load(k + 2)
                if k in (3, 4) or k % 2 == 0 and k >= LOOK + YR:
                    wload(N_OUT1 + (k - 1 if k < 5 else 4 + (k - LOOK - YR) // 2))
            for h in range(2):
                for n in (range(N_OUT1 + 4 + (KE - LOOK - YR) // 2, N_OUT1 + 12), ())[h]:
                    wload(n)
                for t in range(T):
                    sp.wait_ge(o_h[0], T * h + t + 1)
                    sp.dma_start(h_d[t, :, HALF * h:HALF * (h + 1)], xres[:, t]).then_inc(h_st[h], 16)
                sp.wait_ge(h_st[h], 16 * T)
                if h == 0:
                    sp.dma_start(xres[:], x.rearrange("t p d -> p t d")[:, :, HALF:D]).then_inc(xr_ld[1], 16)
                    for n in range(N_OUT1 + 12, N_DT + 3):
                        wload(n)

            norm_loads(1, h_d)

            wload(N_DT + 3)

            def stores(n, b):
                sp.wait_ge(b_te, 4 * n + 2 * b + 2)
                dst = xs_d.rearrange("t p e -> p t e")[:, :, bass.ds((2 * n + b) * P, P)]
                sp.dma_start(dst, stg[:, b]).then_inc(b_st[b], 16)

            def xside(j):
                for b in range(2):
                    wload(N_XBC + 3 + b, j, 2)
                    if b == 0:
                        if later(j):
                            stores(j - 1, 1)
                    else:
                        stores(j, 0)
            loop(sp, KE // 2, xside)
            stores(KE // 2 - 1, 1)
            for g in range(G):
                wload(N_XBC + KE + 2 * g + 3)
                sp.wait_ge(b_sil, KE + 2 * g + 1)
                sp.dma_start(bc_d.rearrange("t p k g n -> p k g t n")[:, 0, g],
                             csil[:, 0].rearrange("p (t n) -> p t n", t=T)).then_inc(b_sc[0], 16)
                wload(N_XBC + KE + 2 * g + 4)
                sp.wait_ge(b_sil, KE + 2 * g + 2)
                sp.dma_start(bc_d.rearrange("t p k g n -> p k g t n")[:, 1, g],
                             csil[:, 1].rearrange("p (t n) -> p t n", t=T)).then_inc(b_sc[1], 16)
                sp.wait_ge(b_te, 2 * KE + 2 * g + 2)
                sp.dma_start(bc_d.rearrange("t p k g n -> p k g t n")[:, 2, g], stg[:, 0]).then_inc(b_st[0], 16)

            def back_load_x(r):
                sp.dma_start(xs_s[:, r % 2], xs_d[T - 1 - r]).then_inc(p_x[r % 2], 16)

            def back_load_b(r):
                sp.dma_start(bc_s[:, r % 2, 2], bc_d[T - 1 - r, :, 2]).then_inc(p_b[r % 2], 16)

            for q in range(G):
                for m in range(4):
                    if N_Z + 3 + 4 * q + m < N_OUT2 + 2:
                        wload(N_Z + 3 + 4 * q + m)
                if q == 0:
                    for b in range(2):
                        sp.wait_ge(b_st[b], 16 * (KE // 2 + (G if b == 0 else 0)))
                        sp.wait_ge(b_sc[b], 16 * G)
                    back_load_x(0)
                    back_load_x(1)
                    back_load_b(0)
                sp.wait_ge(q_sil, T * (q + 1))
                sp.dma_start(z2_d.rearrange("t p e -> p t e")[:, :, HALF * q:HALF * (q + 1)],
                             z2b[:]).then_inc(q_st, 16)
            sp.wait_ge(q_st, 16 * G)
            back_load_b(1)
            for r in range(2, T - 1):
                sp.wait_ge(p_xb, r - 1)
                back_load_x(r)
                sp.wait_ge(p_mm, r - 1)
                back_load_b(r)
            sp.wait_ge(p_mm, T - 1)

            def src1(d, c):
                return d[c] if isinstance(c, int) else d[bass.ds(c, 1)].squeeze(0)

            def xb_loads(c, b):
                sp.dma_start(xs_s[:, b], src1(xs_d, c)).then_inc(s_x[b], 16)
                sp.dma_start(bc_s[:, b], src1(bc_d, c)).then_inc(s_b[b], 16)

            for b in range(2):
                xb_loads(b, b)
            sp.dma_start(z_s, z2_d[0]).then_inc(s_z, 16)

            def chunk_dma(c2):
                for b in range(2):
                    c = 2 * c2 + b
                    if later(c):
                        sp.wait_ge(s_te, 4 * c)
                        sp.dma_start(z_s, src1(z2_d, c)).then_inc(s_z, 16)
                        sp.wait_ge(s_g, 4 * c)
                        if not (isinstance(c, int) and c + 1 == T):
                            xb_loads(c + 1, 1 - b)
            chunk_dma(0)
            with sp.Fori(1, T // 2 - 1) as c2:
                chunk_dma(c2)
            chunk_dma(T // 2 - 1)

            sp.wait_ge(s_te, 4 * T)
            sp.wait_ge(s_S, 4 * T)
            sp.dma_start(hf[:], h_d.rearrange("t p d -> p t d")).then_inc(xr_ld[0], 16)
            for n in range(N_OUT2 + 2, N_END):
                wload(n)
            for t in range(T):
                sp.wait_ge(f_out, t + 1)
                sp.dma_start(out[t], f_o[:, t % 2]).then_inc(f_st[t % 2], 16)
            for b in range(2):
                sp.wait_ge(f_st[b], 16 * T // 2)

        @block.scalar
        def _(act):
            act.dma_start(r_w[:], rows[0:1, :].to_broadcast([P, D])).then_inc(rw_ld[0], 16)
            for name in C_NAMES:
                act.dma_start(c_f[name][:], cst[name]).then_inc(c_id if name == "ident" else c_ld, 16)
            act.dma_start(vec[:], cvec).then_inc(c_ld, 16)
            act.dma_start(taps[:], dww).then_inc(c_ld, 16)
            act.dma_start(ctaps[:], cw).then_inc(c_ld, 16)
            act.dma_start(hrow[:], srow.to_broadcast([P, 5 * H])).then_inc(c_ld, 16)

            def split(n, i=0, per=0, free=None):
                act.wait_ge(w_raw[n % 2], 16 * (n // 2 + (per // 2) * i + 1))
                if free is not None:
                    act.wait_ge(*free)
                nc.scalar.copy(wh[:, n % 2], wraw[:, n % 2]).then_inc(w_hi, 1)

            def norm(l):
                def hi(t):
                    for q in range(2):
                        act.wait_ge(r_ps[l], 2 * t + q + 1)
                        nc.scalar.copy(xTh[:, 4 * q:4 * q + 4, t * P:(t + 1) * P],
                                       ps[:, 2 * (t % 2) + q].rearrange("p (k s) -> p k s", k=4)).then_inc(r_hi[l], 1)
                for t in range(T):
                    act.wait_ge(r_ld[l][t % 2], 16 * (t // 2 + 1))
                    if t >= 1:
                        act.wait_ge(r_ss[l], t)
                    nc.scalar.activation(r_junk[:], r_x[:, t % 2], ACT.Square,
                                         accum_out=stat[:, t:t + 1]).then_inc(r_ss[l], 1)
                    if t >= 1:
                        hi(t - 1)
                hi(T - 1)

            norm(0)
            split(0)
            split(1)
            act.wait_ge(c_ld, N_CONST)
            nc.scalar.copy(identR[:], c_f["ident"][:])
            nc.scalar.copy(negR[:, 0], c_f["neg_f"][:])
            nc.scalar.copy(negR[:, 1], c_f["neg_b"][:])
            nc.scalar.copy(pickR[:], c_f["pick"][:]).then_inc(cr, 1)

            def conv_out(p):
                for b in range(2):
                    for h in range(2):
                        i = 2 * p + b
                        act.wait_ge(a_conv, 4 * p + 2 * b + h + 1)
                        dst = arena[:, bass.ds(i * S + HALF * h, HALF)]
                        nc.scalar.activation(dst, ps[:, 4 + 2 * b + h], ACT.Identity,
                                             bias=vec[:, bass.ds(V_DWB + i, 1)]).then_inc(a_cv, 1)

            def evac(m, i, per, kind, tile):
                n = m + per * i
                for h in range(2):
                    act.wait_ge(a_fill, 2 * n + h + 1)
                    src = ps[:, (2 * m + h) % 4]
                    if kind != "z" and later(tile):
                        act.wait_ge(a_um, 2 * tile - 1 + h)
                    if kind == "g":
                        nc.scalar.activation(sigb[:, h], src, ACT.Sigmoid).then_inc(a_evac, 1)
                    elif kind == "v":
                        nc.scalar.copy(vb[:, h], src).then_inc(a_evac, 1)
                    else:
                        zi, b = tile
                        if later(zi):
                            act.wait_ge(z_st[b], 16 * zi)
                        nc.scalar.copy(zst[:, b, HALF * h:HALF * (h + 1)], src).then_inc(a_evac, 1)

            def block_step(m, i, per, kind, tile):
                if not (m == 0 and per == 0):
                    split(m + 1, i, per, free=(a_fill, 2 * (m + per * i)))
                evac(m, i, per, kind, tile)

            for m, (kind, tile) in enumerate(FIRST):
                block_step(m, 0, 0, kind, tile if kind != "z" else (0, tile))
            conv_out(0)

            def conf(q):
                for j, (kind, r) in enumerate(STEP):
                    block_step(NB + j, q, NB, kind, 4 * q + 4 + r if kind != "z" else (q + 1, r))
                    if j == NB // 2 - 1:
                        conv_out(2 * q + 1)
                    elif j == NB - 1:
                        conv_out(2 * q + 2)
            loop(act, STEPS, conf)
            for t in range(NZ, ZL):
                block_step(2 * KE + t, 0, 0, "z", (t // 2, t % 2))
            conv_out(KE // 2 - 1)

            for k in range(KE):
                act.wait_ge(l_xc, k + 1)
                if k >= 2:
                    act.wait_ge(l_var, k - 1)
                nc.scalar.square(sqb[:, k % 2], cv[:, k]).then_inc(l_sq, 1)
            split(2 * KE + ZL + 1, free=(a_fill, 2 * (2 * KE + ZL)))
            act.wait_ge(l_var, KE)
            for h in range(2):
                nc.scalar.activation(rstd[:, HALF * h:HALF * (h + 1)], ps[:, 6 + h], ACT.Sqrt,
                                     bias=EPS).then_inc(l_std, 1)
            evac(2 * KE + ZL, 0, 0, "z", (ZL // 2, 0))
            split(N_OUT1, free=(a_fill, 6 * KE - 2))

            def silu_y(k):
                act.wait_ge(z_ld[k % 2], 16 * (k // 2 + 1))
                nc.scalar.activation(gate[:, k % 2], gate[:, k % 2], ACT.Silu).then_inc(n_zs, 1)
                act.wait_ge(n_mul, k + 1)
                nc.scalar.activation(cv[:, k], cv[:, k], ACT.Silu, scale=vec[:, V_LNW + k:V_LNW + k + 1],
                                     bias=vec[:, V_LNB + k:V_LNB + k + 1]).then_inc(n_silu, 1)

            def y_hi(l, m, src, scale):
                if m >= YR:
                    act.wait_ge(*tile_done(l, m - YR))
                if scale is None:
                    nc.scalar.copy(xTh[:, m % YR], src).then_inc(o_hi[l], 1)
                else:
                    nc.scalar.activation(y2h[:, m % YR].rearrange("p (t s) -> p t s", t=T), src, ACT.Copy,
                                         scale=scale).then_inc(o_hi[l], 1)

            for k in range(LOOK):
                silu_y(k)
            act.wait_ge(a_fill, 6 * KE)
            for m in range(2 * KE + YR - 1):
                if m < KE:
                    act.wait_ge(n_y, m + 1)
                if m < 2 * KE:
                    y_hi(0, m, cv[:, m % KE], None)
                if m == 0:
                    evac(3 * KE - 1, 0, 0, "z", (ZL // 2, 1))
                if m == 1:
                    split(N_OUT1 + 1, free=(a_fill, 6 * KE))
                if m + LOOK < KE:
                    silu_y(m + LOOK)
                m -= YR - 1
                if m >= 0 and m % 2 == 1:
                    split(N_OUT1 + m // 2 + 2, free=tile_done(0, m))

            act.wait_ge(o_lo[0], 2 * KE)
            act.dma_start(r_w[:], rows[1:2, :].to_broadcast([P, D])).then_inc(rw_ld[1], 16)
            norm(1)

            act.wait_ge(d_dt, 1)
            nc.scalar.activation(dtt[:, 1], dtt[:, 0], ACT.Abs).then_inc(d_neg, 1)
            act.wait_ge(d_neg, 1)
            nc.scalar.activation(dtt[:, 2], dtt[:, 1], ACT.Exp, scale=-1.0).then_inc(d_exp, 1)
            nc.scalar.activation(arow[:], hrow[:, 2 * H:4 * H], ACT.Exp).then_inc(d_A, 1)

            def evac_sil(j, b):
                for h in range(2):
                    act.wait_ge(b_fill, 4 * j + 2 * b + h + 1)
                    if h == 0 and later(j):
                        act.wait_ge(b_tap, CTAPS * (2 * j + b - 1))
                    if h == 0 and not later(j):
                        act.wait_ge(b_pad, 1)
                    nc.scalar.copy(cpad[:, b, CPAD + HALF * h:CPAD + HALF * (h + 1)], ps[:, h]).then_inc(b_evac, 1)

            def sil(j, b):
                act.wait_ge(b_tap, CTAPS * (2 * j + b + 1))
                nc.scalar.activation(csil[:, b], ps[:, 2 + 2 * b:4 + 2 * b].rearrange("p a s -> p (a s)"),
                                     ACT.Silu).then_inc(b_sil, 1)

            def tr_out(b, cnt):
                for h in range(2):
                    act.wait_ge(b_tr, cnt + h + 1)
                    nc.scalar.copy(stg[:, b, 4 * h:4 * h + 4],
                                   ps[:, 6 + h].rearrange("p (t c) -> p t c", t=4)).then_inc(b_te, 1)

            def xside(j):
                for b in range(2):
                    if later(j) or b:
                        split(N_XBC + b + 1, j, 2, free=(b_fill, 4 * j + 2 * b))
                    else:
                        split(N_XBC + 1, free=(d_ps, 1))
                    evac_sil(j, b)
                    if later(j) or b:
                        jj, bb = (j, 0) if b else (j - 1, 1)
                        if later(jj):
                            act.wait_ge(b_st[bb], 16 * jj)
                        tr_out(bb, 4 * jj + 2 * bb)
                    sil(j, b)
            loop(act, KE // 2, xside)
            act.wait_ge(b_st[1], 16 * (KE // 2 - 1))
            tr_out(1, 4 * (KE // 2 - 1) + 2)

            def flat(v):
                return v.rearrange("p t h -> p (t h)")

            act.wait_ge(d_acs, 3)
            nc.scalar.activation(flat(e_s), ps[:, 4], ACT.Exp).then_inc(d_se, 1)
            nc.scalar.activation(flat(nacs_s), ps[:, 4], ACT.Copy, scale=-1.0).then_inc(d_se, 1)
            act.wait_ge(d_sc, 1)
            nc.scalar.activation(flat(dec_s), ps[:, 5], ACT.Exp).then_inc(d_se, 1)
            nc.scalar.activation(dtt[:, 5], dtt[:, 0], ACT.Exp).then_inc(d_se, 1)

            def decay_rows():
                for u in range(2):
                    pf, pb = (ps[:, 4 + d].rearrange("p (t l) -> p t l", t=4) for d in range(2))
                    cs = slice(4 * u, 4 * u + 4)
                    act.wait_ge(d_tr, 2 * u + 2)
                    nc.scalar.copy(acs_hl[0:32, cs], pf[0:32])
                    nc.scalar.copy(acs_hl[32:64, cs], pb[32:64])
                    if u:
                        act.wait_ge(d_trl, 2)
                    nc.scalar.copy(acs_hi[64:96], pf[64:96])
                    nc.scalar.copy(acs_hi[96:128], pb[96:128]).then_inc(d_trh, 1)

            for g in range(G):
                for b in range(2):
                    j = KE // 2 + g
                    split(N_XBC + KE + 2 * g + b + 1, free=(b_fill, 4 * j + 2 * b))
                    evac_sil(j, b)
                    if g == 0 and b == 0:
                        decay_rows()
                    if b == 1:
                        act.wait_ge(b_st[0], 16 * (KE // 2 + g))
                        tr_out(0, 2 * KE + 2 * g)
                    if g:
                        act.wait_ge(b_sc[b], 16 * g)
                    sil(j, b)

            for q in range(G):
                for m in range(4):
                    n = N_Z + 4 * q + m + 1
                    if m:
                        split(n, free=(q_mm, 3 * q + m))
                    else:
                        split(n, free=(q_t, T * q) if q else (b_fill, 2 * NXBC))
                if q:
                    act.wait_ge(q_st, 16 * q)
                for t in range(T):
                    act.wait_ge(q_t, T * q + t + 1)
                    nc.scalar.activation(z2b[:, t], ps[:, t], ACT.Silu).then_inc(q_sil, 1)
            split(N_OUT2 + 1, free=(q_t, T * G))

            def evac_y(c, i):
                act.wait_ge(s_g, 4 * c + i + 1)
                if i or later(c):
                    act.wait_ge(s_sq, 4 * c + i)
                total = ss_y.rearrange("p t g -> p (t g)")[:, bass.ds(4 * c + i, 1)]
                nc.scalar.activation(sqj, z_s[:, HALF * i:HALF * (i + 1)], ACT.Square,
                                     accum_out=total).then_inc(s_sq, 1)
                act.wait_ge(s_tr, 4 * c + i + 1)
                nc.scalar.copy(keep[:].rearrange("p t e -> p (t e)")[:, bass.ds(c * E + HALF * i, HALF)],
                               ps[:, 7]).then_inc(s_te, 1)

            def chunk(c2):
                for b in range(2):
                    c = 2 * c2 + b
                    if later(c):
                        act.wait_ge(s_ex, 16 * c)
                    nc.scalar.copy(nac, nacs_s[:, bass.ds(c, 1)].rearrange("p a h -> p (a h)")).then_inc(s_nc, 1)
                    act.wait_ge(s_nc, c + 1)
                    for u in range(16):
                        hq, d = divmod(u, 2)
                        act.wait_ge(s_L, 16 * c + u + 1)
                        if u >= 4 or later(c):
                            act.wait_ge(s_M, 16 * c + u - 3)
                        for e in range(4):
                            col = d * H + 4 * hq + e
                            last = nc.scalar.activation(Lb[:, u % 4, e], ps[:, 3 + u % 2, P * e:P * (e + 1)],
                                                        ACT.Exp, bias=nac[:, col:col + 1])
                        last.then_inc(s_ex, 1)
                        if u in (3, 5, 7, 9) and later(c):
                            evac_y(c - 1, (u - 3) // 2)
            loop(act, T // 2, chunk)
            for i in range(4):
                evac_y(T - 1, i)
            for m in range(2 * KE + YR - 1):
                if m < 2 * KE:
                    y_hi(1, m, y_tile2(m % KE), vec[:, V_SNW + m % KE:V_SNW + m % KE + 1])
                m -= YR - 1
                if m >= 0 and m % 2 == 1 and N_OUT2 + m // 2 + 2 < N_END:
                    split(N_OUT2 + m // 2 + 2, free=tile_done(1, m))
                if m == 1 - YR:
                    act.wait_ge(s_S, 4 * T)
                    act.dma_start(f_w[:], rows[2:3, :].to_broadcast([P, D])).then_inc(rw_ld[2], 16)
            for t in range(T):
                act.wait_ge(o_h[1], T + t + 1)
                if t:
                    act.wait_ge(f_ss, t)
                nc.scalar.activation(f_junk, hf[:, t], ACT.Square, accum_out=stat[:, t:t + 1]).then_inc(f_ss, 1)


        @block.gpsimd
        def _(pool):
            tt = nc.gpsimd.tensor_tensor

            def split(n, i=0, per=0):
                pool.wait_ge(w_hi, n + per * i + 1)
                tt(wl[:, n % 2], wraw[:, n % 2], wh[:, n % 2].bitcast(F), ALU.subtract).then_inc(w_lo, 1)

            nc.gpsimd.memset(stat[:, 63:64], -0.5).then_inc(cr2, 1)
            nc.gpsimd.memset(csum, 0.0).then_inc(cr2, 1)
            nc.gpsimd.memset(upad, 0.0).then_inc(a_pad, 1)

            def norm(l):
                for t in range(T):
                    pool.wait_ge(r_ss[l], t + 1)
                    nc.gpsimd.tensor_scalar(stat[:, 16 + t:17 + t], stat[:, t:t + 1], 1.0 / D, EPS,
                                            ALU.mult, ALU.add).then_inc(r_rs[l], 1)
                    pool.wait_ge(r_rs[l], 2 * t + 1)
                    if l == 0 and t == 0:
                        pool.wait_ge(cr2, 1)
                    tt(stat[:, 32 + t:33 + t], stat[:, 16 + t:17 + t], stat[:, 63:64], ALU.pow).then_inc(r_rs[l], 1)

            norm(0)
            split(0)
            split(1)
            pool.wait_ge(a_pad, 1)

            def add_tile(i):
                pool.wait_ge(a_cv, 2 * i + 2)
                pool.wait_ge(a_csum, i) if later(i) else pool.wait_ge(cr2, 2)
                tt(csum, csum, arena[:, bass.ds(i * S, S)], ALU.add).then_inc(a_csum, 1)

            def make_u(i, slot, evacs):
                if later(i - 3):
                    pool.wait_ge(a_conv, 2 * i - 6)
                for h in range(2):
                    pool.wait_ge(a_evac, evacs + h + 1)
                    tt(upad[:, slot, PAD + HALF * h:PAD + HALF * (h + 1)], sigb[:, h], vb[:, h],
                       ALU.mult).then_inc(a_um, 1)

            def first_taps(i, k0, k1):
                slot, acc = i % 4, cv[:, i]
                before = PTAPS * i - (PTAPS - PTAPS0 if i else 0)
                for k in range(k0, min(k1, PTAPS if i else PTAPS0)):
                    wk = taps[:, i * TAPS + k:i * TAPS + k + 1].to_broadcast([P, S])
                    if k == 0:
                        pool.wait_ge(a_um, 2 * i + 2)
                        tt(acc, upad[:, slot, 0:S], wk, ALU.mult).then_inc(p_tap, 1)
                    else:
                        pool.wait_ge(p_tap, before + k)
                        tt(ptmp[:], upad[:, slot, k:k + S], wk, ALU.mult).then_inc(p_prod, 1)
                        pool.wait_ge(p_prod, before + k - i)
                        tt(acc, acc, ptmp[:], ALU.add).then_inc(p_tap, 1)

            pool.wait_ge(c_ld, N_CONST)
            for m, (kind, i) in enumerate(FIRST):
                if m:
                    split(m + 1)
                if kind == "v":
                    make_u(i, i, 2 * m)
                    first_taps(i, 0, EARLY)
                elif 0 < m <= 8:
                    first_taps(m // 2 - 1, EARLY, PTAPS)

            def conf(q):
                late = None
                for j, (kind, r) in enumerate(STEP):
                    split(NB * (q + 1) + j + 1)
                    i = 4 * q + 4 + r
                    if kind == "v":
                        make_u(i, r, 2 * NB * (q + 1) + 2 * j)
                        first_taps(i, 0, EARLY)
                        late = i
                    elif late is not None:
                        first_taps(late, EARLY, PTAPS)
                        late = None
                    if j in (2, 7):
                        add_tile(4 * q + (j > 2) * 2)
                        add_tile(4 * q + (j > 2) * 2 + 1)
            for q in range(STEPS):
                conf(q)
            for t in range(NZ, ZL):
                split(2 * KE + t + 1)
                if t == NZ + 1:
                    add_tile(KE - 4)
                    add_tile(KE - 3)
            split(2 * KE + ZL + 1)
            split(N_OUT1)

            def y_tile(k):
                pool.wait_ge(n_silu, k + 1)
                pool.wait_ge(n_zs, k + 1)
                tt(cv[:, k], cv[:, k], gate[:, k % 2], ALU.mult).then_inc(n_y, 1)

            for k in range(LOOK):
                y_tile(k)
            split(N_OUT1 + 1)
            for m in range(2 * KE + YR - 1):
                if m + LOOK < KE:
                    y_tile(m + LOOK)
                m -= YR - 1
                if m >= 0 and m % 2 == 1:
                    split(N_OUT1 + m // 2 + 2)

            norm(1)
            pool.wait_ge(r_ps[1], 2 * T)
            nc.gpsimd.memset(cpad, 0.0).then_inc(b_pad, 1)

            def xside(j):
                for b in range(2):
                    split(N_XBC + 1 + b, j, 2)
            loop(pool, KE // 2, xside)
            for g in range(G):
                for b in range(2):
                    split(N_XBC + KE + 2 * g + b + 1)
            for m in range(KE + 1):
                split(N_Z + 1 + m)

            for r, c in enumerate(range(T - 1, 0, -1)):
                b = r % 2
                pool.wait_ge(p_x[b], 16 * (r // 2 + 1))
                if r >= 2:
                    pool.wait_ge(p_mm, r - 1)
                elif r == 0:
                    pool.wait_ge(d_coef, 1)
                tt(xb_s[:, b].rearrange("p (h e) -> p h e", h=H), xs_s[:, b].rearrange("p (h e) -> p h e", h=H),
                   bcast(coef_s[:, c, H:2 * H], HD), ALU.mult).then_inc(p_xb, 1)

            def heads(v):
                return v.rearrange("p (h e) -> p h e", h=8)

            def chunk(c2):
                for b in range(2):
                    c = 2 * c2 + b

                    def x_skip(g):
                        if g == 0:
                            pool.wait_ge(s_x[b], 16 * (c2 + 1))
                        if g >= 2 or later(c):
                            pool.wait_ge(s_yd, 8 * c + 2 * g - 2)
                        if g >= 2 or later(c):
                            pool.wait_ge(s_xD, 4 * c + g - 1)
                        tt(heads(xD[:, g % 2]), heads(xs_s[:, b, HALF * g:HALF * (g + 1)]),
                           bcast(hrow[:, 4 * H + 8 * g:4 * H + 8 * g + 8], HD), ALU.mult).then_inc(s_xD, 1)

                    def x_state(g):
                        if g >= 2 or later(c):
                            pool.wait_ge(s_stt, 4 * c + g - 1)
                            pool.wait_ge(s_xf, 4 * c + g - 1)
                        elif g == 0:
                            pool.wait_ge(p_mm, T - 1)
                        tt(heads(xf_s[:, g % 2]), heads(xs_s[:, b, HALF * g:HALF * (g + 1)]),
                           bcast(coef_s.rearrange("p t h -> p (t h)")[:, bass.ds(c * 2 * H + 8 * g, 8)], HD),
                           ALU.mult).then_inc(s_xf, 1)

                    def y_add(g):
                        pool.wait_ge(s_tb, 4 * c + g + 1)
                        pool.wait_ge(s_ya, 4 * c + g + 1)
                        tt(yacc[:, HALF * g:HALF * (g + 1)], yacc[:, HALF * g:HALF * (g + 1)], tmpb[:, g % 2],
                           ALU.add).then_inc(s_ad, 1)

                    def gate(g):
                        if g == 0:
                            pool.wait_ge(s_z, 16 * (c + 1))
                        pool.wait_ge(s_dd, 4 * c + g + 1)
                        tt(z_s[:, HALF * g:HALF * (g + 1)], yacc[:, HALF * g:HALF * (g + 1)],
                           z_s[:, HALF * g:HALF * (g + 1)], ALU.mult).then_inc(s_g, 1)

                    x_skip(0)
                    y_add(0)
                    x_skip(1)
                    x_state(0)
                    y_add(1)
                    gate(0)
                    x_state(1)
                    x_skip(2)
                    y_add(2)
                    gate(1)
                    x_state(2)
                    x_skip(3)
                    x_state(3)
                    y_add(3)
                    gate(2)
                    gate(3)
            loop(pool, T // 2, chunk)

            pool.wait_ge(rs_r, 1)
            nc.gpsimd.tensor_scalar(rs_y[:, 1], rs_y[:, 0], 1.0 / E, EPS, ALU.mult, ALU.add).then_inc(rs_p, 1)
            pool.wait_ge(rs_p, 1)
            tt(rs_y[:, 2], rs_y[:, 1], stat[:, 63:64].to_broadcast([P, T]), ALU.pow).then_inc(rs_p, 1)
            for m in range(1, 2 * KE, 2):
                if N_OUT2 + m // 2 + 2 < N_END:
                    split(N_OUT2 + m // 2 + 2)
            for t in range(T):
                pool.wait_ge(f_ss, t + 1)
                nc.gpsimd.tensor_scalar(stat[:, 16 + t:17 + t], stat[:, t:t + 1], 1.0 / D, EPS,
                                        ALU.mult, ALU.add).then_inc(f_rs, 1)
                pool.wait_ge(f_rs, 2 * t + 1)
                tt(stat[:, 32 + t:33 + t], stat[:, 16 + t:17 + t], stat[:, 63:64], ALU.pow).then_inc(f_rs, 1)

        @block.vector
        def _(dve):
            tt, ts, stt = nc.vector.tensor_tensor, nc.vector.tensor_scalar, nc.vector.scalar_tensor_tensor

            def norm(l):
                def lo(t):
                    for q in range(2):
                        dve.wait_ge(r_hi[l], 2 * t + q + 1)
                        cols = (slice(None), slice(4 * q, 4 * q + 4), slice(t * P, (t + 1) * P))
                        tt(xTl[cols], ps[:, 2 * (t % 2) + q].rearrange("p (k s) -> p k s", k=4),
                           xTh[cols].bitcast(F), ALU.subtract).then_inc(r_lo[l], 1)
                for t in range(T):
                    if t == 0:
                        dve.wait_ge(rw_ld[l], 16)
                    dve.wait_ge(r_rs[l], 2 * t + 2)
                    if t >= 2:
                        dve.wait_ge(r_ps[l], 2 * t - 2)
                    stt(r_n[:, t % 2], r_x[:, t % 2], stat[:, 32 + t:33 + t], r_w, ALU.mult,
                        ALU.mult).then_inc(r_xn[l], 1)
                    if t >= 1:
                        lo(t - 1)
                lo(T - 1)

            norm(0)

            def conv(q):
                dve.wait_ge(c_ld, N_CONST)
                if later(q):
                    dve.wait_ge(a_conv, 8 * q)
                nc.vector.tensor_copy(tap4[:], taps[:, bass.ds(q * 4 * TAPS, 4 * TAPS)]).then_inc(a_tap4, 1)
                dve.wait_ge(a_tap4, q + 1)
                for pp in range(2):
                    p = 2 * q + pp
                    base = 2 * (TAPS - PTAPS - 1) * p + (PTAPS - PTAPS0 if later(p) else 0)

                    def w(b, k):
                        return tap4[:, (2 * pp + b) * TAPS + k:(2 * pp + b) * TAPS + k + 1]

                    def acc(b):
                        return ps[:, 4 + 2 * b:6 + 2 * b].rearrange("p a s -> p (a s)")

                    def first(b):
                        i = 2 * p + b
                        k = PTAPS if later(i) else PTAPS0
                        dve.wait_ge(a_um, 2 * i + 2)
                        dve.wait_ge(p_tap, PTAPS * (i + 1) - (PTAPS - PTAPS0))
                        if later(p):
                            dve.wait_ge(a_cv, 4 * p - 4 + 2 * b + 2)
                        stt(acc(b), upad[:, 2 * pp + b, k:k + S], w(b, k), arena[:, bass.ds(i * S, S)],
                            ALU.mult, ALU.add).then_inc(a_tap, 1)

                    def tap(b, k, before):
                        dve.wait_ge(a_tap, base + before)
                        stt(acc(b), upad[:, 2 * pp + b, k:k + S], w(b, k), acc(b), ALU.mult, ALU.add).then_inc(a_tap, 1)

                    def last(b, before):
                        dve.wait_ge(a_tap, base + before)
                        k = TAPS - 1
                        for h in range(2):
                            half = ps[:, 4 + 2 * b + h]
                            stt(half, upad[:, 2 * pp + b, k + HALF * h:k + HALF * (h + 1)], w(b, k), half, ALU.mult,
                                ALU.add).then_inc(a_conv, 1)

                    if later(p):
                        first(0)
                        first(1)
                        for k in range(PTAPS + 1, TAPS - 1):
                            for b in range(2):
                                tap(b, k, 2 * (k - PTAPS - 1) + b + 1)
                        for b in range(2):
                            last(b, 2 * (TAPS - PTAPS - 2) + b + 1)
                    else:
                        done = 0
                        for b in range(2):
                            first(b)
                            done += 1
                            for k in range((PTAPS if b else PTAPS0) + 1, TAPS - 1):
                                tap(b, k, done)
                                done += 1
                            last(b, done)
            loop(dve, KE // 4, conv)

            dve.wait_ge(l_mean, 2)
            dve.wait_ge(a_cv, 2 * KE)
            for k in range(KE):
                tt(cv[:, k], cv[:, k], ps[:, 4:6].rearrange("p a s -> p (a s)"), ALU.subtract).then_inc(l_xc, 1)
            for h in range(2):
                dve.wait_ge(l_std, h + 1)
                half = rstd[:, HALF * h:HALF * (h + 1)]
                nc.vector.reciprocal(half, half).then_inc(l_rstd, 1)
            dve.wait_ge(l_rstd, 2)

            def mul(k):
                tt(cv[:, k], cv[:, k], rstd, ALU.mult).then_inc(n_mul, 1)

            def y_lo(l, m, src, scale):
                dve.wait_ge(o_hi[l], m + 1)
                if scale is None:
                    tt(xTl[:, m % YR], src, xTh[:, m % YR].bitcast(F), ALU.subtract).then_inc(o_lo[l], 1)
                else:
                    yh, yl = (v[:, m % YR].rearrange("p (t s) -> p t s", t=T) for v in (y2h, y2l))
                    stt(yl, src, scale, yh.bitcast(F), ALU.mult, ALU.subtract).then_inc(o_lo[l], 1)

            for k in range(LOOK + 1):
                mul(k)

            def residual(h):
                dve.wait_ge(xr_ld[h], 16)
                for t in range(T):
                    dve.wait_ge(o_t[0], T * h + t + 1)
                    tt(xres[:, t], ps[:, t], xres[:, t], ALU.add).then_inc(o_h[0], 1)

            for m in range(2 * KE):
                if m + LOOK + 1 < KE:
                    mul(m + LOOK + 1)
                if m == KE + YR - 1:
                    residual(0)
                y_lo(0, m, cv[:, m % KE], None)
            residual(1)

            norm(1)

            steps = [0]

            def step(ins):
                steps[0] += 1
                ins.then_inc(d_v, 1)
                dve.wait_ge(d_v, steps[0])

            dve.wait_ge(d_ps, 1)
            tt(dtt[:, 0].rearrange("p (t h) -> p t h", t=T), ps[:, 7].rearrange("p (t h) -> p t h", t=T),
               hrow[:, 0:2 * H].unsqueeze(1).to_broadcast([P, T, 2 * H]), ALU.add).then_inc(d_dt, 1)
            v, w1, e, r2, _, _ = (dtt[:, n] for n in range(6))
            dve.wait_ge(d_exp, 1)
            step(ts(r2, e, 2.0, None, ALU.add))
            step(nc.vector.reciprocal(w1, r2))
            step(tt(e, e, w1, ALU.mult))
            step(tt(r2, e, e, ALU.mult))
            step(ts(w1, r2, 1.0 / 17, None, ALU.mult))
            for j in range(7, 0, -1):
                step(stt(w1, w1, 1.0 / (2 * j + 1), r2, ALU.add, ALU.mult))
            step(stt(w1, w1, 1.0, e, ALU.add, ALU.mult))
            step(ts(v, v, 0.0, None, ALU.max))
            step(stt(dt_s.rearrange("p t h -> p (t h)"), w1, 2.0, v, ALU.mult, ALU.add))
            dve.wait_ge(d_A, 1)
            for n in range(2):
                stt(a2[:, :, n], dt_s, -1.0, arow[:].unsqueeze(1).to_broadcast([P, T, 2 * H]), ALU.mult,
                    ALU.mult).then_inc(d_a, 1)

            def taps5(j, b):
                i = 2 * j + b
                acc = ps[:, 2 + 2 * b:4 + 2 * b].rearrange("p a s -> p (a s)")
                dve.wait_ge(b_evac, 2 * i + 2)
                if later(j):
                    dve.wait_ge(b_sil, i - 1)
                for k in range(CTAPS):
                    wk = ctaps[:, bass.ds(i * CTAPS + k, 1)]
                    if k == 0:
                        ts(acc, cpad[:, b, 0:S], wk, vec[:, bass.ds(V_CB + i, 1)], ALU.mult, ALU.add).then_inc(b_tap, 1)
                    else:
                        dve.wait_ge(b_tap, CTAPS * i + k)
                        stt(acc, cpad[:, b, k:k + S], wk, acc, ALU.mult, ALU.add).then_inc(b_tap, 1)

            def xside(j):
                taps5(j, 0)
                taps5(j, 1)
            loop(dve, KE // 2, xside)
            dve.wait_ge(d_se, 2)
            nc.vector.tensor_copy(w1, ps[:, 4]).then_inc(d_v, 1)
            steps[0] += 1
            dve.wait_ge(d_v, steps[0])
            tt(v, ps[:, 5], w1, ALU.subtract).then_inc(d_sc, 1)
            dve.wait_ge(d_se, 4)
            tt(coef_s.rearrange("p t h -> p (t h)"), dtt[:, 5], dt_s.rearrange("p t h -> p (t h)"),
               ALU.mult).then_inc(d_coef, 1)

            def decay_rows():
                for u in range(2):
                    cs = slice(4 * u, 4 * u + 4)
                    dve.wait_ge(d_trh, u + 1)
                    for d in range(2):
                        rows_ = slice(64 + 32 * d, 96 + 32 * d)
                        tt(acs_hl[rows_, cs], ps[rows_, 4 + d].rearrange("p (t l) -> p t l", t=4),
                           acs_hi[rows_].bitcast(F), ALU.subtract).then_inc(d_trl, 1)

            for g in range(G):
                if g == 0:
                    decay_rows()
                taps5(KE // 2 + g, 0)
                taps5(KE // 2 + g, 1)

            dve.wait_ge(q_t, T * G)
            nc.vector.memset(keep[:, T - 1], 0.0).then_inc(p_s, 1)
            dve.wait_ge(q_st, 16 * G)
            nc.vector.memset(sf, 0.0).then_inc(s_zero, 1)
            for r, c in enumerate(range(T - 1, 0, -1)):
                old, new = keep[:, c], keep[:, c - 1]
                dve.wait_ge(p_s, r + 1)
                tt(new.rearrange("p (h e) -> p h e", h=H), old.rearrange("p (h e) -> p h e", h=H),
                   bcast(dec_s[:, c, H:2 * H], HD), ALU.mult).then_inc(p_dec, 1)
                dve.wait_ge(p_dec, r + 1)
                dve.wait_ge(p_mm, r + 1)
                tt(new, new, ps[:, 4 * (r % 2):4 * (r % 2) + 4].rearrange("p a s -> p (a s)"), ALU.add).then_inc(p_s, 1)

            def heads(v_):
                return v_.rearrange("p (h e) -> p h e", h=8)

            def head_col(tab, c, col):
                return bcast(tab.rearrange("p t h -> p (t h)")[:, bass.ds(c * 2 * H + col, 8)], HD)

            def chunk(c2):
                for b in range(2):
                    c = 2 * c2 + b
                    if later(c):
                        dve.wait_ge(s_M, 16 * c)
                    nc.vector.tensor_copy(dtc, dt_s.rearrange("p t h -> p (t h)")[
                        :, bass.ds(c * 2 * H, 2 * H)]).then_inc(s_dc, 1)

                    def from_states(g):
                        dve.wait_ge(s_yo, 8 * c + 2 * g + 1)
                        if later(c):
                            dve.wait_ge(s_g, 4 * c + g - 3)
                        tt(heads(yacc[:, HALF * g:HALF * (g + 1)]), heads(ps[:, 1]), head_col(e_s, c, 8 * g),
                           ALU.mult).then_inc(s_ya, 1)
                        dve.wait_ge(s_yo, 8 * c + 2 * g + 2)
                        if g >= 2 or later(c):
                            dve.wait_ge(s_ad, 4 * c + g - 1)
                        tt(heads(tmpb[:, g % 2]), heads(ps[:, 2]), head_col(e_s, c, H + 8 * g),
                           ALU.mult).then_inc(s_tb, 1)

                    def masked(u):
                        hq, d = divmod(u, 2)
                        if u == 0:
                            dve.wait_ge(s_dc, c + 1)
                            dve.wait_ge(s_cb, c + 1)
                        dve.wait_ge(s_ex, 16 * c + u + 1)
                        if u >= 4 or later(c):
                            dve.wait_ge(s_yd, 8 * c + hq - 1)
                        for n in range(4):
                            col = d * H + 4 * hq + n
                            last = stt(Mb[:, u % 4, n], Lb[:, u % 4, n], dtc[:, col:col + 1],
                                       ps[:, 0, P * (hq // 2):P * (hq // 2 + 1)], ALU.mult, ALU.mult)
                        last.then_inc(s_M, 1)

                    def diag(g):
                        dve.wait_ge(s_yd, 8 * c + 2 * g + 2)
                        dve.wait_ge(s_ad, 4 * c + g + 1)
                        tt(yacc[:, HALF * g:HALF * (g + 1)], ps[:, 5 + g % 2], yacc[:, HALF * g:HALF * (g + 1)],
                           ALU.add).then_inc(s_dd, 1)

                    def state(g):
                        cols = slice(HALF * g, HALF * (g + 1))
                        dve.wait_ge(s_yo, 8 * c + 2 * g + 1)
                        if later(c):
                            dve.wait_ge(s_S, 4 * c + g - 3)
                        tt(heads(sf[:, cols]), heads(sf[:, cols]), head_col(dec_s, c, 8 * g), ALU.mult).then_inc(s_sd, 1)
                        dve.wait_ge(s_sd, 4 * c + g + 1)
                        dve.wait_ge(s_stt, 4 * c + g + 1)
                        tt(sf[:, cols], sf[:, cols], ps[:, 7], ALU.add).then_inc(s_S, 1)

                    from_states(0)
                    for hq in range(8):
                        masked(2 * hq)
                        masked(2 * hq + 1)
                        if hq in (1, 3, 5):
                            from_states((hq + 1) // 2)
                        if hq >= 4:
                            state(hq - 4)
                        if hq in (2, 4, 6):
                            diag(hq // 2 - 1)
                    diag(3)
            loop(dve, T // 2, chunk)

            dve.wait_ge(s_sq, 4 * T)
            nc.vector.tensor_reduce(rs_y[:, 0], ss_y, mybir.AxisListType.X, ALU.add).then_inc(rs_r, 1)

            def residual2(h):
                dve.wait_ge(xr_ld[0], 32)
                if h == 0:
                    dve.wait_ge(rs_p, 2)
                for t in range(T):
                    dve.wait_ge(o_t[1], T * h + t + 1)
                    cols = hf[:, t, HALF * h:HALF * (h + 1)]
                    stt(cols, ps[:, t], rs_y[:, 2, t:t + 1], cols, ALU.mult, ALU.add).then_inc(o_h[1], 1)

            for m in range(2 * KE):
                if m == KE + YR - 1:
                    residual2(0)
                y_lo(1, m, y_tile2(m % KE), vec[:, V_SNW + m % KE:V_SNW + m % KE + 1])
            residual2(1)
            for t in range(T):
                if t == 0:
                    dve.wait_ge(rw_ld[2], 16)
                dve.wait_ge(f_rs, 2 * t + 2)
                if t >= 2:
                    dve.wait_ge(f_st[t % 2], 16 * (t // 2))
                stt(f_o[:, t % 2], hf[:, t], stat[:, 32 + t:33 + t], f_w, ALU.mult, ALU.mult).then_inc(f_out, 1)

        @block.tensor
        def _(pe):
            def mm3(dst, lh, ll, rh, rl, start, stop):
                mm(dst, ll, rh, start=start, stop=False)
                mm(dst, lh, rl, start=False, stop=False)
                return mm(dst, lh, rh, start=False, stop=stop)

            def norm(l):
                for t in range(T):
                    pe.wait_ge(r_xn[l], t + 1)
                    for q in range(2):
                        if t >= 2:
                            pe.wait_ge(r_lo[l], 2 * (t - 2) + q + 1)
                        for k in range(4):
                            last = nc.tensor.transpose(ps[:, 2 * (t % 2) + q, P * k:P * (k + 1)],
                                                       r_n[:, t % 2, P * (4 * q + k):P * (4 * q + k + 1)],
                                                       c_f["ident"][:])
                        last.then_inc(r_ps[l], 1)

            def by_channel(n, h, bank, sem_):
                cols = slice(HALF * h, HALF * (h + 1))
                for k in range(KD):
                    wc = slice(P * k, P * (k + 1))
                    last = mm3(ps[:, bank], wh[:, n % 2, wc], wl[:, n % 2, wc], xTh[:, k, cols], xTl[:, k, cols],
                               k == 0, k == KD - 1)
                last.then_inc(sem_, 1)

            pe.wait_ge(c_id, 16)
            norm(0)
            pe.wait_ge(c_ld, N_CONST)
            pe.wait_ge(r_lo[0], 2 * T)

            def conf_block(m, i=0, per=0):
                pe.wait_ge(w_lo, m + per * i + 1)
                for h in range(2):
                    f = 2 * m + h
                    if f >= 4:
                        pe.wait_ge(a_evac, f + 2 * per * i - 3)
                    by_channel(m, h, f % 4, a_fill)

            for m in range(len(FIRST)):
                conf_block(m)

            def conf(q):
                for j in range(NB):
                    conf_block(NB + j, q, NB)
            loop(pe, STEPS, conf)
            for m in range(2 * KE + NZ, 2 * KE + ZL):
                conf_block(m)

            pe.wait_ge(a_csum, KE - 2)
            pe.wait_ge(a_cv, 2 * KE)
            for h in range(2):
                cols = slice(HALF * h, HALF * (h + 1))
                mm(ps[:, 4 + h], c_f["mean"][:], csum[:, cols], start=True, stop=False)
                mm(ps[:, 4 + h], c_f["mean"][:], cv[:, KE - 2, cols], start=False, stop=False)
                mm(ps[:, 4 + h], c_f["mean"][:], cv[:, KE - 1, cols], start=False, stop=True).then_inc(l_mean, 1)
            for k in range(KE):
                pe.wait_ge(l_sq, k + 1)
                for h in range(2):
                    last = mm(ps[:, 6 + h], c_f["mean"][:], sqb[:, k % 2, HALF * h:HALF * (h + 1)],
                              start=k == 0, stop=k == KE - 1)
                last.then_inc(l_var, 1)
            for m in range(2 * KE + ZL, 3 * KE):
                conf_block(m)

            def out_product(l, n0, bank_free):
                for h in range(2):
                    def pair(kp, first=False, final=False):
                        for kk in range(2):
                            m = KE * h + 2 * kp + kk
                            if kk == 0:
                                pe.wait_ge(w_lo, n0 + KE // 2 * h + kp + 1)
                            pe.wait_ge(o_lo[l], m + 1)
                            for t in range(T):
                                if first and kk == 0:
                                    if h:
                                        pe.wait_ge(o_h[l], t + 1)
                                    elif t in (0, 2):
                                        bank_free(t)
                                tc = slice(P * t, P * (t + 1))
                                wc = slice(HALF * kk, HALF * (kk + 1))
                                s_ = (n0 + KE // 2 * h + parity(kp)) % 2
                                yh, yl = ((xTh, xTl), (y2h, y2l))[l]
                                ys = 2 * parity(kp) + kk
                                last = mm3(ps[:, t], yh[:, ys, tc], yl[:, ys, tc], wh[:, s_, wc], wl[:, s_, wc],
                                           first and kk == 0, final and kk == 1)
                                if final and kk == 1:
                                    last.then_inc(o_t[l], 1)
                            if not (final and kk == 1):
                                last.then_inc(o_mm[l], 1)
                    par = [0]

                    def parity(kp):
                        return par[0]
                    par[0] = 0
                    pair(0, first=True)
                    with pe.Fori(0, KE // 4 - 1) as i:
                        par[0] = 1
                        pair(2 * i + 1)
                        par[0] = 0
                        pair(2 * i + 2)
                    par[0] = 1
                    pair(KE // 2 - 1, final=True)

            def conf_banks(t):
                pe.wait_ge(a_evac, 6 * KE - 2 + t)
                if t == 0:
                    pe.wait_ge(l_std, 2)
                    pe.wait_ge(l_xc, KE)

            out_product(0, N_OUT1, conf_banks)

            norm(1)

            pe.wait_ge(w_lo, N_DT + 1)
            pe.wait_ge(r_lo[1], 2 * T)
            s_ = N_DT % 2
            for t in range(T):
                for k in range(KD):
                    tc, wc = slice(P * t, P * (t + 1)), slice(2 * H * k, 2 * H * (k + 1))
                    last = mm3(ps[:, 7, 2 * H * t:2 * H * (t + 1)], xTh[:, k, tc], xTl[:, k, tc],
                               wh[:, s_, wc], wl[:, s_, wc], k == 0, k == KD - 1)
            last.then_inc(d_ps, 1)

            def fill(j, b):
                i = 2 * j + b
                pe.wait_ge(w_lo, N_XBC + i + 1)
                for h in range(2):
                    if later(j) or b:
                        pe.wait_ge(b_evac, 2 * i + h - 1)
                    by_channel(N_XBC + b, h, h, b_fill)

            def turn(b, sil_count, evac_count):
                pe.wait_ge(b_sil, sil_count)
                for h in range(2):
                    if evac_count is not None:
                        pe.wait_ge(b_te, evac_count + h)
                    for t in range(4):
                        last = nc.tensor.transpose(ps[:, 6 + h, P * t:P * (t + 1)],
                                                   csil[:, b, P * (4 * h + t):P * (4 * h + t + 1)], c_f["ident"][:])
                    last.then_inc(b_tr, 1)

            def xside(j):
                fill(j, 0)
                if later(j):
                    turn(1, 2 * j, 4 * j - 3)
                else:
                    pe.wait_ge(d_dt, 1)
                fill(j, 1)
                turn(0, 2 * j + 1, 4 * j - 1 if later(j) else None)
            loop(pe, KE // 2, xside)
            turn(1, KE, 2 * KE - 3)
            a_ = a2[:, :, 0]
            pe.wait_ge(d_a, 2)
            acs = ps[:, 4].rearrange("p (t h) -> p t h", t=T)
            mm(acs[:, :, 0:H], c_f["upto"][:], a_[:, :, 0:H], start=True, stop=True).then_inc(d_acs, 1)
            mm(acs[:, :, H:2 * H], c_f["from_"][:], a_[:, :, H:2 * H], start=True, stop=True).then_inc(d_acs, 1)
            mm(ps[:, 5].rearrange("p (t h) -> p t h", t=T), c_f["ones"][:], a_, start=True, stop=True).then_inc(d_acs, 1)
            fill(KE // 2, 0)
            for u in range(2):
                if u == 0:
                    pe.wait_ge(d_se, 4)
                else:
                    pe.wait_ge(d_trl, 2)
                for d, tri in enumerate(("upto", "from_")):
                    for c in range(4):
                        last = mm(ps[:, 4 + d, P * c:P * (c + 1)],
                                  a2[:, 4 * u + c].rearrange("p n h -> p (n h)"), c_f[tri][:],
                                  start=True, stop=True)
                    last.then_inc(d_tr, 1)
            for g in range(G):
                if g:
                    fill(KE // 2 + g, 0)
                fill(KE // 2 + g, 1)
                turn(0, KE + 2 * g + 1, 2 * KE + 2 * g - 1)

            for q in range(G):
                for kp in range(4):
                    n = N_Z + 4 * q + kp
                    pe.wait_ge(w_lo, n + 1)
                    for kk in range(2):
                        for t in range(T):
                            if kp == 0 and kk == 0:
                                if q:
                                    pe.wait_ge(q_sil, T * (q - 1) + t + 1)
                                elif t == 0:
                                    pe.wait_ge(b_te, 2 * (KE + G))
                                    pe.wait_ge(b_sil, NXBC)
                            k = 2 * kp + kk
                            tc, wc = slice(P * t, P * (t + 1)), slice(HALF * kk, HALF * (kk + 1))
                            last = mm3(ps[:, t], xTh[:, k, tc], xTl[:, k, tc], wh[:, n % 2, wc], wl[:, n % 2, wc],
                                       k == 0, k == KD - 1)
                            if k == KD - 1:
                                last.then_inc(q_t, 1)
                    if kp < 3:
                        last.then_inc(q_mm, 1)

            pe.wait_ge(q_sil, T * G)
            for r in range(T - 1):
                b = r % 2
                pe.wait_ge(p_b[b], 16 * (r // 2 + 1))
                pe.wait_ge(p_xb, r + 1)
                if r >= 2:
                    pe.wait_ge(p_s, r)
                for g in range(G):
                    last = mm(ps[:, 4 * b + g], bc_s[:, b, 2, g], xb_s[:, b, HALF * g:HALF * (g + 1)], start=True, stop=True)
                last.then_inc(p_mm, 1)

            pe.wait_ge(p_s, T)
            pe.wait_ge(cr, 1)

            def chunk(c2):
                for b in range(2):
                    c = 2 * c2 + b

                    def decay_ahead(u):
                        if u < 16:
                            decay(u, c)
                        elif not (isinstance(c, int) and c == T - 1):
                            decay(u - 16, c + 1)

                    def decay(u, c):
                        hq, d = divmod(u, 2)
                        if u >= 2 or later(c):
                            pe.wait_ge(s_ex, 16 * c + u - 1)
                        bank = 3 + u % 2
                        for e in range(4):
                            col = d * H + 4 * hq + e
                            mm(ps[:, bank, P * e:P * (e + 1)], pickR[:, col:col + 1].to_broadcast([P, P]),
                                      acs_hl[:, bass.ds(c, 1)].rearrange("p a l -> p (a l)"), start=e == 0, stop=False,
                               skip_group_check=True)
                        mm(ps[:, bank].rearrange("p (e l) -> p e l", e=4), identR[:],
                           negR[:, d].unsqueeze(1).to_broadcast([P, 4, P]), start=False, stop=True,
                           skip_group_check=True).then_inc(s_L, 1)

                    def from_states(g):
                        cols = slice(HALF * g, HALF * (g + 1))
                        if g or later(c):
                            pe.wait_ge(s_ya, 4 * c + g)
                        if g == 0:
                            pe.wait_ge(s_zero, 1) if not later(c) else pe.wait_ge(s_S, 4 * c)
                        mm(ps[:, 1], bc_s[:, b, 1, g], sf[:, cols], start=True, stop=True).then_inc(s_yo, 1)
                        if g or later(c):
                            pe.wait_ge(s_tb, 4 * c + g)
                        mm(ps[:, 2], bc_s[:, b, 1, g],
                           keep[:].rearrange("p t e -> p (t e)")[:, bass.ds(c * E + HALF * g, HALF)],
                           start=True, stop=True).then_inc(s_yo, 1)

                    def inside(hq):
                        g = hq // 2
                        if hq % 2 == 0:
                            if g >= 2 or later(c):
                                pe.wait_ge(s_dd, 4 * c + g - 1)
                        for d in range(2):
                            u = 2 * hq + d
                            pe.wait_ge(s_M, 16 * c + u + 1)
                            for n in range(4):
                                h8 = 4 * (hq % 2) + n
                                last = mm(ps[:, 5 + g % 2, HD * h8:HD * (h8 + 1)], Mb[:, u % 4, n],
                                          xs_s[:, b, HD * (8 * g + h8):HD * (8 * g + h8 + 1)],
                                          start=hq % 2 == 0 and d == 0 and n == 0, stop=False, skip_group_check=True)
                        if hq % 2:
                            pe.wait_ge(s_xD, 4 * c + g + 1)
                            last = mm(ps[:, 5 + g % 2], c_f["ident"][:], xD[:, g % 2], start=False, stop=True,
                                      skip_group_check=True)
                        last.then_inc(s_yd, 1)

                    def state(g):
                        pe.wait_ge(s_xf, 4 * c + g + 1)
                        if g:
                            pe.wait_ge(s_S, 4 * c + g)
                        elif later(c):
                            pe.wait_ge(s_te, 4 * c)
                        mm(ps[:, 7], bc_s[:, b, 2, g], xf_s[:, g % 2], start=True, stop=True).then_inc(s_stt, 1)

                    if b == 0:
                        pe.wait_ge(s_x[0], 16 * (c2 + 1))
                    else:
                        pe.wait_ge(s_x[1], 16 * (c2 + 1))
                    pe.wait_ge(s_b[b], 16 * (c2 + 1))
                    if later(c):
                        pe.wait_ge(s_M, 16 * c)
                    for g in range(G):
                        last = mm(ps[:, 0, P * g:P * (g + 1)], bc_s[:, b, 0, g], bc_s[:, b, 1, g], start=True, stop=True)
                    last.then_inc(s_cb, 1)
                    if not later(c):
                        for u in range(4):
                            decay(u, c)
                    from_states(0)
                    for hq in range(8):
                        decay_ahead(2 * hq + 4)
                        decay_ahead(2 * hq + 5)
                        if hq < 4 and later(c):
                            turn_y(c - 1, hq)
                        if hq in (1, 3, 5):
                            from_states((hq + 1) // 2)
                        if hq >= 4:
                            state(hq - 4)
                        inside(hq)

            def turn_y(c, i):
                pe.wait_ge(s_g, 4 * c + i + 1)
                if i:
                    pe.wait_ge(s_te, 4 * c + i)
                else:
                    pe.wait_ge(s_S, 4 * c + 4)
                for n in range(4):
                    j = 4 * i + n
                    last = nc.tensor.transpose(ps[:, 7, P * n:P * (n + 1)], z_s[:, P * j:P * (j + 1)], c_f["ident"][:])
                last.then_inc(s_tr, 1)

            chunk(0)
            with pe.Fori(1, T // 2 - 1) as c2:
                chunk(c2)
            chunk(T // 2 - 1)
            for i in range(4):
                turn_y(T - 1, i)
            out_product(1, N_OUT2, lambda t: t == 0 and (pe.wait_ge(s_te, 4 * T), pe.wait_ge(s_dd, 4 * T)))


def kernel(**inputs):
    import numpy as np
    import concourse.bacc as bacc
    from concourse.bass_utils import run_bass_kernel_spmd

    f = {k: np.asarray(v) for k, v in inputs.items()}

    def by_channel(w):
        return w.reshape(KD, P, -1, P).transpose(2, 1, 0, 3).reshape(-1, P, W)

    def by_token(w, cols=HALF):
        k = w.shape[0] // P
        return w.reshape(k // 2, 2, P, -1, cols).transpose(3, 0, 2, 1, 4).reshape(-1, P, 2 * cols)

    w_in = by_channel(f["cm_w_in"][0]).reshape(3, KE, P, W)
    v, g, z = w_in
    stream = []
    for kind, i in (FIRST + [(kind, i + (4 if kind != "z" else 2) + (4 if kind != "z" else 2) * q)
                             for q in range(STEPS) for kind, i in STEP] + [("z", i) for i in range(NZ, KE)]):
        stream.append({"g": g, "v": v, "z": z}[kind][i])
    w_in = np.stack(stream)
    s_in = f["ssd_w_in"][0]
    nx = E + 2 * G * P
    order = list(range(KE)) + [KE + k * G + g for g in range(G) for k in range(2)]
    w_xbc = by_channel(s_in[:, E:E + nx])[order]
    w_dt = np.zeros((1, P, W), np.float32)
    w_dt[0, :, :KD * 2 * H] = s_in[:, E + nx:].reshape(KD, P, 2 * H).transpose(1, 0, 2).reshape(P, -1)
    wst = np.concatenate([w_in, by_token(f["cm_w_out"][0]), w_dt, w_xbc, by_token(s_in[:, :E]),
                          by_token(f["ssd_w_out"][0])])

    def col(v):
        return v.reshape(-1, P).T

    cvec = np.concatenate([col(f["cm_dw_b"][0]), col(f["cm_ln_w"][0]), col(f["cm_ln_b"][0]),
                           col(f["ssd_conv_b"][0])[:, order], col(f["ssd_norm_w"][0])], axis=1)
    dww = f["cm_dw_w"][0].reshape(TAPS, KE, P).transpose(2, 1, 0).reshape(P, -1)
    cw = f["ssd_conv_w"][0].reshape(CTAPS, NXBC, P)[:, order].transpose(2, 1, 0).reshape(P, -1)
    rows = np.concatenate([f["norm_w"], f["final_norm_w"][None]])
    srow = np.concatenate([f["ssd_dt_bias"].reshape(1, -1), f["ssd_A_log"].reshape(1, -1), f["ssd_D"].reshape(1, -1)],
                          axis=1)
    i = np.arange(P)
    tri = {"ident": i[:, None] == i, "upto": i[:, None] <= i, "from_": i[:, None] >= i, "ones": i[:, None] >= 0 * i}
    consts = {n: m.astype(np.float32) for n, m in tri.items()}
    consts["mean"] = np.full((P, P), 1.0 / E, np.float32)
    consts["neg_f"] = np.where(i[:, None] <= i, 0.0, -1e30).astype(np.float32)
    consts["neg_b"] = np.where(i[:, None] >= i, 0.0, -1e30).astype(np.float32)
    consts["pick"] = (i[:, None] % (2 * H) == np.arange(2 * H)).astype(np.float32)

    arrays = {"wst": wst, "x": f["x"].reshape(T, P, D), "cvec": cvec, "dww": dww, "cw": cw, "rows": rows,
              "srow": srow, **{"c_" + n: m for n, m in consts.items()}}
    arrays = {n + "_dram": np.ascontiguousarray(a) for n, a in arrays.items()}
    nc = bacc.Bacc("TRN2", target_bir_lowering=False, num_devices=1)
    aps = {n[:-5]: nc.dram_tensor(n, a.shape, mybir.dt.float32, kind="ExternalInput").ap() for n, a in arrays.items()}
    out = nc.dram_tensor("out_dram", (T, P, D), mybir.dt.float32, kind="ExternalOutput").ap()
    cst = {n: aps.pop("c_" + n) for n in C_NAMES}
    program(nc, out=out, cst=cst, **aps)
    r = run_bass_kernel_spmd(nc, [arrays], core_ids=[0])
    return r.results[0]["out_dram"].reshape(1, S, D)
```
